# Optimizing a Trainium2 kernel written in Bass

```python
import math
import jax, jax.numpy as jnp
from jax import lax
import numpy as np

D_MODEL = 1024
BATCH = 1
SEQ = 512
DEPTH = 1

ATTN_WIDTH = D_MODEL // 2
POOL_WIDTH = D_MODEL - ATTN_WIDTH
DIFF_HEADS = 4
DIFF_HEAD_DIM = ATTN_WIDTH // DIFF_HEADS
DIFF_QK_DIM = DIFF_HEAD_DIM // 2
ROT_DIM = DIFF_QK_DIM // 4
ROPE_THETA = 500000.0
POOL_WINDOWS = (2, 4, 8, 16)
POOL_GROUPS = len(POOL_WINDOWS)
POOL_GROUP_DIM = POOL_WIDTH // POOL_GROUPS
IN_WIDTH = 3 * ATTN_WIDTH + POOL_WIDTH
N_EXPERTS = 32
TOP_K = 4
D_FF = D_MODEL
SWIGLU_ALPHA = 1.702
SWIGLU_LIMIT = 7.0
Q_BLOCK = 128
MOE_BLOCK = 128
EPS = 1e-5

kernel_name = "hymba_diffattn_pool_moe_block"

def rms_norm(x, w):
    xf = x.astype(jnp.float32)
    y = xf * lax.rsqrt(jnp.mean(xf * xf, axis=-1, keepdims=True) + EPS)
    return (y * w.astype(jnp.float32)).astype(x.dtype)

def rope_tables(positions):
    inv_freq = ROPE_THETA ** (-jnp.arange(0, ROT_DIM, 2, dtype=jnp.float32) / ROT_DIM)
    ang = positions.astype(jnp.float32)[..., None] * inv_freq
    return jnp.cos(ang)[:, :, None, None, :], jnp.sin(ang)[:, :, None, None, :]

def apply_partial_rope(t, cos, sin):
    half = ROT_DIM // 2
    tr = t[..., :ROT_DIM].astype(jnp.float32)
    t1, t2 = tr[..., :half], tr[..., half:]
    rot = jnp.concatenate([t1 * cos - t2 * sin, t2 * cos + t1 * sin], axis=-1)
    return jnp.concatenate([rot.astype(t.dtype), t[..., ROT_DIM:]], axis=-1)

def diff_attention(q, k, v, lam, lam_init, subln_w):
    B, H, _, S, dk = q.shape
    dv = v.shape[-1]
    n_blocks = S // Q_BLOCK
    scale = dk ** -0.5
    kf = k.astype(jnp.float32)
    vf = v.astype(jnp.float32)
    k_idx = jnp.arange(S)

    def one_block(i):
        q0 = i * Q_BLOCK
        qb = lax.dynamic_slice_in_dim(q, q0, Q_BLOCK, axis=3).astype(jnp.float32)
        s = jnp.einsum('bhmqd,bhmkd->bhmqk', qb, kf) * scale
        q_idx = q0 + jnp.arange(Q_BLOCK)
        mask = k_idx[None, :] <= q_idx[:, None]
        p = jax.nn.softmax(jnp.where(mask, s, -jnp.inf), axis=-1)
        a = p[:, :, 0] - lam * p[:, :, 1]
        return jnp.einsum('bhqk,bhkd->bhqd', a, vf)

    o = lax.map(one_block, jnp.arange(n_blocks))
    o = o.transpose(1, 0, 3, 2, 4).reshape(B, S, H, dv)
    o = rms_norm(o, subln_w) * (1.0 - lam_init)
    return o.reshape(B, S, H * dv).astype(v.dtype)

def multiscale_pool(u, pool_w, pool_scale):
    B, S, C = u.shape
    uf = u.astype(jnp.float32).reshape(B, S, POOL_GROUPS, POOL_GROUP_DIM)
    c = jnp.cumsum(uf, axis=1)
    t = jnp.arange(1, S + 1, dtype=jnp.float32)
    pooled = []
    for g, w in enumerate(POOL_WINDOWS):
        cg = c[:, :, g]
        lower = jnp.pad(cg, ((0, 0), (w, 0), (0, 0)))[:, :S]
        count = jnp.minimum(t, float(w))[None, :, None]
        pooled.append((cg - lower) / count)
    pooled = jnp.stack(pooled, axis=2)
    y = jnp.einsum('bsgc,gcd->bsgd', pooled - uf, pool_w.astype(jnp.float32))
    y = y.reshape(B, S, C) * pool_scale.astype(jnp.float32)
    return y.astype(u.dtype)

def moe_ffn(h, router_w, router_b, w_gu, b_gu, w_down, b_down):
    B, S, D = h.shape
    T = B * S
    A = T * TOP_K
    hf = h.reshape(T, D)
    logits = (hf @ router_w + router_b).astype(jnp.float32)
    top_vals, top_idx = lax.top_k(logits, TOP_K)
    gates = jax.nn.softmax(top_vals, axis=-1)
    e_flat = top_idx.reshape(A)
    g_flat = gates.reshape(A)
    tok_flat = jnp.arange(A, dtype=jnp.int32) // TOP_K
    order = jnp.argsort(e_flat, stable=True)
    e_sorted, tok_sorted, g_sorted = e_flat[order], tok_flat[order], g_flat[order]
    counts = jax.ops.segment_sum(jnp.ones((A,), jnp.int32), e_flat, num_segments=N_EXPERTS)
    padded = (counts + MOE_BLOCK - 1) // MOE_BLOCK * MOE_BLOCK
    starts = jnp.cumsum(counts) - counts
    pad_ends = jnp.cumsum(padded)
    pad_starts = pad_ends - padded
    dest = pad_starts[e_sorted] + (jnp.arange(A, dtype=jnp.int32) - starts[e_sorted])
    P = A + N_EXPERTS * MOE_BLOCK
    n_blocks = P // MOE_BLOCK
    row_tok = jnp.zeros((P,), jnp.int32).at[dest].set(tok_sorted)
    row_gate = jnp.zeros((P,), jnp.float32).at[dest].set(g_sorted)
    block_start = jnp.arange(n_blocks, dtype=jnp.int32) * MOE_BLOCK
    block_expert = jnp.minimum(jnp.searchsorted(pad_ends, block_start, side='right'),
                               N_EXPERTS - 1)

    def step(acc, blk):
        rows, rgate, e = blk
        xs = hf[rows]
        gu = xs @ w_gu[e] + b_gu[e]
        gate = jnp.minimum(gu[:, :D_FF], SWIGLU_LIMIT)
        up = jnp.clip(gu[:, D_FF:], -SWIGLU_LIMIT, SWIGLU_LIMIT)
        glu = gate * jax.nn.sigmoid(SWIGLU_ALPHA * gate)
        y = ((up + 1.0) * glu) @ w_down[e] + b_down[e]
        acc = acc.at[rows].add(y.astype(jnp.float32) * rgate[:, None])
        return acc, None

    out, _ = lax.scan(step, jnp.zeros((T, D), jnp.float32),
                      (row_tok.reshape(n_blocks, MOE_BLOCK),
                       row_gate.reshape(n_blocks, MOE_BLOCK), block_expert))
    return out.reshape(B, S, D).astype(h.dtype)

def setup_inputs(seed: int = 0) -> dict:
    key = jax.random.key(seed)
    ks = jax.random.split(key, 20)
    f32 = jnp.float32
    L = DEPTH
    nrm = lambda k, shape, s: jax.random.normal(k, shape, f32) * s
    x = jax.random.normal(ks[0], (BATCH, SEQ, D_MODEL), f32)
    start = jax.random.randint(ks[1], (BATCH, 1), 0, 4096, dtype=jnp.int32)
    positions = start + jnp.arange(SEQ, dtype=jnp.int32)[None, :]
    return {
        "x": x,
        "positions": positions,
        "attn_norm_w": 1.0 + nrm(ks[2], (L, D_MODEL), 0.02),
        "w_in": nrm(ks[3], (L, D_MODEL, IN_WIDTH), D_MODEL ** -0.5),
        "lambda_q1": nrm(ks[4], (L, DIFF_QK_DIM), 0.1),
        "lambda_k1": nrm(ks[5], (L, DIFF_QK_DIM), 0.1),
        "lambda_q2": nrm(ks[6], (L, DIFF_QK_DIM), 0.1),
        "lambda_k2": nrm(ks[7], (L, DIFF_QK_DIM), 0.1),
        "subln_w": 1.0 + nrm(ks[8], (L, DIFF_HEAD_DIM), 0.02),
        "pool_w": nrm(ks[9], (L, POOL_GROUPS, POOL_GROUP_DIM, POOL_GROUP_DIM), POOL_GROUP_DIM ** -0.5),
        "pool_scale": 1.0 + nrm(ks[10], (L, POOL_WIDTH), 0.02),
        "w_out": nrm(ks[11], (L, D_MODEL, D_MODEL), D_MODEL ** -0.5),
        "ffn_norm_w": 1.0 + nrm(ks[12], (L, D_MODEL), 0.02),
        "router_w": nrm(ks[13], (L, D_MODEL, N_EXPERTS), D_MODEL ** -0.5),
        "router_b": nrm(ks[14], (L, N_EXPERTS), 0.01),
        "w_gate_up": nrm(ks[15], (L, N_EXPERTS, D_MODEL, 2 * D_FF), D_MODEL ** -0.5),
        "b_gate_up": nrm(ks[16], (L, N_EXPERTS, 2 * D_FF), 0.01),
        "w_down": nrm(ks[17], (L, N_EXPERTS, D_FF, D_MODEL), D_FF ** -0.5),
        "b_down": nrm(ks[18], (L, N_EXPERTS, D_MODEL), 0.01),
        "final_norm_w": 1.0 + nrm(ks[19], (D_MODEL,), 0.02),
    }

def reference(x, positions, attn_norm_w, w_in, lambda_q1, lambda_k1, lambda_q2, lambda_k2,
              subln_w, pool_w, pool_scale, w_out, ffn_norm_w, router_w, router_b,
              w_gate_up, b_gate_up, w_down, b_down, final_norm_w):
    B, S, _ = x.shape
    cos, sin = rope_tables(positions)
    for l in range(DEPTH):
        lam_init = 0.8 - 0.6 * math.exp(-0.3 * l)
        h = rms_norm(x, attn_norm_w[l])
        proj = h @ w_in[l]
        q, k, v, u = jnp.split(proj, [ATTN_WIDTH, 2 * ATTN_WIDTH, 3 * ATTN_WIDTH], axis=-1)
        q = apply_partial_rope(q.reshape(B, S, DIFF_HEADS, 2, DIFF_QK_DIM), cos, sin)
        k = apply_partial_rope(k.reshape(B, S, DIFF_HEADS, 2, DIFF_QK_DIM), cos, sin)
        q = q.transpose(0, 2, 3, 1, 4)
        k = k.transpose(0, 2, 3, 1, 4)
        v = v.reshape(B, S, DIFF_HEADS, DIFF_HEAD_DIM).transpose(0, 2, 1, 3)
        lam = (jnp.exp(jnp.sum(lambda_q1[l].astype(jnp.float32) * lambda_k1[l].astype(jnp.float32)))
               - jnp.exp(jnp.sum(lambda_q2[l].astype(jnp.float32) * lambda_k2[l].astype(jnp.float32)))
               + lam_init)
        attn = diff_attention(q, k, v, lam, lam_init, subln_w[l])
        pool = multiscale_pool(u, pool_w[l], pool_scale[l])
        x = x + jnp.concatenate([attn, pool], axis=-1) @ w_out[l]
        x = x + moe_ffn(rms_norm(x, ffn_norm_w[l]), router_w[l], router_b[l],
                        w_gate_up[l], b_gate_up[l], w_down[l], b_down[l])
    return rms_norm(x, final_norm_w)


_drawn_inputs = setup_inputs


def setup_inputs(seed=0):
    import zlib

    import numpy as np

    out = dict(_drawn_inputs(seed))
    spreads = {}
    factors = {'b_gate_up': 8.0, 'b_down': 8.0, 'final_norm_w': 2.829}
    for name, (base, spread) in spreads.items():
        noise = np.random.default_rng([zlib.crc32(name.encode()), seed]).standard_normal(out[name].shape)
        drawn = base * np.exp(spread * noise) if base else spread * noise
        out[name] = __import__('jax').numpy.asarray(drawn.astype(out[name].dtype))
    for name, factor in factors.items():
        out[name] = (out[name] * factor).astype(out[name].dtype)
    return out
```

```python
import concourse.bass as bass
from concourse import mybir
from contextlib import ExitStack
import math

import numpy as np

F32 = mybir.dt.float32
BF16 = mybir.dt.bfloat16
I32 = mybir.dt.int32
U32 = mybir.dt.uint32
ALU = mybir.AluOpType
ACT = mybir.ActivationFunctionType
AX = mybir.AxisListType.X

P = 128
S = 512
D = 1024
TT = S // P
KT = D // P
HEADS = 4
QKD = 64
ROT = 16
WINDOWS = (2, 4, 8, 16)
POOL_ORDER = (3, 2, 1, 0)
NE = 32
TOPK = 4
F = D
FT = F // P
BLK = 128
MAX_EXTRA = 15
LAM_INIT = 0.8 - 0.6 * math.exp(0.0)
SCALE = QKD ** -0.5
EPS = 1e-5
ALPHA = 1.702
LIMIT = 7.0
THETA = 500000.0
NEG = -1.0e30
OUT_OF_TOKENS = 1024
OUT_OF_ROWS = 4096
PI2_A = 6.28125
PI2_B = float(np.float32(2 * math.pi - PI2_A).view(np.int32) & -4096 and
              np.array([np.float32(2 * math.pi - PI2_A).view(np.int32) & -4096], np.int32).view(np.float32)[0])
PI2_C = float(np.float32(2 * math.pi - PI2_A - PI2_B))
ROUND = 12582912.0
PI_SAFE = 3.1415925


LOOP_DVE = 2 * (3 + 2 + 2 * FT)
EXTRA_DVE = 1 + 2 + 3 + 2 * FT


class Count:

    def __init__(self, eng, sem):
        self.eng, self.sem, self.n, self.off = eng, sem, 0, None

    def tick(self, ins):
        ins.then_inc(self.sem, 1)
        self.n += 1
        return self

    def settle(self):
        if self.off is None:
            self.eng.wait_ge(self.sem, self.n)
        else:
            self.eng.wait_ge(self.sem, self.off + self.n)


def hybrid_block(nc, x, positions, attn_norm_w, w_in, lambda_q1, lambda_k1, lambda_q2, lambda_k2,
                 subln_w, pool_w, pool_scale, w_out, ffn_norm_w, router_w, router_b,
                 w_gate_up, b_gate_up, w_down, b_down, final_norm_w, out, dbg=None):
    ctx = ExitStack()
    with ctx:
        def sb(name, shape, dt=F32):
            return ctx.enter_context(nc.sbuf_tensor(name, shape, dt))

        def sem(name):
            return ctx.enter_context(nc.semaphore(name))

        gu_slot = [sb("gu_slot_a", [P, KT, 2 * F]), sb("gu_slot_b", [P, KT, 2 * F])]
        dn_slot = sb("dn_slot", [P, FT, D])
        shared = sb("shared", [P, 10240])
        ident = sb("ident", [P, P])
        ident_h = sb("ident_h", [P, P], BF16)
        causal = sb("causal", [P, P], BF16)
        before = sb("before", [P, P], BF16)
        ones_h = sb("ones_h", [P, P], BF16)
        iota_n = sb("iota_n", [P, BLK])
        bias_t = sb("bias_t", [P, NE, 24])
        router_sb = sb("router_sb", [P, KT, NE])
        router_bias = sb("router_bias", [P, NE])
        logits = sb("logits", [P, TT, NE])
        vec_t = sb("vec_t", [P, 36])
        small = sb("small", [P, 184])
        counts_i = sb("counts_i", [1, NE + 2 + MAX_EXTRA], I32)

        slot_a = gu_slot[0][:, :, :].rearrange("p a b -> p (a b)")
        slot_b = gu_slot[1][:, :, :].rearrange("p a b -> p (a b)")

        def part(flat, at, *dims):
            n = int(np.prod(dims))
            v = flat[:, at:at + n]
            if len(dims) == 1:
                return v
            names = "abcd"[:len(dims)]
            return v.rearrange("p (%s) -> p %s" % (" ".join(names), " ".join(names)),
                               **dict(zip(names, dims)))

        h_t = part(slot_a, 0, KT, S)
        qk_tok = part(slot_a, 4096, 2, TT, 512)
        qk_t = part(slot_a, 8192, 2, HEADS, S)
        v_sb = part(slot_a, 12288, TT, 512)
        u_t = part(slot_a, 14336, TT, S)
        probs = part(slot_a, 4096, 2, 2, 512)
        mix = part(slot_a, 6144, 2, 512)
        mix_t = part(slot_a, 7168, 2, 512)
        xn1_sb = part(slot_a, 14336, 2, D)
        w_in_sb = gu_slot[1]
        w_out_sb = dn_slot

        sh = shared[:, :]
        x_sb = part(sh, 0, TT, D)
        cat_t = part(sh, 4096, KT, S)
        o_sb = part(sh, 8192, TT, HEADS, P)
        pool_tmp = cat_t[:, 0, :]
        square_out = cat_t[:, 1, :]
        pool_w_sb = cat_t[:, 3, :].rearrange("p (g c) -> p g c", g=4)
        pool_d = cat_t[:, 4:8, :]
        bias_rows = shared[0:NE, 4096:4096 + 3 * F]
        xn_sb = part(sh, 8192, D)
        h2_t = part(sh, 9216, KT, P)
        xg = part(sh, 0, D)
        xe_t = part(sh, 1024, 2, KT, BLK)
        one_hot = part(sh, 3072, TT, BLK)
        table = part(sh, 4096, TT, NE + 1, 3)
        spot = part(sh, 4608, TT, NE + 1)
        g_t = part(sh, 4864, 2, BLK)
        s_t = part(sh, 5120, 2, BLK)
        u1_t = part(sh, 5376, 2, BLK)
        u2_t = part(sh, 5632, 2, BLK)
        act_t = part(sh, 5888, FT, BLK)
        eq4 = part(sh, 6912, TT, TOPK, NE)
        eq4b = part(sh, 7424, TT, TOPK, NE)
        y_t = part(sh, 8192, KT, BLK)
        y_rows = part(sh, 9216, D)
        top8 = part(sh, 5888, TT, 8)
        top_idx = part(sh, 5920, TT, 8).bitcast(U32)
        idx_f = part(sh, 5952, TT, 8)
        mask_f = part(sh, 5984, TT, NE)
        mask_h = part(sh, 6112, TT * NE // 2).bitcast(BF16).rearrange("p (i e) -> p i e", i=TT)
        neg_top = part(sh, 6176, TT)
        gate4 = part(sh, 6180, TT, TOPK)
        gate_sum = part(sh, 6196, TT)
        dst4 = part(sh, 6200, TT, TOPK)
        tid4 = part(sh, 6216, TT)
        count_f = part(sh, 6220, NE)
        over = part(sh, 6252, NE)
        over_sum = part(sh, 6284, NE)
        zero32 = part(sh, 6316, NE)
        ov_e = part(sh, 6348, MAX_EXTRA)
        ov_b = part(sh, 6364, MAX_EXTRA)
        ov_cmp = part(sh, 6912, MAX_EXTRA, NE)
        ov_cmp2 = part(sh, 7424, MAX_EXTRA, NE)

        sm = small[:, :]
        ss_x = sm[:, 0:4]
        rstd_x = sm[:, 4:8]
        neg_lam = sm[:, 8:9]
        mx = part(sm, 9, 2, 2)
        nbias = part(sm, 13, 2, 2)
        esum = part(sm, 17, 2, 2)
        rsum = part(sm, 21, 2, 2)
        coef = part(sm, 25, 2, 1)
        ss_o = part(sm, 27, TT, HEADS)
        rstd_o = part(sm, 43, TT, HEADS)
        half_neg = sm[:, 59:75]
        bias_now = part(sm, 75, 2, 24)
        gate_col = part(sm, 123, 2, 1)
        idx_src = sm[:, 125:127].bitcast(U32)
        idx_dst = sm[:, 127:129].bitcast(U32)
        next_gate = sm[:, 162:163]
        next_dst = sm[:, 163:164]
        spot_now = sm[:, 156:160]
        junk_f = sm[:, 160:161]
        row_id = sm[:, 161:162]
        edge = sm[:, 164:180]
        extra_e = counts_i[0:1, NE + 2:NE + 2 + MAX_EXTRA]
        ss_2 = sm[:, 130:134]
        rstd_2 = sm[:, 134:138]
        extra_base = sm[:, 138:138 + MAX_EXTRA]

        rows = part(sh, 7168, P)[0:36, :]
        rows_i = part(sh, 7296, P)[0:36, :].bitcast(I32)
        AN, FN, PS, SL, POS = 0, 8, 16, 20, 32
        lam_in = part(sh, 7424, 256)[0:1, :].rearrange("p (a b c) -> p a b c", a=2, b=2)
        lam_pr = part(sh, 7680, 128)[0:1, :].rearrange("p (a c) -> p a c", a=2)
        lam_s = part(sh, 7808, 8)[0:1, :]
        ones_f = part(sh, 7824, P)[0:1, :]
        ang = part(sh, 8192, TT, 8)
        ang2 = part(sh, 8224, TT, 8)
        ang3 = part(sh, 8256, TT, 8)
        ang4 = part(sh, 8288, TT, 8)
        cos2 = part(sh, 8320, TT, ROT)
        sin2 = part(sh, 8384, TT, ROT)
        rot_a = part(sh, 8448, 2, 8, ROT)
        rot_b = part(sh, 8704, 2, 8, ROT)
        sq_junk = part(sh, 9216, D)

        ps = ctx.enter_context(nc.psum_tensor("ps", [P, 8, 512], F32))

        def bank4(b):
            return ps[:, b, :].rearrange("p (a c) -> p a c", a=4)

        x2_dram = nc.dram_tensor("x2_dram", [S, D], F32).ap()
        xn_dram = nc.dram_tensor("xn_dram", [S, D], F32).ap()
        ys_dram = nc.dram_tensor("ys_dram", [TOPK * S, D], F32).ap()

        x_tiles = x[0].rearrange("(i p) d -> i p d", p=P)
        out_tiles = out[0].rearrange("(i p) d -> i p d", p=P)
        x2_tiles = x2_dram.rearrange("(i p) d -> i p d", p=P)
        xn_tiles = xn_dram.rearrange("(i p) d -> i p d", p=P)
        ys_tiles = ys_dram.rearrange("(k i p) d -> i p k d", i=TT, p=P)
        w_in_v = w_in[0].rearrange("(j p) c -> p j c", p=P)
        w_out_v = w_out[0].rearrange("(j p) c -> p j c", p=P)
        w_gu_v = w_gate_up[0].rearrange("e (j p) c -> e p j c", p=P)
        w_dn_v = w_down[0].rearrange("e (j p) c -> e p j c", p=P)

        s_x = [sem(f"x_loaded{i}") for i in range(TT)]
        s_win = [sem(f"w_in_loaded{i}") for i in range(4)]
        s_wout = sem("w_out_loaded")
        s_small = sem("small_loaded")
        s_lam_in = sem("lambda_loaded")
        s_bias = sem("bias_rows_loaded")
        s_router = sem("router_loaded")
        s_poolw = sem("pool_w_loaded")
        gu_loaded = [sem("gu_loaded_a"), sem("gu_loaded_b")]
        dn_loaded = [sem(f"dn_loaded{c}") for c in range(4)]
        dve_seq = sem("dve_seq")
        act_seq = sem("act_seq")
        pool_seq = sem("pool_seq")
        consts = sem("consts_ready")
        rows_ready = sem("rows_ready")
        turned = sem("vectors_turned")
        vec_ready = sem("vectors_ready")
        lam_exp = sem("lambda_exp")
        lam_sum = sem("lambda_sum")
        lam_bc = sem("lambda_spread")
        ang_ready = sem("angles_ready")
        sincos = sem("sincos_ready")
        rot_ready = sem("rope_tables_ready")
        sumsq = sem("sumsq_x")
        rstd_done = sem("rstd_x_done")
        xn_ready = sem("xn_ready")
        xn_turned = sem("xn_turned")
        ht_ready = sem("h_t_ready")
        proj = sem("qk_projected")
        proj_copied = sem("qk_copied")
        roped = sem("qk_roped")
        qk_turned = sem("qk_turned")
        qkt_ready = sem("qk_t_ready")
        v_proj = sem("v_projected")
        v_ready = sem("v_ready")
        u_proj = sem("u_projected")
        u_ready = sem("u_t_ready")
        scored = sem("scored")
        maxed = sem("row_max_ready")
        exped = sem("exp_done")
        coefed = sem("coef_ready")
        scaled = sem("map1_scaled")
        mixed = sem("mixed")
        mix_turned = sem("mix_turned")
        mixt_ready = sem("mix_t_ready")
        pv_done = sem("pv_done")
        o_copied = sem("o_copied")
        o_rstd = sem("o_rstd_done")
        o_normed = sem("o_normed")
        o_turned = sem("o_turned")
        cat_attn = sem("cat_attn_ready")
        pooled = sem("pool_diff_ready")
        pool_mm = sem("pool_projected")
        cat_pool = sem("cat_pool_ready")
        out_proj = sem("out_projected")
        x2_ready = sem("x2_ready")
        sumsq2 = sem("sumsq_x2")
        rstd2_done = sem("rstd_x2_done")
        xn2_ready = sem("xn2_ready")
        x2_stored = sem("x2_stored")
        xn_stored = sem("xn_stored")
        xn2_turned = sem("xn2_turned")
        h2_ready = sem("h2_t_ready")
        routed = sem("router_projected")
        logit_ready = sem("logits_ready")
        top_ready = sem("top_ready")
        gate_exp = sem("gate_exp_done")
        mask_ready = sem("mask_ready")
        spot_sum = sem("spots_summed")
        tables = sem("tables_ready")
        extra_ready = sem("extra_tasks_ready")
        hot_ready = sem("one_hot_ready")
        idx_sum = sem("indices_summed")
        idx_ready = sem("indices_ready")
        gathered = sem("rows_gathered")
        x_turned = sem("expert_rows_turned")
        xe_ready = sem("expert_x_t_ready")
        gu_done = sem("gu_pair_done")
        g_ready = sem("gate_clamped")
        gu_evac = sem("gu_pair_evacuated")
        sig_ready = sem("sigmoid_ready")
        act_ready = sem("act_tile_ready")
        dn_used = sem("dn_chunk_used")
        yt_ready = sem("y_t_ready")
        y_turned = sem("y_turned")
        yr_ready = sem("y_rows_ready")
        scattered = sem("y_rows_scattered")
        all_scattered = sem("all_scattered")
        pool_touched = sem("pool_touched")
        ex_loaded = sem("extra_weights_loaded")
        ys_loaded = [sem(f"ys_loaded{i}") for i in range(TT)]
        fnw_loaded = sem("final_norm_w_loaded")
        moe_sum = sem("moe_summed")
        sumsq3 = sem("sumsq_final")
        rstd3_done = sem("rstd_final_done")
        out_ready = sem("out_tile_ready")
        out_stored = sem("out_stored")

        ys_sb = part(slot_a, 0, TT, TOPK, D)
        x2_sb = part(slot_b, 0, TT, D)
        fnw_sb = part(slot_b, 4096, D)
        sq3 = part(slot_b, 5120, D)

        block = ctx.enter_context(nc.Block())

        @block.sync
        def _(sp):
            for i in range(TT):
                sp.dma_start(x_sb[:, i, :], x_tiles[i]).then_inc(s_x[i], 16)
            for s in range(4):
                sp.dma_start(w_in_sb[:, :, 512 * s:512 * s + 512],
                             w_in_v[:, :, 512 * s:512 * s + 512]).then_inc(s_win[s], 16)
            sp.dma_start(w_out_sb[:, :, :], w_out_v).then_inc(s_wout, 16)

            def load_gu(slot, e, signal):
                for c in range(4):
                    src = w_gu_v[e] if isinstance(e, int) else \
                        w_gu_v[bass.ds(e, 1)].rearrange("a p j c -> (a p) j c")
                    sp.dma_start(gu_slot[slot][:, 2 * c:2 * c + 2, :],
                                 src[:, 2 * c:2 * c + 2, :]).then_inc(signal, 16)

            def load_dn_chunk(c, e, signal):
                src = w_dn_v[e] if isinstance(e, int) else \
                    w_dn_v[bass.ds(e, 1)].rearrange("a p j c -> (a p) j c")
                sp.dma_start(dn_slot[:, 2 * c:2 * c + 2, :], src[:, 2 * c:2 * c + 2, :]).then_inc(signal, 16)

            sp.wait_ge(u_proj, 4)
            load_gu(1, 0, gu_loaded[1])
            sp.wait_ge(pool_mm, 4)
            sp.wait_ge(pv_done, 16)
            sp.wait_ge(o_copied, 16)
            load_gu(0, 1, gu_loaded[0])
            with sp.Fori(0, NE // 2 - 1) as it:
                for s in range(2):
                    for c in range(4):
                        sp.wait_ge(dn_used, it * 8 + (4 * s + c + 1))
                        load_dn_chunk(c, it * 2 + s, dn_loaded[c])
                    sp.wait_ge(gu_done, it * 16 + (8 * s + 8))
                    load_gu(1 - s, it * 2 + (s + 2), gu_loaded[1 - s])
            for e in range(NE - 2, NE):
                for c in range(4):
                    sp.wait_ge(dn_used, 4 * e + c + 1)
                    load_dn_chunk(c, e, dn_loaded[c])
            sp.wait_ge(extra_ready, 1)
            n_extra = sp.value_load(counts_i[0:1, NE:NE + 1], min_val=0, max_val=MAX_EXTRA)
            with sp.Fori(0, MAX_EXTRA) as i:
                with sp.If(n_extra > i):
                    e = sp.value_load(extra_e[0:1, bass.ds(i, 1)], min_val=0, max_val=NE - 1)
                    sp.wait_ge(gu_done, i * FT + FT * NE)
                    load_gu(0, e, ex_loaded)
                    sp.wait_ge(dn_used, i * 4 + 4 * (NE + 1))
                    for c in range(4):
                        load_dn_chunk(c, e, ex_loaded)
            sp.wait_ge(all_scattered, 1)
            for i in range(TT):
                sp.dma_start(x2_sb[:, i, :], x2_tiles[i]).then_inc(ys_loaded[i], 16)
                for k in range(0, TOPK, 2):
                    sp.dma_start(ys_sb[:, i, k:k + 2, :], ys_tiles[i][:, k:k + 2, :]).then_inc(ys_loaded[i], 16)
            for i in range(TT):
                sp.wait_ge(out_ready, i + 1)
                sp.dma_start(out_tiles[i], x2_sb[:, i, :]).then_inc(out_stored, 16)
            sp.wait_ge(out_stored, 16 * TT)

        @block.gpsimd
        def _(pool):
            seq = Count(pool, pool_seq)
            seq.tick(nc.gpsimd.memset(ident[:, :], 0.0))
            seq.tick(nc.gpsimd.memset(ident_h[:, :], 0.0))
            seq.tick(nc.gpsimd.memset(causal[:, :], 0.0))
            seq.tick(nc.gpsimd.memset(before[:, :], 1.0))
            nc.gpsimd.memset(ones_h[:, :], 1.0).then_inc(consts, 1)
            nc.gpsimd.memset(half_neg, -0.5).then_inc(consts, 1)
            nc.gpsimd.memset(ones_f, 1.0).then_inc(consts, 1)
            seq.settle()
            for t in (ident, ident_h):
                nc.gpsimd.affine_select(out=t[:, :], in_=t[:, :], compare_op=ALU.not_equal, fill=1.0,
                                        base=0, pattern=[[-1, P]], channel_multiplier=1).then_inc(consts, 1)
            nc.gpsimd.affine_select(out=causal[:, :], in_=causal[:, :], compare_op=ALU.is_ge, fill=NEG,
                                    base=0, pattern=[[-1, P]], channel_multiplier=1).then_inc(consts, 1)
            nc.gpsimd.affine_select(out=before[:, :], in_=before[:, :], compare_op=ALU.is_ge, fill=0.0,
                                    base=-1, pattern=[[1, P]], channel_multiplier=-1).then_inc(consts, 1)
            nc.gpsimd.iota(row_id, pattern=[[0, 1]], base=0, channel_multiplier=1,
                           allow_small_or_imprecise_dtypes=True).then_inc(consts, 1)
            nc.gpsimd.iota(iota_n[:, :], pattern=[[1, BLK]], base=0, channel_multiplier=0,
                           allow_small_or_imprecise_dtypes=True).then_inc(consts, 1)

            def rstd(sums, result, exponent, width, signal):
                seq.tick(nc.gpsimd.tensor_scalar(result, sums, 1.0 / width, EPS, ALU.mult, ALU.add))
                seq.settle()
                nc.gpsimd.tensor_tensor(result, result, exponent, ALU.pow).then_inc(signal, 1)

            pool.wait_ge(consts, 9)
            for i in range(TT):
                pool.wait_ge(sumsq, i + 1)
                rstd(ss_x[:, i:i + 1], rstd_x[:, i:i + 1], half_neg[:, 0:1], D, rstd_done)

            def o_rstds(i):
                pool.wait_ge(o_copied, 4 * i + 4)
                rstd(ss_o[:, i, :], rstd_o[:, i, :], half_neg[:, 0:4], P, o_rstd)

            pool.wait_ge(turned, 2)
            pool.wait_ge(lam_bc, 1)
            pool.dma_start(pool_w_sb, pool_w[0].rearrange("g c d -> c g d")).then_inc(s_poolw, 16)
            pool.wait_ge(rows_ready, 3)
            for n, g in enumerate(POOL_ORDER):
                w = WINDOWS[g]
                pool.wait_ge(u_ready, n + 1)
                bufs = [pool_tmp, pool_d[:, g, :]]
                src, step = u_t[:, g, :], 1
                while step < w:
                    dst = bufs[0]
                    seq.tick(nc.gpsimd.tensor_copy(dst[:, 0:step], src[:, 0:step]))
                    seq.tick(nc.gpsimd.tensor_tensor(dst[:, step:S], src[:, step:S], src[:, 0:S - step], ALU.add))
                    seq.settle()
                    src, step, bufs = dst, 2 * step, bufs[::-1]
                seq.tick(nc.gpsimd.tensor_tensor(src[:, 0:w], src[:, 0:w], edge[:, 0:w], ALU.mult))
                seq.tick(nc.gpsimd.tensor_scalar(src[:, w:S], src[:, w:S], 1.0 / w, 0.0, ALU.mult, ALU.add))
                seq.settle()
                nc.gpsimd.tensor_tensor(pool_d[:, g, :], src, u_t[:, g, :], ALU.subtract).then_inc(pooled, 1)
                pool.wait_ge(pooled, n + 1)
            for i in range(TT):
                o_rstds(i)

            for i in range(TT):
                pool.wait_ge(sumsq2, i + 1)
                rstd(ss_2[:, i:i + 1], rstd_2[:, i:i + 1], half_neg[:, 0:1], D, rstd2_done)

            pool.wait_ge(x2_stored, 16 * TT)
            pool.wait_ge(xn2_ready, TT)
            nc.gpsimd.memset(xg, 0.0).then_inc(tables, 1)
            pool.wait_ge(tables, 1)

            def touch(at, signal=pool_touched):
                return nc.gpsimd.tensor_tensor(sm[:, 180 + at:181 + at], half_neg[:, 0:1], half_neg[:, 0:1],
                                               ALU.add).then_inc(signal, 1)

            def gather(b, n_idx):
                pool.wait_ge(idx_ready, n_idx)
                touch(2)
                pool.indirect_dma_start(
                    out=xg, out_offset=None, in_=xn_dram,
                    in_offset=bass.IndirectOffsetOnAxis(ap=idx_src[:, b:b + 1], axis=0),
                    bounds_check=S - 1, oob_is_err=False).then_inc(gathered, 16)

            def scatter(b, n_rows):
                pool.wait_ge(yr_ready, n_rows + 1)
                touch(b)
                pool.indirect_dma_start(
                    out=ys_dram, out_offset=bass.IndirectOffsetOnAxis(ap=idx_dst[:, b:b + 1], axis=0),
                    in_=y_rows, in_offset=None,
                    bounds_check=TOPK * S - 1, oob_is_err=False).then_inc(scattered, 16)

            pool.wait_ge(xn_stored, 16 * TT)
            pool.wait_ge(idx_ready, 1)
            pool.dma_start(y_rows[:, 0:P], xg[:, 0:P]).then_inc(scattered, 16)
            pool.wait_ge(scattered, 16)
            gather(0, 1)
            with pool.Fori(0, NE // 2) as it:
                for s in range(2):
                    scatter(1 - s, it * 2 + (s + 1))
                    gather(1 - s, it * 2 + (s + 2))
            scatter(1, NE + 1)
            pool.wait_ge(extra_ready, 1)
            n_extra = pool.value_load(counts_i[0:1, NE:NE + 1], min_val=0, max_val=MAX_EXTRA)
            with pool.Fori(0, MAX_EXTRA) as i:
                with pool.If(n_extra > i):
                    gather(0, i + (NE + 2))
                    scatter(0, i + (NE + 2))
            pool.wait_ge(scattered, n_extra * 16 + 16 * (NE + 2))
            touch(3, all_scattered)

            for i in range(TT):
                pool.wait_ge(sumsq3, i + 1)
                rstd(ss_x[:, i:i + 1], rstd_x[:, i:i + 1], half_neg[:, 0:1], D, rstd3_done)

        @block.scalar
        def _(act):
            seq = Count(act, act_seq)
            for at, w, n in ((AN, attn_norm_w, 8), (FN, ffn_norm_w, 8), (PS, pool_scale, 4), (SL, subln_w, 1)):
                act.wait_ge(rows_ready, 1)
                act.dma_start(rows[at:at + n, :], w[0].rearrange("(a b) -> a b", b=P)).then_inc(s_small, 16)
            act.dma_start(rows_i[POS:POS + 4, :], positions[0].rearrange("(a b) -> a b", b=P)).then_inc(s_small, 16)
            act.dma_start(bias_rows[:, 0:2 * F], b_gate_up[0]).then_inc(s_bias, 16)
            act.dma_start(bias_rows[:, 2 * F:3 * F], b_down[0]).then_inc(s_bias, 16)
            for a, (q, k) in enumerate(((lambda_q1, lambda_k1), (lambda_q2, lambda_k2))):
                act.dma_start(lam_in[:, a, 0, :], q).then_inc(s_lam_in, 16)
                act.dma_start(lam_in[:, a, 1, :], k).then_inc(s_lam_in, 16)
            act.dma_start(router_sb[:, :, :], router_w[0].rearrange("(j p) e -> p j e", p=P)).then_inc(s_router, 16)
            act.dma_start(router_bias[:, :], router_b.to_broadcast([P, NE])).then_inc(s_router, 16)
            for i in range(TT):
                act.wait_ge(s_x[i], 16)
                if i:
                    act.wait_ge(sumsq, i)
                nc.scalar.activation(sq_junk, x_sb[:, i, :], ACT.Square, accum_out=ss_x[:, i:i + 1]).then_inc(sumsq, 1)
            act.wait_ge(lam_sum, 1)
            nc.scalar.activation(lam_s[:, 2:4], lam_s[:, 0:2], ACT.Exp).then_inc(lam_exp, 1)
            act.wait_ge(ang_ready, 1)
            nc.scalar.activation(ang3, ang, ACT.Sin).then_inc(sincos, 1)
            nc.scalar.activation(ang4, ang2, ACT.Sin).then_inc(sincos, 1)

            def copy_qkt(n):
                s, i = divmod(n, TT)
                act.wait_ge(qk_turned, n + 1)
                nc.scalar.activation(qk_t[:, s, :, P * i:P * i + P], bank4(4 + n % 2), ACT.Copy).then_inc(qkt_ready, 1)

            for n in range(8):
                act.wait_ge(proj, n + 1)
                nc.scalar.activation(qk_tok[:, n // TT, n % TT, :], ps[:, n % 4, :], ACT.Copy).then_inc(proj_copied, 1)
                if n >= 2:
                    copy_qkt(n - 2)
            copy_qkt(6)
            copy_qkt(7)
            for i in range(TT):
                act.wait_ge(v_proj, i + 1)
                nc.scalar.activation(v_sb[:, i, :], ps[:, i, :], ACT.Copy).then_inc(v_ready, 1)

            def take_o(n):
                i, h = divmod(n, HEADS)
                act.wait_ge(pv_done, n + 1)
                if n == 0:
                    act.wait_ge(roped, 8)
                seq.tick(nc.scalar.activation(o_sb[:, i, h, :], ps[:, 6, P * h:P * h + P], ACT.Copy))
                nc.scalar.activation(square_out[:, P * h:P * h + P], ps[:, 6, P * h:P * h + P], ACT.Square,
                                     accum_out=ss_o[:, i, h:h + 1]).then_inc(o_copied, 1)

            for n in range(16):
                i, h = divmod(n, HEADS)
                b, w = n % 2, P * (i + 1)
                act.wait_ge(maxed, n + 1)
                if n >= 2:
                    act.wait_ge(mixed, n - 1)
                for m in range(2):
                    nc.scalar.activation(probs[:, b, m, 0:w], ps[:, 2 * b + m, 0:w], ACT.Exp,
                                         bias=nbias[:, b, m:m + 1], scale=SCALE,
                                         accum_out=esum[:, b, m:m + 1]).then_inc(exped, 1)
                act.wait_ge(coefed, n + 1)
                act.wait_ge(exped, 2 * n + 2)
                nc.scalar.activation(probs[:, b, 1, 0:w], probs[:, b, 1, 0:w], ACT.Copy,
                                     scale=coef[:, b, 0:1]).then_inc(scaled, 1)
                if n % 4 == 3:
                    g = n // 4
                    act.wait_ge(u_proj, g + 1)
                    nc.scalar.activation(u_t[:, POOL_ORDER[g], :], ps[:, 7, :], ACT.Copy).then_inc(u_ready, 1)
                if n >= 3:
                    take_o(n - 3)
            for n in range(13, 16):
                take_o(n)
            act.wait_ge(o_copied, 16)
            for n, g in enumerate(POOL_ORDER):
                act.wait_ge(pool_mm, n + 1)
                nc.scalar.activation(cat_t[:, 4 + g, :], ps[:, g, :], ACT.Copy,
                                     scale=vec_t[:, PS + g:PS + g + 1]).then_inc(cat_pool, 1)

            for i in range(TT):
                act.wait_ge(x2_ready, i + 1)
                act.dma_start(x2_tiles[i], x_sb[:, i, :]).then_inc(x2_stored, 16)
                if i:
                    act.wait_ge(h2_ready, i)
                    act.wait_ge(routed, i)
                nc.scalar.activation(h2_t.rearrange("p a b -> p (a b)"), x_sb[:, i, :], ACT.Square,
                                     accum_out=ss_2[:, i:i + 1]).then_inc(sumsq2, 1)
                act.wait_ge(xn2_ready, i + 1)
                act.dma_start(xn_tiles[i], xn_sb).then_inc(xn_stored, 16)

            act.wait_ge(top_ready, 1)
            for i in range(TT):
                nc.scalar.activation(gate4[:, i, :], top8[:, i, 0:TOPK], ACT.Exp, bias=neg_top[:, i:i + 1],
                                     accum_out=gate_sum[:, i:i + 1]).then_inc(gate_exp, 1)

            def sigmoid(b, n):
                act.wait_ge(g_ready, n)
                nc.scalar.activation(s_t[:, b, :], g_t[:, b, :], ACT.Sigmoid, scale=ALPHA).then_inc(sig_ready, 1)

            def take_rows(b, n):
                act.wait_ge(y_turned, n)
                nc.scalar.activation(y_rows, ps[:, 6:8, :].rearrange("p a b -> p (a b)"), ACT.Copy,
                                     scale=gate_col[:, b, 0:1]).then_inc(yr_ready, 1)

            with act.Fori(0, NE // 2) as it:
                for s in range(2):
                    for m in range(FT):
                        sigmoid(m % 2, it * 16 + (8 * s + m + 1))
                        if m == 1:
                            act.wait_ge(scattered, it * 32 + 16 * (s + 1))
                            take_rows(1 - s, it * 2 + (s + 1))
            act.wait_ge(scattered, 16 * (NE + 1))
            take_rows(1, NE + 1)
            act.wait_ge(extra_ready, 1)
            n_extra = act.value_load(counts_i[0:1, NE:NE + 1], min_val=0, max_val=MAX_EXTRA)
            with act.Fori(0, MAX_EXTRA) as i:
                with act.If(n_extra > i):
                    for m in range(FT):
                        sigmoid(m % 2, i * 8 + (8 * NE + m + 1))
                    act.wait_ge(scattered, i * 16 + 16 * (NE + 2))
                    take_rows(0, i + (NE + 2))

            act.wait_ge(all_scattered, 1)
            act.dma_start(fnw_sb, final_norm_w.rearrange("(a n) -> a n", a=1).to_broadcast([P, D])).then_inc(fnw_loaded, 16)
            for i in range(TT):
                act.wait_ge(moe_sum, i + 1)
                if i:
                    act.wait_ge(sumsq3, i)
                nc.scalar.activation(sq3, x2_sb[:, i, :], ACT.Square,
                                     accum_out=ss_x[:, i:i + 1]).then_inc(sumsq3, 1)

        @block.vector
        def _(dve):
            V = nc.vector
            seq = Count(dve, dve_seq)
            V.memset(rows, 0.0).then_inc(rows_ready, 1)
            dve.wait_ge(s_small, 16 * 5)
            V.tensor_copy(rows[POS:POS + 4, :], rows_i[POS:POS + 4, :]).then_inc(rows_ready, 1)
            dve.wait_ge(consts, 9)
            seq.tick(V.tensor_scalar(edge, iota_n[:, 0:16], 1.0, None, ALU.add))
            seq.settle()
            V.reciprocal(edge, edge).then_inc(rows_ready, 1)
            dve.wait_ge(s_lam_in, 64)
            seq.tick(V.tensor_tensor(lam_pr, lam_in[:, :, 0, :], lam_in[:, :, 1, :], ALU.mult))
            seq.settle()
            V.reduce_sum(lam_s[:, 0:2], lam_pr, AX).then_inc(lam_sum, 1)

            def norm_x(i):
                dve.wait_ge(rstd_done, i + 1)
                if i >= 2:
                    dve.wait_ge(xn_turned, i - 1)
                V.tensor_scalar(xn1_sb[:, i % 2, :], x_sb[:, i, :], rstd_x[:, i:i + 1], None, ALU.mult).then_inc(xn_ready, 1)

            dve.wait_ge(turned, 1)
            V.tensor_copy(vec_t[:, :], ps[:, 3, 0:36]).then_inc(vec_ready, 1)
            dve.wait_ge(turned, 2)
            seq.tick(V.tensor_copy(bias_t[:, :, 0:16].rearrange("p e c -> p c e"),
                                   ps[:, 6, :].rearrange("p (c e) -> p c e", c=16)))
            V.tensor_copy(bias_t[:, :, 16:24].rearrange("p e c -> p c e"),
                          ps[:, 7, 256:512].rearrange("p (c e) -> p c e", c=8)).then_inc(vec_ready, 1)
            norm_x(0)
            for i in range(TT):
                if i + 1 < TT:
                    norm_x(i + 1)
                dve.wait_ge(xn_turned, i + 1)
                for half in range(2):
                    V.tensor_tensor(h_t[:, 4 * half:4 * half + 4, P * i:P * i + P], bank4(4 + half),
                                    vec_t[:, AN + 4 * half:AN + 4 * half + 4, None].to_broadcast([P, 4, P]),
                                    ALU.mult).then_inc(ht_ready, 1)
                if i == 0:
                    dve.wait_ge(lam_exp, 1)
                    seq.tick(V.tensor_tensor(lam_s[:, 4:5], lam_s[:, 3:4], lam_s[:, 2:3], ALU.subtract))
                    seq.settle()
                    V.tensor_scalar(lam_s[:, 5:6], lam_s[:, 4:5], -LAM_INIT, None, ALU.add).then_inc(lam_sum, 1)
            inv_freq = np.float32(THETA) ** (-np.arange(0, ROT, 2, dtype=np.float32) / np.float32(ROT))
            for f in range(ROT // 2):
                seq.tick(V.tensor_scalar(ang[:, :, f], vec_t[:, POS:POS + 4], float(inv_freq[f]), None, ALU.mult))
            seq.settle()
            seq.tick(V.tensor_scalar(ang2, ang, 1.0 / (2 * math.pi), ROUND, ALU.mult, ALU.add))
            seq.settle()
            seq.tick(V.tensor_scalar(ang2, ang2, -ROUND, None, ALU.add))
            seq.settle()
            for piece in (PI2_A, PI2_B, PI2_C):
                seq.tick(V.scalar_tensor_tensor(ang, ang2, -piece, ang, ALU.mult, ALU.add))
                seq.settle()
            seq.tick(V.tensor_scalar(ang2, ang, math.pi / 2, None, ALU.add))
            seq.settle()
            seq.tick(V.tensor_scalar(ang3, ang2, math.pi, -2 * math.pi, ALU.is_gt, ALU.mult))
            seq.settle()
            seq.tick(V.tensor_tensor(ang2, ang2, ang3, ALU.add))
            seq.tick(V.tensor_scalar(ang, ang, PI_SAFE, -PI_SAFE, ALU.min, ALU.max))
            seq.settle()
            V.tensor_scalar(ang2, ang2, PI_SAFE, -PI_SAFE, ALU.min, ALU.max).then_inc(ang_ready, 1)
            dve.wait_ge(sincos, 2)
            seq.tick(V.tensor_copy(cos2[:, :, 0:8], ang4))
            seq.tick(V.tensor_copy(cos2[:, :, 8:16], ang4))
            seq.tick(V.tensor_copy(sin2[:, :, 8:16], ang3))
            seq.tick(V.tensor_scalar(sin2[:, :, 0:8], ang3, -1.0, None, ALU.mult))
            seq.settle()
            dve.wait_ge(lam_bc, 1)
            seq.tick(V.tensor_copy(neg_lam, ps[:, 7, 0:1]))

            for n in range(8):
                s, i = divmod(n, TT)
                dve.wait_ge(proj_copied, n + 1)
                src = ps[:, n % 4, :].rearrange("p (g d) -> p g d", g=8)
                dst = qk_tok[:, s, i, :].rearrange("p (g d) -> p g d", g=8)
                ra, rb = rot_a[:, n % 2], rot_b[:, n % 2]
                co = cos2[:, i, None, :].to_broadcast([P, 8, ROT])
                si = sin2[:, i, None, :].to_broadcast([P, 8, ROT])
                seq.tick(V.tensor_tensor(ra, src[:, :, 0:16], co, ALU.mult))
                seq.tick(V.tensor_tensor(rb[:, :, 0:8], src[:, :, 8:16], si[:, :, 0:8], ALU.mult))
                seq.tick(V.tensor_tensor(rb[:, :, 8:16], src[:, :, 0:8], si[:, :, 8:16], ALU.mult))
                seq.settle()
                V.tensor_tensor(dst[:, :, 0:16], ra, rb, ALU.add).then_inc(roped, 1)

            def evac_mix(n):
                w = P * (n // HEADS + 1)
                dve.wait_ge(mix_turned, n + 1)
                V.tensor_copy(mix_t[:, n % 2, 0:w], ps[:, 4 + n % 2, 0:w]).then_inc(mixt_ready, 1)

            for n in range(16):
                b, w = n % 2, P * (n // HEADS + 1)
                dve.wait_ge(scored, n + 1)
                seq.tick(V.reduce_max(mx[:, b, :], ps[:, 2 * b:2 * b + 2, 0:w], AX))
                seq.settle()
                V.tensor_scalar(nbias[:, b, :], mx[:, b, :], -SCALE, None, ALU.mult).then_inc(maxed, 1)
                if n >= 2:
                    evac_mix(n - 2)
                dve.wait_ge(exped, 2 * n + 2)
                seq.tick(V.reciprocal(rsum[:, b, :], esum[:, b, :]))
                seq.settle()
                V.tensor_tensor(coef[:, b, :], rsum[:, b, 1:2], neg_lam, ALU.mult).then_inc(coefed, 1)
                dve.wait_ge(scaled, n + 1)
                V.scalar_tensor_tensor(mix[:, b, 0:w], probs[:, b, 0, 0:w], rsum[:, b, 0:1], probs[:, b, 1, 0:w],
                                       ALU.mult, ALU.add).then_inc(mixed, 1)
            evac_mix(14)
            evac_mix(15)
            def take_cat(i):
                dve.wait_ge(o_turned, i + 1)
                V.tensor_scalar(cat_t[:, 0:4, P * i:P * i + P], bank4(4 + i % 2), vec_t[:, SL:SL + 1],
                                1.0 - LAM_INIT, ALU.mult, ALU.mult).then_inc(cat_attn, 1)

            for i in range(TT):
                dve.wait_ge(o_rstd, i + 1)
                V.tensor_tensor(o_sb[:, i], o_sb[:, i], rstd_o[:, i, :, None].to_broadcast([P, HEADS, P]),
                                ALU.mult).then_inc(o_normed, 1)
                if i:
                    take_cat(i - 1)
            take_cat(TT - 1)

            for i in range(TT):
                dve.wait_ge(out_proj, i + 1)
                V.tensor_tensor(x_sb[:, i, :], x_sb[:, i, :],
                                ps[:, 2 * (i % 2):2 * (i % 2) + 2, :].rearrange("p a b -> p (a b)"),
                                ALU.add).then_inc(x2_ready, 1)
                dve.wait_ge(rstd2_done, i + 1)
                if i:
                    dve.wait_ge(xn_stored, 16 * i)
                    dve.wait_ge(xn2_turned, i)
                V.tensor_scalar(xn_sb, x_sb[:, i, :], rstd_2[:, i:i + 1], None, ALU.mult).then_inc(xn2_ready, 1)
                dve.wait_ge(xn2_turned, i + 1)
                V.tensor_tensor(h2_t, ps[:, 4:6, :].rearrange("p a (c n) -> p (a c) n", c=4),
                                vec_t[:, FN:FN + 8, None].to_broadcast([P, KT, P]), ALU.mult).then_inc(h2_ready, 1)
                dve.wait_ge(routed, i + 1)
                V.tensor_tensor(logits[:, i, :], ps[:, 6, NE * i:NE * i + NE], router_bias[:, :],
                                ALU.add).then_inc(logit_ready, 1)

            dve.wait_ge(logit_ready, TT)
            for i in range(TT):
                seq.tick(V.max(top8[:, i, :], logits[:, i, :]))
            seq.settle()
            seq.tick(V.tensor_scalar(neg_top, top8[:, :, 0], -1.0, None, ALU.mult))
            for i in range(TT):
                seq.tick(V.max_index(top_idx[:, i, :], top8[:, i, :], logits[:, i, :]))
            seq.settle()
            V.tensor_copy(idx_f, top_idx).then_inc(top_ready, 1)
            dve.wait_ge(top_ready, 1)
            seq.tick(V.tensor_tensor(eq4, iota_n[:, None, None, 0:NE].to_broadcast([P, TT, TOPK, NE]),
                                     idx_f[:, :, 0:TOPK, None].to_broadcast([P, TT, TOPK, NE]), ALU.is_equal))
            seq.settle()
            seq.tick(V.reduce_sum(mask_f, eq4.rearrange("p i k e -> p i e k"), AX))
            seq.settle()
            V.tensor_copy(mask_h, mask_f).then_inc(mask_ready, 1)
            dve.wait_ge(gate_exp, TT)
            seq.tick(V.reciprocal(gate_sum, gate_sum))
            seq.settle()
            seq.tick(V.tensor_tensor(gate4, gate4, gate_sum[:, :, None].to_broadcast([P, TT, TOPK]), ALU.mult))
            for i in range(TT):
                seq.tick(V.tensor_scalar(tid4[:, i:i + 1], row_id, float(P * i - OUT_OF_TOKENS), None, ALU.add))
                for k in range(TOPK):
                    seq.tick(V.tensor_scalar(dst4[:, i, k:k + 1], row_id, float(S * k + P * i - OUT_OF_ROWS), None,
                                             ALU.add))
            seq.settle()
            for i in range(TT):
                seq.tick(V.tensor_scalar(table[:, i, :, 0], iota_n[:, 0:NE + 1], 0.0, tid4[:, i:i + 1],
                                         ALU.mult, ALU.add))
            seq.tick(V.tensor_tensor(eq4b, eq4, gate4[:, :, :, None].to_broadcast([P, TT, TOPK, NE]), ALU.mult))
            seq.settle()
            seq.tick(V.reduce_sum(table[:, :, 0:NE, 1], eq4b.rearrange("p i k e -> p i e k"), AX))
            seq.tick(V.memset(table[:, :, NE, 1], 0.0))
            seq.tick(V.memset(table[:, :, NE, 2], 0.0))
            seq.settle()
            seq.tick(V.tensor_tensor(eq4b, eq4, dst4[:, :, :, None].to_broadcast([P, TT, TOPK, NE]), ALU.mult))
            seq.settle()
            seq.tick(V.reduce_sum(table[:, :, 0:NE, 2], eq4b.rearrange("p i k e -> p i e k"), AX))
            dve.wait_ge(spot_sum, 1)
            seq.tick(V.scalar_tensor_tensor(spot[:, :, 0:NE], ps[:, 4, 0:TT * NE].rearrange("p (i e) -> p i e", i=TT),
                                            1.0, mask_f, ALU.add, ALU.mult))
            seq.tick(V.memset(spot[:, :, NE], 0.0))
            seq.settle()
            seq.tick(V.tensor_scalar(spot, spot, -1.0, None, ALU.add))
            seq.tick(V.tensor_copy(counts_i[0:1, 0:NE], ps[0:1, 5, 0:NE]))
            seq.tick(V.tensor_copy(count_f, ps[:, 5, 0:NE]))
            seq.settle()

            def hot(e):
                src = spot[:, :, e:e + 1] if isinstance(e, int) else spot[:, :, bass.ds(e, 1)]
                V.tensor_tensor(one_hot, iota_n[:, None, :].to_broadcast([P, TT, BLK]),
                                src.to_broadcast([P, TT, BLK]), ALU.is_equal).then_inc(hot_ready, 1)

            def take_indices(b, n):
                dve.wait_ge(idx_sum, n)
                seq.tick(V.tensor_copy(next_gate, ps[:, 4, 1:2]))
                seq.tick(V.tensor_scalar(next_dst, ps[:, 4, 2:3], float(OUT_OF_ROWS), None, ALU.add))
                V.tensor_scalar(idx_src[:, b:b + 1], ps[:, 4, 0:1], float(OUT_OF_TOKENS), None,
                                ALU.add).then_inc(idx_ready, 1)

            def start_block(b, e, n_before, n_touched):
                dve.wait_ge(scattered, n_before)
                dve.wait_ge(pool_touched, n_touched)
                seq.settle()
                seq.tick(V.tensor_copy(gate_col[:, b, :], next_gate))
                seq.tick(V.tensor_copy(idx_dst[:, b:b + 1], next_dst))
                src = bias_t[:, e, :] if isinstance(e, int) else \
                    bias_t[:, bass.ds(e, 1), :].rearrange("p a c -> p (a c)")
                seq.tick(V.tensor_copy(bias_now[:, b, :], src))
                seq.settle()

            def take_x(b, n):
                dve.wait_ge(x_turned, n)
                V.tensor_tensor(xe_t[:, b], ps[:, 4:6, :].rearrange("p a (c n) -> p (a c) n", c=4),
                                vec_t[:, FN:FN + 8, None].to_broadcast([P, KT, BLK]), ALU.mult).then_inc(xe_ready, 1)

            def take_y(b, n):
                dve.wait_ge(dn_used, n * 4)
                V.tensor_tensor(y_t, ps[:, 2:4, :].rearrange("p a (c n) -> p (a c) n", c=4),
                                bias_now[:, b, 16:24, None].to_broadcast([P, KT, BLK]), ALU.add).then_inc(yt_ready, 1)

            def clamp(b, s, m, n):
                dve.wait_ge(gu_done, n)
                V.tensor_scalar(g_t[:, b, :], ps[:, b, 0:BLK], bias_now[:, s, m:m + 1], LIMIT,
                                ALU.add, ALU.min).then_inc(g_ready, 1)
                V.tensor_scalar(u1_t[:, b, :], ps[:, b, BLK:2 * BLK], bias_now[:, s, FT + m:FT + m + 1], -LIMIT,
                                ALU.add, ALU.max).then_inc(gu_evac, 1)

            def finish_act(b, m, n):
                dve.wait_ge(gu_evac, n + 2)
                seq.tick(V.tensor_scalar(u2_t[:, b, :], u1_t[:, b, :], LIMIT, 1.0, ALU.min, ALU.add))
                dve.wait_ge(sig_ready, n)
                seq.tick(V.tensor_tensor(s_t[:, b, :], g_t[:, b, :], s_t[:, b, :], ALU.mult))
                seq.settle()
                V.tensor_tensor(act_t[:, m, :], u2_t[:, b, :], s_t[:, b, :], ALU.mult).then_inc(act_ready, 1)

            seq.tick(V.memset(bias_now[:, 1, :], 0.0))
            seq.tick(V.memset(gate_col[:, 1, :], 0.0))
            seq.tick(V.memset(junk_f, float(OUT_OF_ROWS)))
            seq.settle()
            seq.tick(V.tensor_copy(idx_dst[:, 1:2], junk_f))
            seq.settle()
            dve.wait_ge(x2_stored, 16 * TT)
            dve.wait_ge(x2_ready, TT)
            dve.sem_inc(gu_evac, 2)
            dve.sem_inc(yr_ready, 1)
            hot(0)
            take_indices(0, 1)
            seq.tick(V.tensor_scalar(over, count_f, float(BLK), None, ALU.is_gt))
            seq.settle()
            for j in (2, 3):
                seq.tick(V.scalar_tensor_tensor(over, count_f, float(BLK * j), over, ALU.is_gt, ALU.add))
                seq.settle()
            seq.tick(V.memset(zero32, 0.0))
            seq.settle()
            seq.tick(V.tensor_tensor_scan(over_sum, over, zero32, 0.0, ALU.add, ALU.add))
            seq.settle()
            seq.tick(V.tensor_tensor(ov_cmp, over_sum[:, None, :].to_broadcast([P, MAX_EXTRA, NE]),
                                     iota_n[:, 0:MAX_EXTRA, None].to_broadcast([P, MAX_EXTRA, NE]), ALU.is_le))
            seq.settle()
            seq.tick(V.reduce_sum(ov_e, ov_cmp, AX))
            seq.tick(V.tensor_tensor(ov_cmp2, ov_cmp, over[:, None, :].to_broadcast([P, MAX_EXTRA, NE]), ALU.mult))
            seq.settle()
            seq.tick(V.reduce_sum(ov_b, ov_cmp2, AX))
            seq.settle()
            seq.tick(V.tensor_tensor(extra_base, iota_n[:, 0:MAX_EXTRA], ov_b, ALU.subtract))
            seq.tick(V.tensor_scalar(ov_e, ov_e, float(NE - 1), None, ALU.min))
            seq.settle()
            seq.tick(V.tensor_scalar(extra_base, extra_base, 1.0, float(BLK), ALU.add, ALU.mult))
            seq.tick(V.tensor_copy(extra_e, ov_e[0:1, :]))
            seq.settle()
            V.tensor_copy(counts_i[0:1, NE:NE + 1], over_sum[0:1, NE - 1:NE]).then_inc(extra_ready, 1)
            take_x(0, 1)
            dve.wait_ge(extra_ready, 1)

            n0 = seq.n
            per = 0
            with dve.Fori(0, NE // 2) as it:
                seq.off = it * LOOP_DVE
                for s in range(2):
                    def ex(k, c):
                        return it * (2 * k) + (k * s + c)
                    take_y(1 - s, ex(1, 1))
                    start_block(s, it * 2 + s, it * 32 + 16 * (s + 1), it * 4 + (2 * s + 1))
                    for m in range(FT):
                        b = m % 2
                        clamp(b, s, m, ex(FT, m + 1))
                        if m:
                            finish_act(1 - b, m - 1, ex(FT, m))
                        if m == 1:
                            hot(it * 2 + (s + 1))
                        if m == 3:
                            take_indices(1 - s, ex(1, 2))
                    take_x(1 - s, ex(1, 2))
                    finish_act(1, FT - 1, ex(FT, FT))
                per = seq.n - n0
            assert per == LOOP_DVE, per
            seq.n, seq.off = n0 + LOOP_DVE * (NE // 2), None
            take_y(1, NE + 1)
            seq.settle()
            n_extra = dve.value_load(counts_i[0:1, NE:NE + 1], min_val=0, max_val=MAX_EXTRA)
            n1 = seq.n
            with dve.Fori(0, MAX_EXTRA) as i:
                with dve.If(n_extra > i):
                    seq.off = i * EXTRA_DVE
                    e = dve.value_load(extra_e[0:1, bass.ds(i, 1)], min_val=0, max_val=NE - 1)
                    dve.wait_ge(pool_touched, i * 2 + (2 * NE + 2))
                    seq.tick(V.tensor_scalar(spot_now, spot[:, :, bass.ds(e, 1)].rearrange("p i a -> p (i a)"),
                                             extra_base[:, bass.ds(i, 1)], None, ALU.subtract))
                    seq.settle()
                    V.tensor_tensor(one_hot, iota_n[:, None, :].to_broadcast([P, TT, BLK]),
                                    spot_now[:, :, None].to_broadcast([P, TT, BLK]),
                                    ALU.is_equal).then_inc(hot_ready, 1)
                    dve.wait_ge(yr_ready, i + (NE + 2))
                    dve.wait_ge(scattered, i * 16 + 16 * (NE + 2))
                    take_indices(0, i + (NE + 2))
                    start_block(0, e, i * 16 + 16 * (NE + 2), i * 2 + (2 * NE + 2))
                    take_x(0, i + (NE + 2))
                    for m in range(FT):
                        clamp(m % 2, 0, m, i * FT + (FT * NE + m + 1))
                        finish_act(m % 2, m, i * FT + (FT * NE + m + 1))
                    take_y(0, i + (NE + 2))
                    per = seq.n - n1
            assert per == EXTRA_DVE, per
            seq.off = n_extra * EXTRA_DVE
            seq.n = n1

            def finish_tile(i):
                dve.wait_ge(rstd3_done, i + 1)
                V.scalar_tensor_tensor(x2_sb[:, i, :], x2_sb[:, i, :], rstd_x[:, i:i + 1], fnw_sb,
                                       ALU.mult, ALU.mult).then_inc(out_ready, 1)
            for i in range(TT):
                dve.wait_ge(ys_loaded[i], 48)
                seq.tick(V.tensor_tensor(ys_sb[:, i, 0:2, :], ys_sb[:, i, 0:2, :], ys_sb[:, i, 2:4, :], ALU.add))
                seq.settle()
                seq.tick(V.tensor_tensor(ys_sb[:, i, 0, :], ys_sb[:, i, 0, :], ys_sb[:, i, 1, :], ALU.add))
                seq.settle()
                V.tensor_tensor(x2_sb[:, i, :], x2_sb[:, i, :], ys_sb[:, i, 0, :], ALU.add).then_inc(moe_sum, 1)
                if i == 1:
                    dve.wait_ge(fnw_loaded, 16)
                if i:
                    finish_tile(i - 1)
            finish_tile(TT - 1)

        @block.tensor
        def _(pe):
            MM = nc.tensor.matmul
            TR = nc.tensor.transpose
            pe.wait_ge(consts, 9)
            pe.wait_ge(rows_ready, 2)
            TR(ps[:, 3, 0:36], rows, ident[0:36, 0:36]).then_inc(turned, 1)
            pe.wait_ge(s_bias, 32)
            for c in range(24):
                o = ps[:, 6, 32 * c:32 * c + 32] if c < 16 else ps[:, 7, 256 + 32 * (c - 16):288 + 32 * (c - 16)]
                mm = TR(o, bias_rows[:, P * c:P * c + P], ident[0:NE, 0:NE])
            mm.then_inc(turned, 1)
            for i in range(TT):
                pe.wait_ge(xn_ready, i + 1)
                if i:
                    pe.wait_ge(ht_ready, 2 * i)
                for j in range(KT):
                    mm = TR(bank4(4 + j // 4)[:, j % 4, :], xn1_sb[:, i % 2, P * j:P * j + P], ident[:, :])
                mm.then_inc(xn_turned, 1)
            pe.wait_ge(lam_sum, 2)
            pe.wait_ge(vec_ready, 2)
            MM(ps[:, 7, 0:1], ones_f, lam_s[:, 5:6], start=True, stop=True).then_inc(lam_bc, 1)

            def turn_qk(n):
                s, i = divmod(n, TT)
                pe.wait_ge(roped, n + 1)
                if n < 2:
                    pe.wait_ge(ht_ready, 2 * TT)
                else:
                    pe.wait_ge(qkt_ready, n - 1)
                for h in range(HEADS):
                    mm = TR(bank4(4 + n % 2)[:, h, :], qk_tok[:, s, i, P * h:P * h + P], ident[:, :])
                mm.then_inc(qk_turned, 1)

            for n in range(8):
                s, i = divmod(n, TT)
                pe.wait_ge(s_win[s], 16)
                pe.wait_ge(ht_ready, 2 * i + 2)
                if n >= 4:
                    pe.wait_ge(roped, n - 3)
                for j in range(KT):
                    mm = MM(ps[:, n % 4, :], h_t[:, j, P * i:P * i + P], w_in_sb[:, j, 512 * s:512 * s + 512],
                            start=(j == 0), stop=(j == KT - 1))
                mm.then_inc(proj, 1)
                if n >= 2:
                    turn_qk(n - 2)
            pe.wait_ge(s_win[2], 16)
            for i in range(TT):
                pe.wait_ge(roped, 5 + i)
                for j in range(KT):
                    mm = MM(ps[:, i, :], h_t[:, j, P * i:P * i + P], w_in_sb[:, j, 1024:1536],
                            start=(j == 0), stop=(j == KT - 1))
                mm.then_inc(v_proj, 1)
                if i < 2:
                    turn_qk(6 + i)

            def scores(n):
                i, h = divmod(n, HEADS)
                b = n % 2
                if n == 0:
                    pe.wait_ge(qkt_ready, 8)
                if n < 2:
                    pe.wait_ge(v_ready, 2 * n + 2)
                else:
                    pe.wait_ge(exped, 2 * n - 2)
                for m in range(2):
                    r = slice(QKD * m, QKD * m + QKD)
                    o = ps[:, 2 * b + m, :]
                    MM(o[:, P * i:P * i + P], ident_h[:, :], causal[:, :], start=True, stop=False,
                       skip_group_check=True)
                    mm = MM(o[:, 0:P * (i + 1)], qk_t[r, 0, h, P * i:P * i + P], qk_t[r, 1, h, 0:P * (i + 1)],
                            start=False, stop=True, skip_group_check=True)
                mm.then_inc(scored, 1)

            def turn_mix(n):
                i = n // HEADS
                pe.wait_ge(mixed, n + 1)
                if n < 2:
                    pe.wait_ge(qkt_ready, 8)
                else:
                    pe.wait_ge(mixt_ready, n - 1)
                for kb in range(i + 1):
                    mm = TR(bank4(4 + n % 2)[:, kb, :], mix[:, n % 2, P * kb:P * kb + P], ident[:, :])
                mm.then_inc(mix_turned, 1)

            def pv(n):
                i, h = divmod(n, HEADS)
                pe.wait_ge(mixt_ready, n + 1)
                if n == 0:
                    pe.wait_ge(v_ready, TT)
                else:
                    pe.wait_ge(o_copied, n)
                for kb in range(i + 1):
                    mm = MM(ps[:, 6, P * h:P * h + P], mix_t[:, n % 2, P * kb:P * kb + P],
                            v_sb[:, kb, P * h:P * h + P], start=(kb == 0), stop=(kb == i))
                mm.then_inc(pv_done, 1)

            pe.wait_ge(s_win[3], 16)
            for n in range(16):
                scores(n)
                c, r = divmod(n, 4)
                if r == 0 and c:
                    pe.wait_ge(u_ready, c)
                uc = 1536 + P * POOL_ORDER[c]
                for j in (2 * r, 2 * r + 1):
                    mm = MM(ps[:, 7, :], w_in_sb[:, j, uc:uc + P], h_t[:, j, :],
                            start=(j == 0), stop=(j == KT - 1))
                if r == 3:
                    mm.then_inc(u_proj, 1)
                if n >= 2:
                    turn_mix(n - 2)
                if n >= 3:
                    pv(n - 3)
            turn_mix(14)
            pv(13)
            turn_mix(15)
            pv(14)
            pv(15)
            pe.wait_ge(s_poolw, 16)
            pe.wait_ge(exped, 32)
            for n, g in enumerate(POOL_ORDER):
                pe.wait_ge(pooled, n + 1)
                MM(ps[:, g, :], pool_w_sb[:, g, :], pool_d[:, g, :], start=True, stop=True).then_inc(pool_mm, 1)
            for i in range(TT):
                pe.wait_ge(o_normed, i + 1)
                if i < 2:
                    pe.wait_ge(mixt_ready, 16)
                else:
                    pe.wait_ge(cat_attn, i - 1)
                for h in range(HEADS):
                    mm = TR(bank4(4 + i % 2)[:, h, :], o_sb[:, i, h, :], ident[:, :])
                mm.then_inc(o_turned, 1)

            def router(i):
                pe.wait_ge(xn2_ready, i + 1)
                if i == 0:
                    pe.wait_ge(cat_attn, TT)
                else:
                    pe.wait_ge(h2_ready, i)
                for j in range(KT):
                    mm = TR(bank4(4 + j // 4)[:, j % 4, :], xn_sb[:, P * j:P * j + P], ident[:, :])
                mm.then_inc(xn2_turned, 1)
                pe.wait_ge(h2_ready, i + 1)
                if i == 0:
                    pe.wait_ge(o_copied, 16)
                    pe.wait_ge(s_router, 32)
                for j in range(KT):
                    mm = MM(ps[:, 6, NE * i:NE * i + NE], h2_t[:, j, :], router_sb[:, j, :],
                            start=(j == 0), stop=(j == KT - 1))
                mm.then_inc(routed, 1)

            pe.wait_ge(s_wout, 16)
            pe.wait_ge(cat_pool, 4)
            for i in range(TT):
                pe.wait_ge(cat_attn, i + 1)
                if i >= 2:
                    pe.wait_ge(x2_ready, i - 1)
                for half in range(2):
                    for n, j in enumerate((4, 5, 6, 7, 0, 1, 2, 3)):
                        mm = MM(ps[:, 2 * (i % 2) + half, :], cat_t[:, j, P * i:P * i + P],
                                w_out_sb[:, j, 512 * half:512 * half + 512], start=(n == 0), stop=(n == KT - 1))
                mm.then_inc(out_proj, 1)
                if i:
                    router(i - 1)
            router(TT - 1)
            pe.wait_ge(x2_ready, TT)
            pe.sem_inc(dn_used, 4)
            pe.wait_ge(mask_ready, 1)
            pe.wait_ge(h2_ready, TT)
            for i in range(TT):
                for k in range(i + 1):
                    MM(ps[:, 4, NE * i:NE * i + NE], before[:, :] if k == i else ones_h[:, :], mask_h[:, k, :],
                       start=(k == 0), stop=(k == i))
            for k in range(TT):
                mm = MM(ps[:, 5, 0:NE], ones_h[:, :], mask_h[:, k, :], start=(k == 0), stop=(k == TT - 1))
            mm.then_inc(spot_sum, 1)

            def sum_indices(e, n):
                pe.wait_ge(hot_ready, n)
                for i in range(TT):
                    r = table[:, i, e, :] if isinstance(e, int) else \
                        table[:, i, bass.ds(e, 1), :].rearrange("p a c -> p (a c)")
                    mm = MM(ps[:, 4, 0:3], one_hot[:, i, :], r, start=(i == 0), stop=(i == TT - 1))
                mm.then_inc(idx_sum, 1)

            def turn_x(n, n16):
                pe.wait_ge(gathered, n16)
                pe.wait_ge(idx_ready, n)
                for j in range(KT):
                    mm = TR(bank4(4 + j // 4)[:, j % 4, :], xg[:, P * j:P * j + P], ident[:, :])
                mm.then_inc(x_turned, 1)

            def turn_y(n):
                pe.wait_ge(yt_ready, n)
                pe.wait_ge(yr_ready, n)
                for j in range(KT):
                    mm = TR(bank4(6 + j // 4)[:, j % 4, :], y_t[:, j, :], ident[:, :])
                mm.then_inc(y_turned, 1)

            def gate_up(slot, xb, m, width, n):
                b = m % 2
                pe.wait_ge(gu_evac, n)
                for half in range(2):
                    for j in range(KT):
                        c = F * half + P * m
                        mm = MM(ps[:, b, BLK * half:BLK * half + width], gu_slot[slot][:, j, c:c + P],
                                xe_t[:, xb, j, 0:width], start=(j == 0), stop=(j == KT - 1))
                mm.then_inc(gu_done, 1)
                return mm

            def down(f, width, n_act):
                pe.wait_ge(act_ready, n_act)
                for d in range(KT):
                    mm = MM(bank4(2 + d // 4)[:, d % 4, 0:width], dn_slot[:, f, P * d:P * d + P],
                            act_t[:, f, 0:width], start=(f == 0 and d % 4 == 0), stop=(f == FT - 1),
                            skip_group_check=True)
                return mm

            sum_indices(0, 1)
            turn_x(1, 16)
            pe.wait_ge(extra_ready, 1)

            with pe.Fori(0, NE // 2) as it:
                for s in range(2):
                    slot = 1 - s

                    def ex(k, c):
                        return it * (2 * k) + (k * s + c)
                    pe.wait_ge(gu_loaded[slot], it * 64 + 64)
                    pe.wait_ge(xe_ready, ex(1, 1))
                    count = pe.value_load(counts_i[0:1, bass.ds(it * 2 + s, 1)], min_val=0, max_val=S)

                    def work(width):
                        for m in range(FT):
                            gate_up(slot, s, m, width, ex(FT, m + 1))
                            if m == 0:
                                turn_y(ex(1, 1))
                            if m == 2:
                                sum_indices(it * 2 + (s + 1), ex(1, 2))
                            if m == FT - 2:
                                turn_x(ex(1, 2), (it * 2 + (s + 2)) * 16)
                        for f in range(FT):
                            if f % 2 == 0:
                                pe.wait_ge(dn_loaded[f // 2], ex(16, 16))
                            mm = down(f, width, ex(FT, f + 1))
                            if f % 2:
                                mm.then_inc(dn_used, 1)
                    with pe.If(count > 96):
                        work(128)
                    with pe.Else():
                        with pe.If(count > 64):
                            work(96)
                        with pe.Else():
                            work(64)
            turn_y(NE + 1)
            n_extra = pe.value_load(counts_i[0:1, NE:NE + 1], min_val=0, max_val=MAX_EXTRA)
            with pe.Fori(0, MAX_EXTRA) as i:
                with pe.If(n_extra > i):
                    e = pe.value_load(extra_e[0:1, bass.ds(i, 1)], min_val=0, max_val=NE - 1)
                    sum_indices(e, i + (NE + 2))
                    turn_x(i + (NE + 2), (i + (NE + 2)) * 16)
                    pe.wait_ge(xe_ready, i + (NE + 2))
                    pe.wait_ge(ex_loaded, i * 128 + 128)
                    for m in range(FT):
                        gate_up(0, 0, m, BLK, i * FT + (FT * NE + m + 1))
                    for f in range(FT):
                        mm = down(f, BLK, i * FT + (FT * NE + f + 1))
                        if f % 2:
                            mm.then_inc(dn_used, 1)
                    turn_y(i + (NE + 2))


_INS = ["x", "positions", "attn_norm_w", "w_in", "lambda_q1", "lambda_k1", "lambda_q2", "lambda_k2",
        "subln_w", "pool_w", "pool_scale", "w_out", "ffn_norm_w", "router_w", "router_b",
        "w_gate_up", "b_gate_up", "w_down", "b_down", "final_norm_w"]


def kernel(**inputs):
    import numpy as _np
    import concourse.bacc as _bacc
    from concourse import mybir as _mybir
    from concourse.bass_utils import run_bass_kernel_spmd as _run

    nc = _bacc.Bacc("TRN2", target_bir_lowering=False, num_devices=1)
    arrays, args = {}, []
    for name in _INS:
        a = _np.ascontiguousarray(inputs[name])
        arrays[f"in_{name}"] = a
        args.append(nc.dram_tensor(f"in_{name}", a.shape, _mybir.dt.from_np(a.dtype), kind="ExternalInput").ap())
    args.append(nc.dram_tensor("out_dram", (1, S, D), _mybir.dt.float32, kind="ExternalOutput").ap())
    hybrid_block(nc, *args)
    r = _run(nc, [arrays], core_ids=[0])
    return r.results[0]["out_dram"]
```

```python
import concourse.bass as bass
from concourse import mybir
from contextlib import ExitStack
import math

import numpy as np

F32 = mybir.dt.float32
BF16 = mybir.dt.bfloat16
I32 = mybir.dt.int32
U32 = mybir.dt.uint32
ALU = mybir.AluOpType
ACT = mybir.ActivationFunctionType
AX = mybir.AxisListType.X

P = 128
S = 512
D = 1024
TT = S // P
KT = D // P
HEADS = 4
QKD = 64
ROT = 16
WINDOWS = (2, 4, 8, 16)
O_BANK = (5, 5, 4, 5)
POOL_ORDER = (3, 2, 1, 0)
NE = 32
TOPK = 4
F = D
FT = F // P
BLK = 128
HB = 64
SUB = 256
MAX_EXTRA = 15
LAM_INIT = 0.8 - 0.6 * math.exp(0.0)
SCALE = QKD ** -0.5
EPS = 1e-5
ALPHA = 1.702
LIMIT = 7.0
THETA = 500000.0
NEG = -1.0e30
OUT_OF_TOKENS = 1024
OUT_OF_ROWS = 4096
PI2_A = 6.28125
PI2_B = float(np.float32(2 * math.pi - PI2_A).view(np.int32) & -4096 and
              np.array([np.float32(2 * math.pi - PI2_A).view(np.int32) & -4096], np.int32).view(np.float32)[0])
PI2_C = float(np.float32(2 * math.pi - PI2_A - PI2_B))
ROUND = 12582912.0
PI_SAFE = 3.1415925


AHEAD = 3
LOOP_DVE = 2 * 8
EXTRA_DVE = 9
Q_AT = NE + 2 + MAX_EXTRA
D_AT = Q_AT + NE + 1


class Count:

    def __init__(self, eng, sem):
        self.eng, self.sem, self.n, self.off = eng, sem, 0, None

    def tick(self, ins):
        ins.then_inc(self.sem, 1)
        self.n += 1
        return self

    def settle(self):
        if self.off is None:
            self.eng.wait_ge(self.sem, self.n)
        else:
            self.eng.wait_ge(self.sem, self.off + self.n)


def hybrid_block(nc, x, positions, attn_norm_w, w_in, lambda_q1, lambda_k1, lambda_q2, lambda_k2,
                 subln_w, pool_w, pool_scale, w_out, ffn_norm_w, router_w, router_b,
                 w_gate_up, b_gate_up, w_down, b_down, final_norm_w, out, dbg=None):
    ctx = ExitStack()
    with ctx:
        def sb(name, shape, dt=F32):
            return ctx.enter_context(nc.sbuf_tensor(name, shape, dt))

        def sem(name):
            return ctx.enter_context(nc.semaphore(name))

        gu_slot = [sb("gu_slot_a", [P, KT, 2 * F]), sb("gu_slot_b", [P, KT, 2 * F])]
        dn_slot = sb("dn_slot", [P, FT, D])
        shared = sb("shared", [P, 9216])
        ident = sb("ident", [P, P])
        ident_h = sb("ident_h", [P, P], BF16)
        causal = sb("causal", [P, P], BF16)
        before = sb("before", [P, P], BF16)
        ones_h = sb("ones_h", [P, P], BF16)
        iota_n = sb("iota_n", [P, BLK])
        bias_parts = sb("bias_parts", [3 * NE, 3 * F], BF16)
        sel3 = sb("sel3", [3 * NE, NE + 1], BF16)
        router_sb = sb("router_sb", [P, KT, NE])
        router_bias = sb("router_bias", [P, NE])
        logits = sb("logits", [P, TT, NE])
        vec_t = sb("vec_t", [P, 36])
        small = sb("small", [P, 200])
        counts_i = sb("counts_i", [1, D_AT + NE + 1], I32)

        slot_a = gu_slot[0][:, :, :].rearrange("p a b -> p (a b)")
        slot_b = gu_slot[1][:, :, :].rearrange("p a b -> p (a b)")

        def part(flat, at, *dims):
            n = int(np.prod(dims))
            v = flat[:, at:at + n]
            if len(dims) == 1:
                return v
            names = "abcd"[:len(dims)]
            return v.rearrange("p (%s) -> p %s" % (" ".join(names), " ".join(names)),
                               **dict(zip(names, dims)))

        h_t = part(slot_a, 0, KT, S)
        qk_tok = part(slot_a, 4096, 2, TT, 512)
        qk_t = part(slot_a, 8192, 2, HEADS, S)
        v_sb = part(slot_a, 12288, TT, 512)
        u_t = part(slot_a, 14336, TT, S)
        probs = part(slot_a, 4096, 2, 2, 512)
        mix = part(slot_a, 6144, 2, 512)
        mix_t = part(slot_a, 7168, 2, 512)
        xn1_sb = part(slot_a, 14336, 2, D)
        w_in_sb = gu_slot[1]
        w_out_sb = dn_slot

        sh = shared[:, :]
        x_sb = part(sh, 0, TT, D)
        cat_t = part(sh, 4096, KT, S)
        o_sb = part(sh, 8192, 2, HEADS, P)
        pool_tmp = gu_slot[1][:, KT - 1, 0:S]
        pool_w_sb = gu_slot[1][:, KT - 1, S:2 * S].rearrange("p (g c) -> p g c", g=4)
        pool_d = cat_t[:, 4:8, :]
        bias_rows = shared[0:3 * NE, 4096:4096 + 3 * F]
        xn_sb = part(sh, 8192, D)
        xg = part(sh, 0, D)
        xe_t = part(sh, 1024, 2, KT, BLK)
        place = part(sh, 3072, 2, 2, HB)
        places = part(sh, 3072, 2 * BLK)
        bias_sel = part(sh, 3328, 64)[0:3 * NE, :].bitcast(BF16).rearrange("p (s n) -> p s n", s=2)
        y_rows = [part(sh, 3392, 512), part(sh, 8016, 512)]
        g_t = part(sh, 3904, 2, SUB)
        s_t = part(sh, 4416, 2, SUB)
        u1_t = part(sh, 4928, 2, SUB)
        act_sb = part(sh, 5440, 2, SUB)
        act_t = [part(sh, 5952, 4, P), part(sh, 8528, 4, P)]
        table = part(sh, 6464, 396).bitcast(BF16).rearrange("p (i e c) -> p i e c", i=TT, c=6)
        spot = part(sh, 9040, TT, NE + 2)
        one_hot = part(sh, 7504, 512).bitcast(BF16).rearrange("p (i n) -> p i n", i=TT)
        eq4 = part(sh, 7504, TT, TOPK, NE)
        eq4b = part(sh, 8016, TT, TOPK, NE)

        top8 = part(sh, 6992, TT, 8)
        top_idx = part(sh, 7024, TT, 8).bitcast(U32)
        idx_f = part(sh, 7056, TT, 8)
        mask_f = part(sh, 7088, TT, NE)
        mask_h = part(sh, 7216, TT * NE // 2).bitcast(BF16).rearrange("p (i e) -> p i e", i=TT)
        neg_top = part(sh, 7280, TT)
        gate4 = part(sh, 7284, TT, TOPK)
        gate_sum = part(sh, 7300, TT)
        dst4 = part(sh, 7304, TT, TOPK)
        tid4 = part(sh, 7320, TT)
        count_f = part(sh, 7324, NE)
        over = part(sh, 7356, NE)
        over_sum = part(sh, 7388, NE)
        zero32 = part(sh, 7420, NE)
        ov_e = part(sh, 7452, MAX_EXTRA)
        ov_b = part(sh, 7468, MAX_EXTRA)
        gate_f = part(sh, 8528, TT, NE)
        gate_r = part(sh, 8656, TT, NE)
        n_blocks = part(sh, 8784, NE)
        q_sum = part(sh, 8816, NE)
        q_f = part(sh, 8848, NE)
        ov_cmp = part(sh, 8016, MAX_EXTRA, NE)

        sm = small[:, :]
        ss_x = sm[:, 0:4]
        rstd_x = sm[:, 4:8]
        neg_lam = sm[:, 8:9]
        mx = part(sm, 9, 2, 2)
        nbias = part(sm, 13, 2, 2)
        esum = part(sm, 17, 2, 2)
        rsum = part(sm, 21, 2, 2)
        coef = part(sm, 25, 2, 1)
        ss_o = part(sm, 27, TT, HEADS)
        rstd_o = part(sm, 43, TT, HEADS)
        half_neg = sm[:, 59:75]
        gate_col = part(sm, 75, 2, 2, 1)
        idx_dst = part(sm, 79, 2, 2, 1).bitcast(U32)
        half_off = sm[:, 83:84]
        tmp_a = part(sm, 84, 2, 1)
        tmp_b = part(sm, 86, 2, 1)
        zero_col = sm[:, 88:89]
        token_sum = sm[:, 89:90]
        idx_src = sm[:, 125:127].bitcast(U32)
        spot_now = sm[:, 156:160]
        row_id = sm[:, 161:162]
        edge = sm[:, 164:180]
        extra_e = counts_i[0:1, NE + 2:NE + 2 + MAX_EXTRA]
        ss_2 = sm[:, 130:134]
        rstd_2 = sm[:, 134:138]
        extra_base = sm[:, 138:138 + MAX_EXTRA]

        rows = part(sh, 7168, P)[0:36, :]
        rows_i = part(sh, 7296, P)[0:36, :].bitcast(I32)
        AN, FN, PS, SL, POS = 0, 8, 16, 20, 32
        lam_in = part(sh, 7424, 256)[0:1, :].rearrange("p (a b c) -> p a b c", a=2, b=2)
        lam_pr = part(sh, 7680, 128)[0:1, :].rearrange("p (a c) -> p a c", a=2)
        lam_s = part(sh, 7808, 8)[0:1, :]
        ones_f = part(sh, 7824, P)[0:1, :]
        ang = part(sh, 8192, TT, 8)
        ang2 = part(sh, 8224, TT, 8)
        ang3 = part(sh, 8256, TT, 8)
        ang4 = part(sh, 8288, TT, 8)
        cos2 = part(sh, 8320, TT, ROT)
        sin2 = part(sh, 8384, TT, ROT)
        rot_a = part(sh, 8448, 2, 8, ROT)
        rot_b = part(sh, 8704, 2, 8, ROT)
        sq_junk = part(slot_a, 12288, D)

        ps = ctx.enter_context(nc.psum_tensor("ps", [P, 8, 512], F32))

        def x2h(i):
            return x_sb[:, i, :].rearrange("p (j t) -> p j t", j=KT)

        def bank4(b):
            return ps[:, b, :].rearrange("p (a c) -> p a c", a=4)

        x2_dram = nc.dram_tensor("x2_dram", [S, D], F32).ap()
        xn_dram = nc.dram_tensor("xn_dram", [S, D], F32).ap()
        ys_dram = nc.dram_tensor("ys_dram", [TOPK * S, D], F32).ap()

        x_tiles = x[0].rearrange("(i p) d -> i p d", p=P)
        out_tiles = out[0].rearrange("(i p) d -> i p d", p=P)
        x2_tiles = x2_dram.rearrange("(i p) d -> i p d", p=P)
        xn_tiles = xn_dram.rearrange("(i p) d -> i p d", p=P)
        ys_halves = ys_dram.rearrange("r (h d) -> (r h) d", h=2)
        ys_tiles = ys_dram.rearrange("(k i p) d -> i p k d", i=TT, p=P)
        w_in_v = w_in[0].rearrange("(j p) c -> p j c", p=P)
        w_out_v = w_out[0].rearrange("(j p) c -> p j c", p=P)
        w_gu_v = w_gate_up[0].rearrange("e (j p) c -> e p j c", p=P)
        w_dn_v = w_down[0].rearrange("e (j p) c -> e p j c", p=P)

        s_x = [sem(f"x_loaded{i}") for i in range(TT)]
        s_win = [sem(f"w_in_loaded{i}") for i in range(4)]
        s_wout = sem("w_out_loaded")
        s_small = sem("small_loaded")
        s_lam_in = sem("lambda_loaded")
        s_bias = sem("bias_rows_loaded")
        s_router = sem("router_loaded")
        s_poolw = sem("pool_w_loaded")
        gu_loaded = [[sem(f"gu_{slot}_loaded{c}") for c in range(KT)] for slot in "ab"]
        dn_loaded = [sem(f"dn_loaded{c}") for c in range(4)]
        dve_seq = sem("dve_seq")
        act_seq = sem("act_seq")
        pool_seq = sem("pool_seq")
        consts = sem("consts_ready")
        rows_ready = sem("rows_ready")
        turned = sem("vectors_turned")
        vec_ready = sem("vectors_ready")
        lam_exp = sem("lambda_exp")
        lam_sum = sem("lambda_sum")
        lam_bc = sem("lambda_spread")
        ang_ready = sem("angles_ready")
        sincos = sem("sincos_ready")
        rot_ready = sem("rope_tables_ready")
        sumsq = sem("sumsq_x")
        rstd_done = sem("rstd_x_done")
        xn_ready = sem("xn_ready")
        xn_turned = sem("xn_turned")
        ht_ready = sem("h_t_ready")
        proj = sem("qk_projected")
        proj_copied = sem("qk_copied")
        roped = sem("qk_roped")
        qk_turned = sem("qk_turned")
        qkt_ready = sem("qk_t_ready")
        v_proj = sem("v_projected")
        v_ready = sem("v_ready")
        u_proj = sem("u_projected")
        u_ready = sem("u_t_ready")
        scored = sem("scored")
        maxed = sem("row_max_ready")
        exped = sem("exp_done")
        coefed = sem("coef_ready")
        scaled = sem("map1_scaled")
        mixed = sem("mixed")
        mix_turned = sem("mix_turned")
        mixt_ready = sem("mix_t_ready")
        pv_done = sem("pv_done")
        o_copied = sem("o_copied")
        o_rstd = sem("o_rstd_done")
        o_normed = sem("o_normed")
        o_turned = sem("o_turned")
        cat_attn = sem("cat_attn_ready")
        pooled = sem("pool_diff_ready")
        pool_mm = sem("pool_projected")
        cat_pool = sem("cat_pool_ready")
        out_proj = sem("out_projected")
        x2_ready = sem("x2_ready")
        sumsq2 = sem("sumsq_x2")
        rstd2_done = sem("rstd_x2_done")
        xn2_ready = sem("xn2_ready")
        x2_stored = sem("x2_stored")
        xn_stored = sem("xn_stored")
        xn2_turned = sem("xn2_turned")
        h2_ready = sem("h2_t_ready")
        routed = sem("router_projected")
        logit_ready = sem("logits_ready")
        top_ready = sem("top_ready")
        gate_exp = sem("gate_exp_done")
        mask_ready = sem("mask_ready")
        spot_sum = sem("spots_summed")
        tables = sem("tables_ready")
        extra_ready = sem("extra_tasks_ready")
        hot_ready = sem("one_hot_ready")
        idx_sum = sem("indices_summed")
        idx_ready = sem("indices_ready")
        gathered = sem("rows_gathered")
        x_turned = sem("expert_rows_turned")
        xe_ready = sem("expert_x_t_ready")
        gu_done = sem("gate_up_done")
        g_ready = sem("gate_clamped")
        gu_evac = sem("gate_up_evacuated")
        sig_ready = sem("sigmoid_ready")
        act_ready = sem("act_ready")
        y_done = sem("y_done")
        glu_ready = sem("glu_ready")
        gates_taken = sem("gates_taken")
        dst_taken = sem("destinations_taken")
        act_turned = sem("act_turned")
        actt_ready = sem("act_t_ready")
        bias_split = sem("bias_parts_ready")
        yr_ready = sem("y_rows_ready")
        scattered = [sem(f"y_rows_scattered_block{b}") for b in range(2)]
        all_scattered = sem("all_scattered")
        pool_touched = sem("pool_touched")
        ex_loaded = sem("extra_weights_loaded")
        ys_loaded = [sem(f"ys_loaded{i}") for i in range(TT)]
        fnw_loaded = sem("final_norm_w_loaded")
        moe_sum = sem("moe_summed")
        sumsq3 = sem("sumsq_final")
        rstd3_done = sem("rstd_final_done")
        out_ready = sem("out_tile_ready")
        out_stored = sem("out_stored")
        slot_free = sem("slot_free")

        ys_sb = part(slot_a, 0, TT, TOPK, D)
        x2_sb = part(slot_b, 0, TT, D)
        fnw_sb = part(slot_b, 4096, D)
        sq3 = part(slot_b, 5120, D)

        block = ctx.enter_context(nc.Block())

        @block.sync
        def _(sp):
            for i in range(TT):
                sp.dma_start(x_sb[:, i, :], x_tiles[i]).then_inc(s_x[i], 16)
            for s in range(4):
                sp.dma_start(w_in_sb[:, :, 512 * s:512 * s + 512],
                             w_in_v[:, :, 512 * s:512 * s + 512]).then_inc(s_win[s], 16)
            sp.dma_start(w_out_sb[:, :, :], w_out_v).then_inc(s_wout, 16)

            def load_gu(slot, e, chunks=range(KT), signal=None, n_gu=None, n_dn=None):
                src = w_gu_v[e] if isinstance(e, int) else \
                    w_gu_v[bass.ds(e, 1)].rearrange("a p j c -> (a p) j c")
                for c in chunks:
                    if n_gu is not None:
                        if c < AHEAD:
                            sp.wait_ge(dn_loaded[4 + c - AHEAD], n_dn)
                        else:
                            sp.wait_ge(gu_loaded[slot][c - AHEAD], n_gu + 16)
                    sp.dma_start(gu_slot[slot][:, c, :], src[:, c, :]).then_inc(signal or gu_loaded[slot][c], 16)

            def load_dn(e, signal=None, slot=None, n_gu=None, n_dn=None):
                src = w_dn_v[e] if isinstance(e, int) else \
                    w_dn_v[bass.ds(e, 1)].rearrange("a p j c -> (a p) j c")
                for c in range(4):
                    if n_gu is not None:
                        if c < AHEAD:
                            sp.wait_ge(gu_loaded[slot][KT + c - AHEAD], n_gu + 16)
                        else:
                            sp.wait_ge(dn_loaded[c - AHEAD], n_dn + 16)
                    sp.dma_start(dn_slot[:, 2 * c:2 * c + 2, :],
                                 src[:, 2 * c:2 * c + 2, :]).then_inc(signal or dn_loaded[c], 16)

            sp.wait_ge(u_proj, 4)
            load_gu(1, 0, range(KT - 1))
            sp.wait_ge(pool_mm, 4)
            load_gu(1, 0, range(KT - 1, KT))
            sp.wait_ge(pv_done, 16)
            sp.wait_ge(o_copied, 16)
            load_gu(0, 1)
            sp.wait_ge(y_done, 1)
            load_dn(0)
            sp.wait_ge(extra_ready, 1)

            def blocks_before(e):
                at = Q_AT + e if isinstance(e, int) else e + Q_AT
                return sp.value_load(counts_i[0:1, at:at + 1] if isinstance(e, int) else
                                     counts_i[0:1, bass.ds(at, 1)], min_val=1, max_val=2 * NE)

            with sp.Fori(0, NE // 2 - 1) as it:
                for s in range(2):
                    q = blocks_before(it * 2 + (s + 1))
                    sp.wait_ge(gu_done, q * 2)
                    sp.sem_inc(slot_free, 1)
                    n_gu, n_dn = it * 16 + 16, it * 32 + (16 * s + 16)
                    load_gu(1 - s, it * 2 + (s + 2), n_gu=n_gu, n_dn=n_dn)
                    sp.wait_ge(y_done, q + 1)
                    sp.sem_inc(slot_free, 1)
                    load_dn(it * 2 + (s + 1), slot=1 - s, n_gu=n_gu, n_dn=n_dn)
            q = blocks_before(NE - 1)
            sp.wait_ge(y_done, q + 1)
            load_dn(NE - 1)
            q_all = blocks_before(NE)
            n_extra = sp.value_load(counts_i[0:1, NE:NE + 1], min_val=0, max_val=MAX_EXTRA)
            with sp.Fori(0, MAX_EXTRA) as i:
                with sp.If(n_extra > i):
                    e = sp.value_load(extra_e[0:1, bass.ds(i, 1)], min_val=0, max_val=NE - 1)
                    sp.wait_ge(y_done, q_all + i * 2 + 1)
                    load_gu(0, e, signal=ex_loaded)
                    load_dn(e, ex_loaded)
            sp.wait_ge(all_scattered, 1)
            for i in range(TT):
                sp.dma_start(x2_sb[:, i, :], x2_tiles[i]).then_inc(ys_loaded[i], 16)
                for k in range(0, TOPK, 2):
                    sp.dma_start(ys_sb[:, i, k:k + 2, :], ys_tiles[i][:, k:k + 2, :]).then_inc(ys_loaded[i], 16)
            for i in range(TT):
                sp.wait_ge(out_ready, i + 1)
                sp.dma_start(out_tiles[i], x2_sb[:, i, :]).then_inc(out_stored, 16)
            sp.wait_ge(out_stored, 16 * TT)

        @block.gpsimd
        def _(pool):
            seq = Count(pool, pool_seq)
            seq.tick(nc.gpsimd.memset(ident[:, :], 0.0))
            seq.tick(nc.gpsimd.memset(ident_h[:, :], 0.0))
            seq.tick(nc.gpsimd.memset(causal[:, :], 0.0))
            seq.tick(nc.gpsimd.memset(before[:, :], 1.0))
            seq.tick(nc.gpsimd.memset(sel3[:, :], 0.0))
            nc.gpsimd.memset(ones_h[:, :], 1.0).then_inc(consts, 1)
            nc.gpsimd.memset(half_neg, -0.5).then_inc(consts, 1)
            nc.gpsimd.memset(ones_f, 1.0).then_inc(consts, 1)
            seq.settle()
            for t in (ident, ident_h):
                nc.gpsimd.affine_select(out=t[:, :], in_=t[:, :], compare_op=ALU.not_equal, fill=1.0,
                                        base=0, pattern=[[-1, P]], channel_multiplier=1).then_inc(consts, 1)
            nc.gpsimd.affine_select(out=causal[:, :], in_=causal[:, :], compare_op=ALU.is_ge, fill=NEG,
                                    base=0, pattern=[[-1, P]], channel_multiplier=1).then_inc(consts, 1)
            nc.gpsimd.affine_select(out=before[:, :], in_=before[:, :], compare_op=ALU.is_ge, fill=0.0,
                                    base=-1, pattern=[[1, P]], channel_multiplier=-1).then_inc(consts, 1)
            for part3 in range(3):
                sel = nc.gpsimd.affine_select(out=sel3[:, 0:NE], in_=sel3[:, 0:NE], compare_op=ALU.not_equal,
                                              fill=1.0, base=-NE * part3, pattern=[[-1, NE]], channel_multiplier=1)
                if part3 < 2:
                    seq.tick(sel)
                    seq.settle()
                else:
                    sel.then_inc(consts, 1)
            nc.gpsimd.iota(row_id, pattern=[[0, 1]], base=0, channel_multiplier=1,
                           allow_small_or_imprecise_dtypes=True).then_inc(consts, 1)
            nc.gpsimd.iota(iota_n[:, :], pattern=[[1, BLK]], base=0, channel_multiplier=0,
                           allow_small_or_imprecise_dtypes=True).then_inc(consts, 1)

            def rstd(sums, result, exponent, width, signal):
                seq.tick(nc.gpsimd.tensor_scalar(result, sums, 1.0 / width, EPS, ALU.mult, ALU.add))
                seq.settle()
                nc.gpsimd.tensor_tensor(result, result, exponent, ALU.pow).then_inc(signal, 1)

            pool.wait_ge(consts, 10)
            for i in range(TT):
                pool.wait_ge(sumsq, i + 1)
                rstd(ss_x[:, i:i + 1], rstd_x[:, i:i + 1], half_neg[:, 0:1], D, rstd_done)

            pool.wait_ge(s_bias, 96)
            copy, sub = nc.gpsimd.tensor_copy, ALU.subtract
            seq.tick(copy(bias_parts[:, :], bias_rows))
            seq.settle()
            for first in (NE, 2 * NE):
                for again in range(first // NE):
                    r3 = slice(first, first + NE)
                    seq.tick(nc.gpsimd.tensor_tensor(bias_rows[r3, :], bias_rows[r3, :], bias_parts[r3, :], sub))
                    seq.settle()
                    seq.tick(copy(bias_parts[r3, :], bias_rows[r3, :]))
                    seq.settle()
            nc.gpsimd.tensor_scalar(zero_col, half_neg[:, 0:1], 0.0, 0.0, ALU.mult, ALU.add).then_inc(bias_split, 1)

            def o_rstds(i):
                pool.wait_ge(o_copied, 4 * i + 4)
                rstd(ss_o[:, i, :], rstd_o[:, i, :], half_neg[:, 0:4], P, o_rstd)

            pool.wait_ge(turned, 1)
            pool.wait_ge(lam_bc, 1)
            pool.wait_ge(v_proj, 4)
            pool.dma_start(pool_w_sb, pool_w[0].rearrange("g c d -> c g d")).then_inc(s_poolw, 16)
            pool.wait_ge(rows_ready, 3)
            for n, g in enumerate(POOL_ORDER):
                w = WINDOWS[g]
                pool.wait_ge(u_ready, n + 1)
                bufs = [pool_tmp, pool_d[:, g, :]]
                src, step = u_t[:, g, :], 1
                while step < w:
                    dst = bufs[0]
                    seq.tick(nc.gpsimd.tensor_copy(dst[:, 0:step], src[:, 0:step]))
                    seq.tick(nc.gpsimd.tensor_tensor(dst[:, step:S], src[:, step:S], src[:, 0:S - step], ALU.add))
                    seq.settle()
                    src, step, bufs = dst, 2 * step, bufs[::-1]
                seq.tick(nc.gpsimd.tensor_tensor(src[:, 0:w], src[:, 0:w], edge[:, 0:w], ALU.mult))
                seq.tick(nc.gpsimd.tensor_scalar(src[:, w:S], src[:, w:S], 1.0 / w, 0.0, ALU.mult, ALU.add))
                seq.settle()
                nc.gpsimd.tensor_tensor(pool_d[:, g, :], src, u_t[:, g, :], ALU.subtract).then_inc(pooled, 1)
                pool.wait_ge(pooled, n + 1)
                o_rstds(n)

            for i in range(TT):
                pool.wait_ge(sumsq2, i + 1)
                rstd(ss_2[:, i:i + 1], rstd_2[:, i:i + 1], half_neg[:, 0:1], D, rstd2_done)

            pool.wait_ge(x2_stored, 16 * TT)
            pool.wait_ge(xn2_ready, TT)
            nc.gpsimd.memset(xg, 0.0).then_inc(tables, 1)
            pool.wait_ge(tables, 1)

            def touch(at, signal=pool_touched):
                return nc.gpsimd.tensor_tensor(sm[:, 180 + at:181 + at], half_neg[:, 0:1], half_neg[:, 0:1],
                                               ALU.add).then_inc(signal, 1)

            def gather(b, n_idx):
                pool.wait_ge(idx_ready, n_idx)
                touch(2)
                pool.indirect_dma_start(
                    out=xg, out_offset=None, in_=xn_dram,
                    in_offset=bass.IndirectOffsetOnAxis(ap=idx_src[:, b:b + 1], axis=0),
                    bounds_check=S - 1, oob_is_err=False).then_inc(gathered, 16)

            def scatter(s, b, n_rows):
                pool.wait_ge(yr_ready, n_rows)
                touch(b)
                pool.indirect_dma_start(
                    out=ys_halves, out_offset=bass.IndirectOffsetOnAxis(ap=idx_dst[:, s, b, :], axis=0),
                    in_=y_rows[b], in_offset=None,
                    bounds_check=2 * TOPK * S - 1, oob_is_err=False).then_inc(scattered[b], 16)

            pool.wait_ge(xn_stored, 16 * TT)
            gather(0, 1)
            pool.wait_ge(extra_ready, 1)
            for b in range(2):
                pool.dma_start(y_rows[b][:, 0:1], half_neg[:, 0:1]).then_inc(scattered[b], 16)
            with pool.Fori(0, NE // 2) as it:
                for s in range(2):
                    e = it * 2 + s
                    q = pool.value_load(counts_i[0:1, bass.ds(e + Q_AT, 1)], min_val=0, max_val=2 * NE)
                    count = pool.value_load(counts_i[0:1, bass.ds(e, 1)], min_val=0, max_val=S)
                    gather(1 - s, it * 2 + (s + 2))
                    scatter(s, 0, q + 2)
                    with pool.If(count > HB):
                        scatter(s, 1, q + 3)
            q_all = pool.value_load(counts_i[0:1, Q_AT + NE:Q_AT + NE + 1], min_val=0, max_val=2 * NE)
            d_all = pool.value_load(counts_i[0:1, D_AT + NE:D_AT + NE + 1], min_val=0, max_val=NE)
            n_extra = pool.value_load(counts_i[0:1, NE:NE + 1], min_val=0, max_val=MAX_EXTRA)
            with pool.Fori(0, MAX_EXTRA) as i:
                with pool.If(n_extra > i):
                    gather(0, i + (NE + 2))
                    scatter(0, 0, q_all + i * 2 + 2)
                    scatter(0, 1, q_all + i * 2 + 3)
            pool.wait_ge(scattered[0], (n_extra + (NE + 1)) * 16)
            pool.wait_ge(scattered[1], (d_all + n_extra + 1) * 16)
            touch(3, all_scattered)

            for i in range(TT):
                pool.wait_ge(sumsq3, i + 1)
                rstd(ss_x[:, i:i + 1], rstd_x[:, i:i + 1], half_neg[:, 0:1], D, rstd3_done)

        @block.scalar
        def _(act):
            seq = Count(act, act_seq)
            for at, w, n in ((AN, attn_norm_w, 8), (FN, ffn_norm_w, 8), (PS, pool_scale, 4), (SL, subln_w, 1)):
                act.wait_ge(rows_ready, 1)
                act.dma_start(rows[at:at + n, :], w[0].rearrange("(a b) -> a b", b=P)).then_inc(s_small, 16)
            act.dma_start(rows_i[POS:POS + 4, :], positions[0].rearrange("(a b) -> a b", b=P)).then_inc(s_small, 16)
            for r in range(3):
                act.dma_start(bias_rows[NE * r:NE * r + NE, 0:2 * F], b_gate_up[0]).then_inc(s_bias, 16)
                act.dma_start(bias_rows[NE * r:NE * r + NE, 2 * F:3 * F], b_down[0]).then_inc(s_bias, 16)
            for a, (q, k) in enumerate(((lambda_q1, lambda_k1), (lambda_q2, lambda_k2))):
                act.dma_start(lam_in[:, a, 0, :], q).then_inc(s_lam_in, 16)
                act.dma_start(lam_in[:, a, 1, :], k).then_inc(s_lam_in, 16)
            act.dma_start(router_sb[:, :, :], router_w[0].rearrange("(j p) e -> p j e", p=P)).then_inc(s_router, 16)
            act.dma_start(router_bias[:, :], router_b.to_broadcast([P, NE])).then_inc(s_router, 16)
            for i in range(TT):
                act.wait_ge(s_x[i], 16)
                if i:
                    act.wait_ge(sumsq, i)
                nc.scalar.activation(sq_junk, x_sb[:, i, :], ACT.Square, accum_out=ss_x[:, i:i + 1]).then_inc(sumsq, 1)
            act.wait_ge(lam_sum, 1)
            nc.scalar.activation(lam_s[:, 2:4], lam_s[:, 0:2], ACT.Exp).then_inc(lam_exp, 1)
            act.wait_ge(ang_ready, 1)
            nc.scalar.activation(ang3, ang, ACT.Sin).then_inc(sincos, 1)
            nc.scalar.activation(ang4, ang2, ACT.Sin).then_inc(sincos, 1)

            def copy_qkt(n):
                s, i = divmod(n, TT)
                act.wait_ge(qk_turned, n + 1)
                nc.scalar.activation(qk_t[:, s, :, P * i:P * i + P], bank4(4 + n % 2), ACT.Copy).then_inc(qkt_ready, 1)

            for n in range(8):
                act.wait_ge(proj, n + 1)
                nc.scalar.activation(qk_tok[:, n // TT, n % TT, :], ps[:, n % 4, :], ACT.Copy).then_inc(proj_copied, 1)
                if n >= 2:
                    copy_qkt(n - 2)
            copy_qkt(6)
            copy_qkt(7)
            for i in range(TT):
                act.wait_ge(v_proj, i + 1)
                nc.scalar.activation(v_sb[:, i, :], ps[:, i, :], ACT.Copy).then_inc(v_ready, 1)

            def take_o(n):
                i, h = divmod(n, HEADS)
                act.wait_ge(pv_done, n + 1)
                if n == 0:
                    act.wait_ge(roped, 8)
                if h == 0 and i >= 2:
                    act.wait_ge(o_turned, i - 1)
                seq.tick(nc.scalar.activation(o_sb[:, i % 2, h, :], ps[:, 6, P * h:P * h + P], ACT.Square,
                                              accum_out=ss_o[:, i, h:h + 1]))
                seq.settle()
                nc.scalar.activation(o_sb[:, i % 2, h, :], ps[:, 6, P * h:P * h + P], ACT.Copy).then_inc(o_copied, 1)

            for n in range(16):
                i, h = divmod(n, HEADS)
                b, w = n % 2, P * (i + 1)
                act.wait_ge(maxed, n + 1)
                if n >= 2:
                    act.wait_ge(mixed, n - 1)
                for m in range(2):
                    nc.scalar.activation(probs[:, b, m, 0:w], ps[:, 2 * b + m, 0:w], ACT.Exp,
                                         bias=nbias[:, b, m:m + 1], scale=SCALE,
                                         accum_out=esum[:, b, m:m + 1]).then_inc(exped, 1)
                act.wait_ge(coefed, n + 1)
                act.wait_ge(exped, 2 * n + 2)
                nc.scalar.activation(probs[:, b, 1, 0:w], probs[:, b, 1, 0:w], ACT.Copy,
                                     scale=coef[:, b, 0:1]).then_inc(scaled, 1)
                if n % 4 == 3:
                    g = n // 4
                    act.wait_ge(u_proj, g + 1)
                    nc.scalar.activation(u_t[:, POOL_ORDER[g], :], ps[:, 7, :], ACT.Copy).then_inc(u_ready, 1)
                if n >= 3:
                    take_o(n - 3)
            for n in range(13, 16):
                take_o(n)
            act.wait_ge(o_copied, 16)
            for n, g in enumerate(POOL_ORDER):
                act.wait_ge(pool_mm, n + 1)
                nc.scalar.activation(cat_t[:, 4 + g, :], ps[:, g, :], ACT.Copy,
                                     scale=vec_t[:, PS + g:PS + g + 1]).then_inc(cat_pool, 1)

            for i in range(TT):
                act.wait_ge(x2_ready, i + 1)
                act.dma_start(x2_tiles[i], x_sb[:, i, :]).then_inc(x2_stored, 16)
                if i:
                    act.wait_ge(xn_stored, 16 * i)
                    act.wait_ge(xn2_turned, i)
                else:
                    act.wait_ge(o_turned, TT)
                nc.scalar.activation(xn_sb, x_sb[:, i, :], ACT.Square,
                                     accum_out=ss_2[:, i:i + 1]).then_inc(sumsq2, 1)
                act.wait_ge(xn2_ready, i + 1)
                act.dma_start(xn_tiles[i], xn_sb).then_inc(xn_stored, 16)

            act.wait_ge(top_ready, 1)
            for i in range(TT):
                nc.scalar.activation(gate4[:, i, :], top8[:, i, 0:TOPK], ACT.Exp, bias=neg_top[:, i:i + 1],
                                     accum_out=gate_sum[:, i:i + 1]).then_inc(gate_exp, 1)

            def sigmoids(q):
                for sub in range(2):
                    act.wait_ge(g_ready, q * 2 + (sub + 1))
                    nc.scalar.activation(s_t[:, sub, :], g_t[:, sub, :], ACT.Sigmoid, scale=ALPHA).then_inc(sig_ready, 1)

            def gate_rows(s, b, q, n_before):
                act.wait_ge(scattered[b], n_before * 16 + 16)
                act.wait_ge(y_done, q + 2)
                nc.scalar.activation(y_rows[b], ps[:, 4, :], ACT.Copy, scale=gate_col[:, s, b, :]).then_inc(yr_ready, 1)

            act.wait_ge(extra_ready, 1)
            with act.Fori(0, NE // 2) as it:
                for s in range(2):
                    e = it * 2 + s
                    q = act.value_load(counts_i[0:1, bass.ds(e + Q_AT, 1)], min_val=0, max_val=2 * NE)
                    d = act.value_load(counts_i[0:1, bass.ds(e + D_AT, 1)], min_val=0, max_val=NE)
                    count = act.value_load(counts_i[0:1, bass.ds(e, 1)], min_val=0, max_val=S)
                    sigmoids(q)
                    with act.If(count > HB):
                        sigmoids(q + 1)
                    gate_rows(s, 0, q, e)
                    with act.If(count > HB):
                        gate_rows(s, 1, q + 1, d)
            q_all = act.value_load(counts_i[0:1, Q_AT + NE:Q_AT + NE + 1], min_val=0, max_val=2 * NE)
            d_all = act.value_load(counts_i[0:1, D_AT + NE:D_AT + NE + 1], min_val=0, max_val=NE)
            n_extra = act.value_load(counts_i[0:1, NE:NE + 1], min_val=0, max_val=MAX_EXTRA)
            with act.Fori(0, MAX_EXTRA) as i:
                with act.If(n_extra > i):
                    sigmoids(q_all + i * 2)
                    sigmoids(q_all + (i * 2 + 1))
                    gate_rows(0, 0, q_all + i * 2, i + NE)
                    gate_rows(0, 1, q_all + (i * 2 + 1), d_all + i)

            act.wait_ge(all_scattered, 1)
            act.dma_start(fnw_sb, final_norm_w.rearrange("(a n) -> a n", a=1).to_broadcast([P, D])).then_inc(fnw_loaded, 16)
            for i in range(TT):
                act.wait_ge(moe_sum, i + 1)
                if i:
                    act.wait_ge(sumsq3, i)
                nc.scalar.activation(sq3, x2_sb[:, i, :], ACT.Square,
                                     accum_out=ss_x[:, i:i + 1]).then_inc(sumsq3, 1)

        @block.vector
        def _(dve):
            V = nc.vector
            seq = Count(dve, dve_seq)
            V.memset(rows, 0.0).then_inc(rows_ready, 1)
            dve.wait_ge(s_small, 16 * 5)
            V.tensor_copy(rows[POS:POS + 4, :], rows_i[POS:POS + 4, :]).then_inc(rows_ready, 1)
            dve.wait_ge(consts, 10)
            seq.tick(V.tensor_scalar(edge, iota_n[:, 0:16], 1.0, None, ALU.add))
            seq.settle()
            V.reciprocal(edge, edge).then_inc(rows_ready, 1)
            dve.wait_ge(s_lam_in, 64)
            seq.tick(V.tensor_tensor(lam_pr, lam_in[:, :, 0, :], lam_in[:, :, 1, :], ALU.mult))
            seq.settle()
            V.reduce_sum(lam_s[:, 0:2], lam_pr, AX).then_inc(lam_sum, 1)

            def norm_x(i):
                dve.wait_ge(rstd_done, i + 1)
                if i >= 2:
                    dve.wait_ge(xn_turned, i - 1)
                V.tensor_scalar(xn1_sb[:, i % 2, :], x_sb[:, i, :], rstd_x[:, i:i + 1], None, ALU.mult).then_inc(xn_ready, 1)

            dve.wait_ge(turned, 1)
            V.tensor_copy(vec_t[:, :], ps[:, 3, 0:36]).then_inc(vec_ready, 1)
            dve.wait_ge(vec_ready, 1)
            norm_x(0)
            for i in range(TT):
                if i + 1 < TT:
                    norm_x(i + 1)
                dve.wait_ge(xn_turned, i + 1)
                for half in range(2):
                    V.tensor_tensor(h_t[:, 4 * half:4 * half + 4, P * i:P * i + P], bank4(4 + half),
                                    vec_t[:, AN + 4 * half:AN + 4 * half + 4, None].to_broadcast([P, 4, P]),
                                    ALU.mult).then_inc(ht_ready, 1)
                if i == 0:
                    dve.wait_ge(lam_exp, 1)
                    seq.tick(V.tensor_tensor(lam_s[:, 4:5], lam_s[:, 3:4], lam_s[:, 2:3], ALU.subtract))
                    seq.settle()
                    V.tensor_scalar(lam_s[:, 5:6], lam_s[:, 4:5], -LAM_INIT, None, ALU.add).then_inc(lam_sum, 1)
            inv_freq = np.float32(THETA) ** (-np.arange(0, ROT, 2, dtype=np.float32) / np.float32(ROT))
            for f in range(ROT // 2):
                seq.tick(V.tensor_scalar(ang[:, :, f], vec_t[:, POS:POS + 4], float(inv_freq[f]), None, ALU.mult))
            seq.settle()
            seq.tick(V.tensor_scalar(ang2, ang, 1.0 / (2 * math.pi), ROUND, ALU.mult, ALU.add))
            seq.settle()
            seq.tick(V.tensor_scalar(ang2, ang2, -ROUND, None, ALU.add))
            seq.settle()
            for piece in (PI2_A, PI2_B, PI2_C):
                seq.tick(V.scalar_tensor_tensor(ang, ang2, -piece, ang, ALU.mult, ALU.add))
                seq.settle()
            seq.tick(V.tensor_scalar(ang2, ang, math.pi / 2, None, ALU.add))
            seq.settle()
            seq.tick(V.tensor_scalar(ang3, ang2, math.pi, -2 * math.pi, ALU.is_gt, ALU.mult))
            seq.settle()
            seq.tick(V.tensor_tensor(ang2, ang2, ang3, ALU.add))
            seq.tick(V.tensor_scalar(ang, ang, PI_SAFE, -PI_SAFE, ALU.min, ALU.max))
            seq.settle()
            V.tensor_scalar(ang2, ang2, PI_SAFE, -PI_SAFE, ALU.min, ALU.max).then_inc(ang_ready, 1)
            dve.wait_ge(sincos, 2)
            seq.tick(V.tensor_copy(cos2[:, :, 0:8], ang4))
            seq.tick(V.tensor_copy(cos2[:, :, 8:16], ang4))
            seq.tick(V.tensor_copy(sin2[:, :, 8:16], ang3))
            seq.tick(V.tensor_scalar(sin2[:, :, 0:8], ang3, -1.0, None, ALU.mult))
            seq.settle()
            dve.wait_ge(lam_bc, 1)
            seq.tick(V.tensor_copy(neg_lam, ps[:, 7, 0:1]))

            for n in range(8):
                s, i = divmod(n, TT)
                dve.wait_ge(proj_copied, n + 1)
                src = ps[:, n % 4, :].rearrange("p (g d) -> p g d", g=8)
                dst = qk_tok[:, s, i, :].rearrange("p (g d) -> p g d", g=8)
                ra, rb = rot_a[:, n % 2], rot_b[:, n % 2]
                co = cos2[:, i, None, :].to_broadcast([P, 8, ROT])
                si = sin2[:, i, None, :].to_broadcast([P, 8, ROT])
                seq.tick(V.tensor_tensor(ra, src[:, :, 0:16], co, ALU.mult))
                seq.tick(V.tensor_tensor(rb[:, :, 0:8], src[:, :, 8:16], si[:, :, 0:8], ALU.mult))
                seq.tick(V.tensor_tensor(rb[:, :, 8:16], src[:, :, 0:8], si[:, :, 8:16], ALU.mult))
                seq.settle()
                V.tensor_tensor(dst[:, :, 0:16], ra, rb, ALU.add).then_inc(roped, 1)

            def evac_mix(n):
                w = P * (n // HEADS + 1)
                dve.wait_ge(mix_turned, n + 1)
                V.tensor_copy(mix_t[:, n % 2, 0:w], ps[:, 4 + n % 2, 0:w]).then_inc(mixt_ready, 1)

            def norm_o(i):
                dve.wait_ge(o_rstd, i + 1)
                V.tensor_tensor(o_sb[:, i % 2], o_sb[:, i % 2], rstd_o[:, i, :, None].to_broadcast([P, HEADS, P]),
                                ALU.mult).then_inc(o_normed, 1)

            def take_cat(i):
                dve.wait_ge(o_turned, i + 1)
                V.tensor_scalar(cat_t[:, 0:4, P * i:P * i + P], bank4(O_BANK[i]), vec_t[:, SL:SL + 1],
                                1.0 - LAM_INIT, ALU.mult, ALU.mult).then_inc(cat_attn, 1)

            for n in range(16):
                b, w = n % 2, P * (n // HEADS + 1)
                if n >= 10 and (n - 10) % 4 == 0:
                    take_cat((n - 10) // 4)
                dve.wait_ge(scored, n + 1)
                seq.tick(V.reduce_max(mx[:, b, :], ps[:, 2 * b:2 * b + 2, 0:w], AX))
                seq.settle()
                V.tensor_scalar(nbias[:, b, :], mx[:, b, :], -SCALE, None, ALU.mult).then_inc(maxed, 1)
                if n >= 2:
                    evac_mix(n - 2)
                if n >= 9 and (n - 9) % 4 == 0:
                    norm_o((n - 9) // 4)
                dve.wait_ge(exped, 2 * n + 2)
                seq.tick(V.reciprocal(rsum[:, b, :], esum[:, b, :]))
                seq.settle()
                V.tensor_tensor(coef[:, b, :], rsum[:, b, 1:2], neg_lam, ALU.mult).then_inc(coefed, 1)
                dve.wait_ge(scaled, n + 1)
                V.scalar_tensor_tensor(mix[:, b, 0:w], probs[:, b, 0, 0:w], rsum[:, b, 0:1], probs[:, b, 1, 0:w],
                                       ALU.mult, ALU.add).then_inc(mixed, 1)
            evac_mix(14)
            evac_mix(15)
            for i in (2, 3):
                norm_o(i)
                take_cat(i)

            for i in range(TT):
                dve.wait_ge(out_proj, i + 1)
                V.tensor_tensor(x_sb[:, i, :], x_sb[:, i, :],
                                ps[:, 2 * (i % 2):2 * (i % 2) + 2, :].rearrange("p a b -> p (a b)"),
                                ALU.add).then_inc(x2_ready, 1)
                dve.wait_ge(rstd2_done, i + 1)
                if i:
                    dve.wait_ge(xn_stored, 16 * i)
                    dve.wait_ge(xn2_turned, i)
                else:
                    dve.wait_ge(cat_attn, TT)
                V.tensor_scalar(xn_sb, x_sb[:, i, :], rstd_2[:, i:i + 1], None, ALU.mult).then_inc(xn2_ready, 1)
                dve.wait_ge(xn2_turned, i + 1)
                dve.wait_ge(x2_stored, 16 * i + 16)
                V.tensor_tensor(x2h(i), ps[:, 4:6, :].rearrange("p a (c n) -> p (a c) n", c=4),
                                vec_t[:, FN:FN + 8, None].to_broadcast([P, KT, P]), ALU.mult).then_inc(h2_ready, 1)
                dve.wait_ge(routed, i + 1)
                V.tensor_tensor(logits[:, i, :], ps[:, 6, NE * i:NE * i + NE], router_bias[:, :],
                                ALU.add).then_inc(logit_ready, 1)

            dve.wait_ge(logit_ready, TT)
            for i in range(TT):
                seq.tick(V.max(top8[:, i, :], logits[:, i, :]))
            seq.settle()
            seq.tick(V.tensor_scalar(neg_top, top8[:, :, 0], -1.0, None, ALU.mult))
            for i in range(TT):
                seq.tick(V.max_index(top_idx[:, i, :], top8[:, i, :], logits[:, i, :]))
            seq.settle()
            V.tensor_copy(idx_f, top_idx).then_inc(top_ready, 1)
            dve.wait_ge(top_ready, 1)
            seq.tick(V.tensor_tensor(eq4, iota_n[:, None, None, 0:NE].to_broadcast([P, TT, TOPK, NE]),
                                     idx_f[:, :, 0:TOPK, None].to_broadcast([P, TT, TOPK, NE]), ALU.is_equal))
            seq.settle()
            seq.tick(V.reduce_sum(mask_f, eq4.rearrange("p i k e -> p i e k"), AX))
            seq.settle()
            V.tensor_copy(mask_h, mask_f).then_inc(mask_ready, 1)
            dve.wait_ge(gate_exp, TT)
            seq.tick(V.reciprocal(gate_sum, gate_sum))
            seq.settle()
            seq.tick(V.tensor_tensor(gate4, gate4, gate_sum[:, :, None].to_broadcast([P, TT, TOPK]), ALU.mult))
            seq.tick(V.memset(half_off[0:HB, :], 2.0 * OUT_OF_ROWS))
            seq.tick(V.memset(half_off[HB:P, :], 2.0 * OUT_OF_ROWS + 1.0))
            seq.tick(V.memset(table, 0.0))
            for k in range(TOPK):
                seq.tick(V.memset(dst4[:, :, k:k + 1], float(S * k - OUT_OF_ROWS + OUT_OF_TOKENS)))
            seq.settle()
            seq.tick(V.tensor_scalar(table[:, :, 0:NE, 0], mask_f, row_id, None, ALU.mult))
            for i in range(TT):
                seq.tick(V.tensor_scalar(table[:, i, 0:NE, 1], mask_f[:, i, :], float(P * i - OUT_OF_TOKENS), None,
                                         ALU.mult))
            dve.wait_ge(xn_stored, 16 * TT)
            seq.tick(V.tensor_tensor(eq4b, eq4, gate4[:, :, :, None].to_broadcast([P, TT, TOPK, NE]), ALU.mult))
            seq.settle()
            seq.tick(V.reduce_sum(gate_f, eq4b.rearrange("p i k e -> p i e k"), AX))
            seq.settle()
            seq.tick(V.tensor_tensor(eq4b, eq4, dst4[:, :, :, None].to_broadcast([P, TT, TOPK, NE]), ALU.mult))
            for c in (2, 3, 4):
                seq.tick(V.tensor_copy(table[:, :, 0:NE, c], gate_f))
                seq.settle()
                if c < 4:
                    seq.tick(V.tensor_tensor(gate_f, gate_f, table[:, :, 0:NE, c], ALU.subtract))
                    seq.settle()
            seq.tick(V.reduce_sum(gate_r, eq4b.rearrange("p i k e -> p i e k"), AX))
            seq.settle()
            seq.tick(V.tensor_copy(table[:, :, 0:NE, 5], gate_r))
            dve.wait_ge(spot_sum, 1)
            seq.tick(V.scalar_tensor_tensor(spot[:, :, 0:NE], ps[:, 4, 0:TT * NE].rearrange("p (i e) -> p i e", i=TT),
                                            1.0, mask_f, ALU.add, ALU.mult))
            seq.tick(V.memset(spot[:, :, NE:NE + 2], 0.0))
            seq.settle()
            seq.tick(V.tensor_scalar(spot, spot, -1.0, None, ALU.add))
            seq.tick(V.tensor_copy(counts_i[0:1, 0:NE], ps[0:1, 5, 0:NE]))
            seq.tick(V.tensor_copy(count_f, ps[:, 5, 0:NE]))
            seq.tick(V.memset(zero32, 0.0))
            seq.settle()
            seq.tick(V.tensor_scalar(n_blocks, count_f, float(HB), 1.0, ALU.is_gt, ALU.add))
            seq.settle()
            seq.tick(V.tensor_tensor_scan(q_sum, n_blocks, zero32, 0.0, ALU.add, ALU.add))
            seq.settle()
            seq.tick(V.tensor_tensor(q_f, q_sum, n_blocks, ALU.subtract))
            seq.tick(V.tensor_copy(counts_i[0:1, Q_AT + NE:Q_AT + NE + 1], q_sum[0:1, NE - 1:NE]))
            seq.settle()
            seq.tick(V.tensor_copy(counts_i[0:1, Q_AT:Q_AT + NE], q_f[0:1, :]))
            seq.tick(V.tensor_tensor(counts_i[0:1, D_AT:D_AT + NE], q_f[0:1, :], iota_n[0:1, 0:NE], ALU.subtract))
            seq.tick(V.tensor_scalar(counts_i[0:1, D_AT + NE:D_AT + NE + 1], q_sum[0:1, NE - 1:NE], -float(NE), None,
                                     ALU.add))

            def select_bias(s, e):
                src = sel3[:, e:e + 1] if isinstance(e, int) else sel3[:, bass.ds(e, 1)]
                seq.tick(V.tensor_copy(bias_sel[:, s, :], src.to_broadcast([3 * NE, HB])))

            def hot(e):
                src = spot[:, :, e:e + 1] if isinstance(e, int) else spot[:, :, bass.ds(e, 1)]
                V.tensor_tensor(one_hot, places[:, None, :].to_broadcast([P, TT, 2 * BLK]),
                                src.to_broadcast([P, TT, 2 * BLK]), ALU.is_equal).then_inc(hot_ready, 1)

            both = ps[:, 5, 2:14].rearrange("p (b c) -> p b c", b=2)

            def take_tokens(s, n):
                dve.wait_ge(idx_sum, n)
                seq.tick(V.tensor_scalar(token_sum, ps[:, 5, 0:1], float(OUT_OF_TOKENS), None, ALU.add))
                seq.settle()
                seq.tick(V.tensor_tensor(token_sum, token_sum, ps[:, 5, 1:2], ALU.add))
                seq.settle()
                V.tensor_copy(idx_src[:, s:s + 1], token_sum).then_inc(idx_ready, 1)

            def take_rows(s):
                seq.tick(V.tensor_copy(tmp_a, both[:, :, 2:3]))
                seq.tick(V.tensor_copy(tmp_b, both[:, :, 0:1]))
                seq.settle()
                seq.tick(V.tensor_tensor(tmp_a, tmp_a, both[:, :, 3:4], ALU.add))
                seq.tick(V.tensor_tensor(tmp_b, tmp_b, both[:, :, 1:2], ALU.add))
                seq.settle()
                V.tensor_tensor(gate_col[:, s], tmp_a, both[:, :, 4:5], ALU.add).then_inc(gates_taken, 1)
                seq.tick(V.tensor_tensor(tmp_b, tmp_b, both[:, :, 5:6], ALU.add))
                seq.settle()
                V.tensor_scalar(idx_dst[:, s], tmp_b, 2.0, half_off, ALU.mult, ALU.add).then_inc(dst_taken, 1)

            def take_x(b, n):
                dve.wait_ge(x_turned, n)
                V.tensor_tensor(xe_t[:, b], ps[:, 6:8, :].rearrange("p a (c n) -> p (a c) n", c=4),
                                vec_t[:, FN:FN + 8, None].to_broadcast([P, KT, BLK]), ALU.mult).then_inc(xe_ready, 1)

            def clamp(sub, q):
                dve.wait_ge(gu_done, q * 2 + (sub + 1))
                V.tensor_scalar(g_t[:, sub, :], ps[:, sub, 0:SUB], LIMIT, None, ALU.min).then_inc(g_ready, 1)
                V.tensor_scalar(u1_t[:, sub, :], ps[:, sub, SUB:2 * SUB], -LIMIT, LIMIT,
                                ALU.max, ALU.min).then_inc(gu_evac, 1)

            def glu(sub, q):
                dve.wait_ge(sig_ready, q * 2 + (sub + 1))
                V.tensor_tensor(s_t[:, sub, :], g_t[:, sub, :], s_t[:, sub, :], ALU.mult).then_inc(glu_ready, 1)
                dve.wait_ge(gu_evac, q * 2 + (sub + 3))
                dve.wait_ge(glu_ready, q * 2 + (sub + 1))
                V.scalar_tensor_tensor(act_sb[:, sub, :], u1_t[:, sub, :], 1.0, s_t[:, sub, :],
                                       ALU.add, ALU.mult).then_inc(act_ready, 1)

            def take_act(b, sub, q):
                dve.wait_ge(act_turned, q * 2 + (sub + 1))
                V.tensor_copy(act_t[b][:, 2 * sub:2 * sub + 2, :],
                              ps[:, 2 + sub, 0:2 * P].rearrange("p (a t) -> p a t", a=2)).then_inc(actt_ready, 1)

            dve.wait_ge(x2_stored, 16 * TT)
            dve.wait_ge(x2_ready, TT)
            dve.sem_inc(gu_evac, 2)
            dve.sem_inc(yr_ready, 1)
            select_bias(0, 0)
            for b in range(2):
                seq.tick(V.tensor_copy(place[:, b], iota_n[:, None, HB * b:HB * b + HB].to_broadcast([P, 2, HB])))
            seq.settle()
            hot(0)
            take_tokens(0, 1)
            take_rows(0)
            hot(1)
            seq.tick(V.tensor_scalar(over, count_f, float(BLK), None, ALU.is_gt))
            seq.settle()
            for j in (2, 3):
                seq.tick(V.scalar_tensor_tensor(over, count_f, float(BLK * j), over, ALU.is_gt, ALU.add))
                seq.settle()
            seq.tick(V.tensor_tensor_scan(over_sum, over, zero32, 0.0, ALU.add, ALU.add))
            seq.settle()
            seq.tick(V.tensor_tensor(ov_cmp, over_sum[:, None, :].to_broadcast([P, MAX_EXTRA, NE]),
                                     iota_n[:, 0:MAX_EXTRA, None].to_broadcast([P, MAX_EXTRA, NE]), ALU.is_le))
            seq.settle()
            seq.tick(V.reduce_sum(ov_e, ov_cmp, AX))
            seq.settle()
            seq.tick(V.tensor_tensor(ov_cmp, ov_cmp, over[:, None, :].to_broadcast([P, MAX_EXTRA, NE]), ALU.mult))
            seq.settle()
            seq.tick(V.reduce_sum(ov_b, ov_cmp, AX))
            seq.settle()
            seq.tick(V.tensor_tensor(extra_base, iota_n[:, 0:MAX_EXTRA], ov_b, ALU.subtract))
            seq.tick(V.tensor_scalar(ov_e, ov_e, float(NE - 1), None, ALU.min))
            seq.settle()
            seq.tick(V.tensor_scalar(extra_base, extra_base, 1.0, float(BLK), ALU.add, ALU.mult))
            seq.tick(V.tensor_copy(extra_e, ov_e[0:1, :]))
            seq.settle()
            V.tensor_copy(counts_i[0:1, NE:NE + 1], over_sum[0:1, NE - 1:NE]).then_inc(extra_ready, 1)
            take_x(0, 1)
            dve.wait_ge(extra_ready, 1)

            n0 = seq.n
            per = 0
            with dve.Fori(0, NE // 2) as it:
                seq.off = it * LOOP_DVE
                for s in range(2):
                    e = it * 2 + s
                    q = dve.value_load(counts_i[0:1, bass.ds(e + Q_AT, 1)], min_val=0, max_val=2 * NE)
                    d = dve.value_load(counts_i[0:1, bass.ds(e + D_AT, 1)], min_val=0, max_val=NE)
                    count = dve.value_load(counts_i[0:1, bass.ds(e, 1)], min_val=0, max_val=S)
                    dve.wait_ge(pool_touched, q + e + 1)
                    take_tokens(1 - s, it * 2 + (s + 2))
                    clamp(0, q)
                    select_bias(1 - s, it * 2 + (s + 1))
                    glu(0, q)
                    clamp(1, q)
                    take_act(0, 0, q)
                    glu(1, q)
                    take_act(0, 1, q)
                    with dve.If(count > HB):
                        clamp(0, q + 1)
                        glu(0, q + 1)
                        clamp(1, q + 1)
                        take_act(1, 0, q + 1)
                        glu(1, q + 1)
                    dve.wait_ge(scattered[0], e * 16 + 16)
                    dve.wait_ge(scattered[1], d * 16 + 16)
                    take_rows(1 - s)
                    take_x(1 - s, it * 2 + (s + 2))
                    with dve.If(count > HB):
                        take_act(1, 1, q + 1)
                    hot(it * 2 + (s + 2))
                per = seq.n - n0
            assert per == LOOP_DVE, per
            seq.n, seq.off = n0 + LOOP_DVE * (NE // 2), None
            q_all = dve.value_load(counts_i[0:1, Q_AT + NE:Q_AT + NE + 1], min_val=0, max_val=2 * NE)
            d_all = dve.value_load(counts_i[0:1, D_AT + NE:D_AT + NE + 1], min_val=0, max_val=NE)
            n_extra = dve.value_load(counts_i[0:1, NE:NE + 1], min_val=0, max_val=MAX_EXTRA)
            n1 = seq.n
            with dve.Fori(0, MAX_EXTRA) as i:
                with dve.If(n_extra > i):
                    seq.off = i * EXTRA_DVE
                    e = dve.value_load(extra_e[0:1, bass.ds(i, 1)], min_val=0, max_val=NE - 1)
                    dve.wait_ge(pool_touched, q_all + i * 3 + (NE + 1))
                    dve.wait_ge(scattered[0], (i + (NE + 1)) * 16)
                    dve.wait_ge(scattered[1], (d_all + i + 1) * 16)
                    seq.tick(V.tensor_scalar(spot_now, spot[:, :, bass.ds(e, 1)].rearrange("p i a -> p (i a)"),
                                             extra_base[:, bass.ds(i, 1)], None, ALU.subtract))
                    seq.settle()
                    V.tensor_tensor(one_hot, places[:, None, :].to_broadcast([P, TT, 2 * BLK]),
                                    spot_now[:, :, None].to_broadcast([P, TT, 2 * BLK]),
                                    ALU.is_equal).then_inc(hot_ready, 1)
                    take_tokens(0, i + (NE + 2))
                    take_rows(0)
                    select_bias(0, e)
                    take_x(0, i + (NE + 2))
                    for b in range(2):
                        q = q_all + (i * 2 + b)
                        clamp(0, q)
                        glu(0, q)
                        clamp(1, q)
                        take_act(b, 0, q)
                        glu(1, q)
                        take_act(b, 1, q)
                    per = seq.n - n1
            assert per == EXTRA_DVE, per
            seq.off = n_extra * EXTRA_DVE
            seq.n = n1

            def finish_tile(i):
                dve.wait_ge(rstd3_done, i + 1)
                V.scalar_tensor_tensor(x2_sb[:, i, :], x2_sb[:, i, :], rstd_x[:, i:i + 1], fnw_sb,
                                       ALU.mult, ALU.mult).then_inc(out_ready, 1)
            for i in range(TT):
                dve.wait_ge(ys_loaded[i], 48)
                seq.tick(V.tensor_tensor(ys_sb[:, i, 0:2, :], ys_sb[:, i, 0:2, :], ys_sb[:, i, 2:4, :], ALU.add))
                seq.settle()
                seq.tick(V.tensor_tensor(ys_sb[:, i, 0, :], ys_sb[:, i, 0, :], ys_sb[:, i, 1, :], ALU.add))
                seq.settle()
                V.tensor_tensor(x2_sb[:, i, :], x2_sb[:, i, :], ys_sb[:, i, 0, :], ALU.add).then_inc(moe_sum, 1)
                if i == 1:
                    dve.wait_ge(fnw_loaded, 16)
                if i:
                    finish_tile(i - 1)
            finish_tile(TT - 1)

        @block.tensor
        def _(pe):
            MM = nc.tensor.matmul
            TR = nc.tensor.transpose
            pe.wait_ge(consts, 10)
            pe.wait_ge(rows_ready, 2)
            TR(ps[:, 3, 0:36], rows, ident[0:36, 0:36]).then_inc(turned, 1)
            for i in range(TT):
                pe.wait_ge(xn_ready, i + 1)
                if i:
                    pe.wait_ge(ht_ready, 2 * i)
                for j in range(KT):
                    mm = TR(bank4(4 + j // 4)[:, j % 4, :], xn1_sb[:, i % 2, P * j:P * j + P], ident[:, :])
                mm.then_inc(xn_turned, 1)
            pe.wait_ge(lam_sum, 2)
            pe.wait_ge(vec_ready, 1)
            MM(ps[:, 7, 0:1], ones_f, lam_s[:, 5:6], start=True, stop=True).then_inc(lam_bc, 1)

            def turn_qk(n):
                s, i = divmod(n, TT)
                pe.wait_ge(roped, n + 1)
                if n < 2:
                    pe.wait_ge(ht_ready, 2 * TT)
                else:
                    pe.wait_ge(qkt_ready, n - 1)
                for h in range(HEADS):
                    mm = TR(bank4(4 + n % 2)[:, h, :], qk_tok[:, s, i, P * h:P * h + P], ident[:, :])
                mm.then_inc(qk_turned, 1)

            for n in range(8):
                s, i = divmod(n, TT)
                pe.wait_ge(s_win[s], 16)
                pe.wait_ge(ht_ready, 2 * i + 2)
                if n >= 4:
                    pe.wait_ge(roped, n - 3)
                for j in range(KT):
                    mm = MM(ps[:, n % 4, :], h_t[:, j, P * i:P * i + P], w_in_sb[:, j, 512 * s:512 * s + 512],
                            start=(j == 0), stop=(j == KT - 1))
                mm.then_inc(proj, 1)
                if n >= 2:
                    turn_qk(n - 2)
            pe.wait_ge(s_win[2], 16)
            for i in range(TT):
                pe.wait_ge(roped, 5 + i)
                for j in range(KT):
                    mm = MM(ps[:, i, :], h_t[:, j, P * i:P * i + P], w_in_sb[:, j, 1024:1536],
                            start=(j == 0), stop=(j == KT - 1))
                mm.then_inc(v_proj, 1)
                if i < 2:
                    turn_qk(6 + i)

            def scores(n):
                i, h = divmod(n, HEADS)
                b = n % 2
                if n == 0:
                    pe.wait_ge(qkt_ready, 8)
                if n < 2:
                    pe.wait_ge(v_ready, 2 * n + 2)
                else:
                    pe.wait_ge(exped, 2 * n - 2)
                for m in range(2):
                    r = slice(QKD * m, QKD * m + QKD)
                    o = ps[:, 2 * b + m, :]
                    MM(o[:, P * i:P * i + P], ident_h[:, :], causal[:, :], start=True, stop=False,
                       skip_group_check=True)
                    mm = MM(o[:, 0:P * (i + 1)], qk_t[r, 0, h, P * i:P * i + P], qk_t[r, 1, h, 0:P * (i + 1)],
                            start=False, stop=True, skip_group_check=True)
                mm.then_inc(scored, 1)

            def turn_mix(n):
                i = n // HEADS
                pe.wait_ge(mixed, n + 1)
                if n < 2:
                    pe.wait_ge(qkt_ready, 8)
                else:
                    pe.wait_ge(mixt_ready, n - 1)
                if n >= 9 and (n - 9) % 4 == 0:
                    pe.wait_ge(cat_attn, (n - 9) // 4 + 1)
                for kb in range(i + 1):
                    mm = TR(bank4(4 + n % 2)[:, kb, :], mix[:, n % 2, P * kb:P * kb + P], ident[:, :])
                mm.then_inc(mix_turned, 1)

            def pv(n):
                i, h = divmod(n, HEADS)
                pe.wait_ge(mixt_ready, n + 1)
                if n == 0:
                    pe.wait_ge(v_ready, TT)
                else:
                    pe.wait_ge(o_copied, n)
                for kb in range(i + 1):
                    mm = MM(ps[:, 6, P * h:P * h + P], mix_t[:, n % 2, P * kb:P * kb + P],
                            v_sb[:, kb, P * h:P * h + P], start=(kb == 0), stop=(kb == i))
                mm.then_inc(pv_done, 1)

            def turn_o(i, n_mix):
                pe.wait_ge(o_normed, i + 1)
                pe.wait_ge(mixt_ready, n_mix)
                for h in range(HEADS):
                    mm = TR(bank4(O_BANK[i])[:, h, :], o_sb[:, i % 2, h, :], ident[:, :])
                mm.then_inc(o_turned, 1)

            pe.wait_ge(s_win[3], 16)
            for n in range(16):
                scores(n)
                c, r = divmod(n, 4)
                if r == 0 and c:
                    pe.wait_ge(u_ready, c)
                uc = 1536 + P * POOL_ORDER[c]
                for j in (2 * r, 2 * r + 1):
                    mm = MM(ps[:, 7, :], w_in_sb[:, j, uc:uc + P], h_t[:, j, :],
                            start=(j == 0), stop=(j == KT - 1))
                if r == 3:
                    mm.then_inc(u_proj, 1)
                if n >= 2:
                    turn_mix(n - 2)
                if n >= 3:
                    pv(n - 3)
                if n >= 9 and (n - 9) % 4 == 0:
                    turn_o((n - 9) // 4, n - 1)
            turn_mix(14)
            pv(13)
            turn_mix(15)
            pv(14)
            pv(15)
            pe.wait_ge(s_poolw, 16)
            pe.wait_ge(exped, 32)
            for n, g in enumerate(POOL_ORDER):
                pe.wait_ge(pooled, n + 1)
                MM(ps[:, g, :], pool_w_sb[:, g, :], pool_d[:, g, :], start=True, stop=True).then_inc(pool_mm, 1)
            for i in (2, 3):
                turn_o(i, 16)

            def router(i):
                pe.wait_ge(xn2_ready, i + 1)
                if i:
                    pe.wait_ge(h2_ready, i)
                for j in range(KT):
                    mm = TR(bank4(4 + j // 4)[:, j % 4, :], xn_sb[:, P * j:P * j + P], ident[:, :])
                mm.then_inc(xn2_turned, 1)
                pe.wait_ge(h2_ready, i + 1)
                if i == 0:
                    pe.wait_ge(o_copied, 16)
                    pe.wait_ge(s_router, 32)
                for j in range(KT):
                    mm = MM(ps[:, 6, NE * i:NE * i + NE], x2h(i)[:, j, :], router_sb[:, j, :],
                            start=(j == 0), stop=(j == KT - 1))
                mm.then_inc(routed, 1)

            pe.wait_ge(s_wout, 16)
            pe.wait_ge(cat_pool, 4)
            for i in range(TT):
                pe.wait_ge(cat_attn, i + 1)
                if i >= 2:
                    pe.wait_ge(x2_ready, i - 1)
                for half in range(2):
                    for n, j in enumerate((4, 5, 6, 7, 0, 1, 2, 3)):
                        mm = MM(ps[:, 2 * (i % 2) + half, :], cat_t[:, j, P * i:P * i + P],
                                w_out_sb[:, j, 512 * half:512 * half + 512], start=(n == 0), stop=(n == KT - 1))
                mm.then_inc(out_proj, 1)
                if i:
                    router(i - 1)
            router(TT - 1)
            pe.wait_ge(x2_ready, TT)
            pe.sem_inc(y_done, 1)
            pe.wait_ge(mask_ready, 1)
            pe.wait_ge(h2_ready, TT)
            for i in range(TT):
                for k in range(i + 1):
                    MM(ps[:, 4, NE * i:NE * i + NE], before[:, :] if k == i else ones_h[:, :], mask_h[:, k, :],
                       start=(k == 0), stop=(k == i))
            for k in range(TT):
                mm = MM(ps[:, 5, 0:NE], ones_h[:, :], mask_h[:, k, :], start=(k == 0), stop=(k == TT - 1))
            mm.then_inc(spot_sum, 1)

            def sum_indices(e, n_hot):
                pe.wait_ge(hot_ready, n_hot)
                for at, n_col, first in ((0, 2, HB), (2, 6, 0), (8, 6, BLK)):
                    for i in range(TT):
                        r = table[:, i, e, 0:n_col] if isinstance(e, int) else \
                            table[:, i, bass.ds(e, 1), 0:n_col].rearrange("p a c -> p (a c)")
                        mm = MM(ps[:, 5, at:at + n_col], one_hot[:, i, first:first + BLK], r,
                                start=(i == 0), stop=(i == TT - 1))
                mm.then_inc(idx_sum, 1)

            def turn_x(n):
                pe.wait_ge(gathered, n * 16)
                for j in range(KT):
                    mm = TR(bank4(6 + j // 4)[:, j % 4, :], xg[:, P * j:P * j + P], ident[:, :])
                mm.then_inc(x_turned, 1)

            def gate_up(slot, s, b, sub, q, n_loaded=None):
                pe.wait_ge(gu_evac, q * 2 + (sub + 1))
                for at, base in ((0, 0), (SUB, F)):
                    for j in range(-1, KT):
                        if n_loaded is not None and j >= 0 and at == 0:
                            pe.wait_ge(gu_loaded[slot][j], n_loaded)
                        for half in range(2):
                            c = base + F // 2 * half + SUB * sub
                            o = ps[HB * half:HB * half + HB, sub, at:at + SUB]
                            if j < 0:
                                MM(o, bias_sel[:, s, :], bias_parts[:, c:c + SUB], start=True, stop=False)
                            else:
                                mm = MM(o, xe_t[:, s, j, HB * b:HB * b + HB], gu_slot[slot][:, j, c:c + SUB],
                                        start=False, stop=(j == KT - 1))
                mm.then_inc(gu_done, 1)

            def turn_act(sub, q):
                pe.wait_ge(act_ready, q * 2 + (sub + 1))
                for a in range(2):
                    mm = TR(ps[:, 2 + sub, P * a:P * a + P], act_sb[:, sub, P * a:P * a + P], ident[:, :])
                mm.then_inc(act_turned, 1)

            def down(s, b, sub, q, n_loaded=None):
                pe.wait_ge(actt_ready, q * 2 + (sub + 1))
                if sub == 0:
                    pe.wait_ge(yr_ready, q + 1)
                    for half in range(2):
                        c = 2 * F + D // 2 * half
                        MM(ps[HB * half:HB * half + HB, 4, :], bias_sel[:, s, :], bias_parts[:, c:c + D // 2],
                           start=True, stop=False)
                for c in (2 * sub, 2 * sub + 1):
                    for upper in range(2):
                        if n_loaded is not None and c % 2 == 0:
                            pe.wait_ge(dn_loaded[2 * upper + sub], n_loaded)
                        for half in range(2):
                            mm = MM(ps[HB * half:HB * half + HB, 4, :], act_t[b][:, c, HB * upper:HB * upper + HB],
                                    dn_slot[:, 4 * upper + c, D // 2 * half:D // 2 * half + D // 2],
                                    start=False, stop=(sub == 1 and c == 3 and upper == 1))
                if sub == 1:
                    mm.then_inc(y_done, 1)

            sum_indices(0, 1)
            turn_x(1)
            pe.wait_ge(extra_ready, 1)

            with pe.Fori(0, NE // 2) as it:
                for s in range(2):
                    slot, e = 1 - s, it * 2 + s
                    q = pe.value_load(counts_i[0:1, bass.ds(e + Q_AT, 1)], min_val=0, max_val=2 * NE)
                    count = pe.value_load(counts_i[0:1, bass.ds(e, 1)], min_val=0, max_val=S)
                    pe.wait_ge(xe_ready, e + 1)
                    sum_indices(it * 2 + (s + 1), it * 2 + (s + 2))
                    gate_up(slot, s, 0, 0, q, it * 16 + 16)
                    gate_up(slot, s, 0, 1, q)
                    turn_act(0, q)
                    with pe.If(count > HB):
                        gate_up(slot, s, 1, 0, q + 1)
                    turn_act(1, q)
                    with pe.If(count > HB):
                        gate_up(slot, s, 1, 1, q + 1)
                        pe.wait_ge(actt_ready, q * 2 + 1)
                        turn_act(0, q + 1)
                    turn_x(it * 2 + (s + 2))
                    with pe.If(count > HB):
                        pe.wait_ge(actt_ready, q * 2 + 2)
                        turn_act(1, q + 1)
                    down(s, 0, 0, q, it * 32 + (16 * s + 16))
                    down(s, 0, 1, q, it * 32 + (16 * s + 16))
                    with pe.If(count > HB):
                        down(s, 1, 0, q + 1)
                        down(s, 1, 1, q + 1)
            q_all = pe.value_load(counts_i[0:1, Q_AT + NE:Q_AT + NE + 1], min_val=0, max_val=2 * NE)
            n_extra = pe.value_load(counts_i[0:1, NE:NE + 1], min_val=0, max_val=MAX_EXTRA)
            with pe.Fori(0, MAX_EXTRA) as i:
                with pe.If(n_extra > i):
                    e = pe.value_load(extra_e[0:1, bass.ds(i, 1)], min_val=0, max_val=NE - 1)
                    sum_indices(e, i + (NE + 3))
                    turn_x(i + (NE + 2))
                    pe.wait_ge(xe_ready, i + (NE + 2))
                    pe.wait_ge(ex_loaded, i * (16 * (KT + 4)) + 16 * (KT + 4))
                    for b in range(2):
                        q = q_all + (i * 2 + b)
                        gate_up(0, 0, b, 0, q)
                        gate_up(0, 0, b, 1, q)
                        for sub in range(2):
                            if b:
                                pe.wait_ge(actt_ready, (q - 1) * 2 + (sub + 1))
                            turn_act(sub, q)
                    for b in range(2):
                        q = q_all + (i * 2 + b)
                        down(0, b, 0, q)
                        down(0, b, 1, q)


_INS = ["x", "positions", "attn_norm_w", "w_in", "lambda_q1", "lambda_k1", "lambda_q2", "lambda_k2",
        "subln_w", "pool_w", "pool_scale", "w_out", "ffn_norm_w", "router_w", "router_b",
        "w_gate_up", "b_gate_up", "w_down", "b_down", "final_norm_w"]


def kernel(**inputs):
    import numpy as _np
    import concourse.bacc as _bacc
    from concourse import mybir as _mybir
    from concourse.bass_utils import run_bass_kernel_spmd as _run

    nc = _bacc.Bacc("TRN2", target_bir_lowering=False, num_devices=1)
    arrays, args = {}, []
    for name in _INS:
        a = _np.ascontiguousarray(inputs[name])
        arrays[f"in_{name}"] = a
        args.append(nc.dram_tensor(f"in_{name}", a.shape, _mybir.dt.from_np(a.dtype), kind="ExternalInput").ap())
    args.append(nc.dram_tensor("out_dram", (1, S, D), _mybir.dt.float32, kind="ExternalOutput").ap())
    hybrid_block(nc, *args)
    r = _run(nc, [arrays], core_ids=[0])
    return r.results[0]["out_dram"]
```

```python
import concourse.bass as bass
from concourse import mybir
from contextlib import ExitStack
import math

import numpy as np

F32 = mybir.dt.float32
BF16 = mybir.dt.bfloat16
I32 = mybir.dt.int32
U32 = mybir.dt.uint32
ALU = mybir.AluOpType
ACT = mybir.ActivationFunctionType
AX = mybir.AxisListType.X

P = 128
S = 512
D = 1024
TT = S // P
KT = D // P
HEADS = 4
QKD = 64
ROT = 16
WINDOWS = (2, 4, 8, 16)
O_BANK = (5, 5, 4, 5)
POOL_ORDER = (3, 2, 1, 0)
NE = 32
TOPK = 4
F = D
FT = F // P
BLK = 128
HB = 32
HALF = BLK // 2
NB = 4
SUB = F // NB
MAX_EXTRA = 15
LAM_INIT = 0.8 - 0.6 * math.exp(0.0)
SCALE = QKD ** -0.5
EPS = 1e-5
ALPHA = 1.702
LIMIT = 7.0
THETA = 500000.0
NEG = -1.0e30
OUT_OF_TOKENS = 1024
OUT_OF_ROWS = 4096
PI2_A = 6.28125
PI2_B = float((np.float32(2 * math.pi - PI2_A).view(np.int32) & np.int32(-4096)).view(np.float32))
PI2_C = float(np.float32(2 * math.pi - PI2_A - PI2_B))
ROUND = 12582912.0
PI_SAFE = 3.1415925

AHEAD = 3
DN_AFTER = 6
LOOP_DVE = 2 * 8
EXTRA_DVE = 9
Q_AT = NE + 2 + MAX_EXTRA
D_AT = Q_AT + NE + 1


class Count:

    def __init__(self, eng, sem):
        self.eng, self.sem, self.n, self.off = eng, sem, 0, None

    def tick(self, ins):
        ins.then_inc(self.sem, 1)
        self.n += 1
        return self

    def settle(self):
        if self.off is None:
            self.eng.wait_ge(self.sem, self.n)
        else:
            self.eng.wait_ge(self.sem, self.off + self.n)


def hybrid_block(nc, x, positions, attn_norm_w, w_in, lambda_q1, lambda_k1, lambda_q2, lambda_k2,
                 subln_w, pool_w, pool_scale, w_out, ffn_norm_w, router_w, router_b,
                 w_gate_up, b_gate_up, w_down, b_down, final_norm_w, out, dbg=None):
    ctx = ExitStack()
    with ctx:
        def sb(name, shape, dt=F32):
            return ctx.enter_context(nc.sbuf_tensor(name, shape, dt))

        def sem(name):
            return ctx.enter_context(nc.semaphore(name))

        gu_slot = [sb("gu_slot_a", [P, KT, 2 * F]), sb("gu_slot_b", [P, KT, 2 * F])]
        dn_slot = sb("dn_slot", [P, FT, D])
        shared = sb("shared", [P, 9216])
        ident = sb("ident", [P, P])
        ident_h = sb("ident_h", [P, P], BF16)
        causal = sb("causal", [P, P], BF16)
        before = sb("before", [P, P], BF16)
        ones_h = sb("ones_h", [P, P], BF16)
        iota_n = sb("iota_n", [P, BLK])
        bias_parts = sb("bias_parts", [3 * NE, 3 * F], BF16)
        sel3 = sb("sel3", [3 * NE, NE + 1], BF16)
        router_sb = sb("router_sb", [P, KT, NE])
        router_bias = sb("router_bias", [P, NE])
        logits = sb("logits", [P, TT, NE])
        vec_t = sb("vec_t", [P, 36])
        small = sb("small", [P, 200])
        counts_i = sb("counts_i", [1, D_AT + (NB - 1) * (NE + 1)], I32)

        slot_a = gu_slot[0][:, :, :].rearrange("p a b -> p (a b)")
        slot_b = gu_slot[1][:, :, :].rearrange("p a b -> p (a b)")

        def part(flat, at, *dims):
            n = int(np.prod(dims))
            v = flat[:, at:at + n]
            if len(dims) == 1:
                return v
            names = "abcd"[:len(dims)]
            return v.rearrange("p (%s) -> p %s" % (" ".join(names), " ".join(names)),
                               **dict(zip(names, dims)))

        h_t = part(slot_a, 0, KT, S)
        qk_tok = part(slot_a, 4096, 2, TT, 512)
        qk_t = part(slot_a, 8192, 2, HEADS, S)
        v_sb = part(slot_a, 12288, TT, 512)
        u_t = part(slot_a, 14336, TT, S)
        probs = part(slot_a, 4096, 2, 2, 512)
        mix = part(slot_a, 6144, 2, 512)
        mix_t = part(slot_a, 7168, 2, 512)
        xn1_sb = part(slot_a, 14336, 2, D)
        w_in_sb = gu_slot[1]
        w_out_sb = dn_slot


        sh = shared[:, :]
        x_sb = part(sh, 0, TT, D)
        cat_t = part(sh, 4096, KT, S)
        o_sb = part(sh, 8192, 2, HEADS, P)
        pool_tmp = gu_slot[1][:, KT - 1, S:2 * S]
        pool_w_sb = gu_slot[1][:, KT - 1, 2 * S:3 * S].rearrange("p (g c) -> p g c", g=4)
        pool_d = cat_t[:, 4:8, :]
        bias_rows = shared[0:3 * NE, 4096:4096 + 3 * F]
        xn_sb = part(sh, 8192, D)
        xg = part(sh, 0, D)
        xe_t = part(sh, 1024, 2, KT, BLK)
        spread = part(sh, 3072, 256).bitcast(BF16).rearrange("p (b r n) -> p b r n", b=NB, r=NB)
        bias_sel = part(sh, 3328, 32)[0:3 * NE, :].bitcast(BF16).rearrange("p (s n) -> p s n", s=2)
        y_rows = [part(sh, at, SUB) for at in (3392, 3648, 8016, 8272)]
        g_t = part(sh, 3904, 2, SUB)
        s_t = part(sh, 4416, 2, SUB)
        u1_t = part(sh, 4928, 2, SUB)
        act_sb = part(sh, 5440, 2, SUB)
        act_t = [part(sh, at, 2, P) for at in (5952, 6208, 8528, 8784)]
        table = part(sh, 6464, 396).bitcast(BF16).rearrange("p (i e c) -> p i e c", i=TT, c=6)
        spot = part(sh, 9040, TT, NE + 2)
        one_hot = part(sh, 7504, 256).bitcast(BF16).rearrange("p (i n) -> p i n", i=TT)
        eq4 = part(sh, 7504, TT, TOPK, NE)
        eq4b = part(sh, 8016, TT, TOPK, NE)

        top8 = part(sh, 6992, TT, 8)
        top_idx = part(sh, 7024, TT, 8).bitcast(U32)
        idx_f = part(sh, 7056, TT, 8)
        mask_f = part(sh, 7088, TT, NE)
        mask_h = part(sh, 7216, TT * NE // 2).bitcast(BF16).rearrange("p (i e) -> p i e", i=TT)
        neg_top = part(sh, 7280, TT)
        gate4 = part(sh, 7284, TT, TOPK)
        gate_sum = part(sh, 7300, TT)
        dst4 = part(sh, 7304, TT, TOPK)
        count_f = part(sh, 7324, NE)
        over = part(sh, 7356, NE)
        over_sum = part(sh, 7388, NE)
        zero32 = part(sh, 7420, NE)
        ov_e = part(sh, 7452, MAX_EXTRA)
        ov_b = part(sh, 7468, MAX_EXTRA)
        gate_f = part(sh, 8528, TT, NE)
        gate_r = part(sh, 8656, TT, NE)
        more = part(sh, 8784, NB - 1, NE)
        more_sum = part(sh, 8880, NB - 1, NE)
        q_f = part(sh, 8976, NE)
        q_total = part(sh, 9008, 1)
        ov_cmp = part(sh, 6992, MAX_EXTRA * NE // 2).bitcast(BF16).rearrange("p (i e) -> p i e", i=MAX_EXTRA)

        sm = small[:, :]
        ss_x = sm[:, 0:4]
        rstd_x = sm[:, 4:8]
        neg_lam = sm[:, 8:9]
        mx = part(sm, 9, 2, 2)
        nbias = part(sm, 13, 2, 2)
        esum = part(sm, 17, 2, 2)
        rsum = part(sm, 21, 2, 2)
        coef = part(sm, 25, 2, 1)
        ss_o = part(sm, 27, TT, HEADS)
        rstd_o = part(sm, 43, TT, HEADS)
        half_neg = sm[:, 59:75]
        gate_col = part(sm, 90, 2, NB, 1)
        idx_dst = part(sm, 98, 2, NB, 1).bitcast(U32)
        tmp_a = part(sm, 106, NB, 1)
        tmp_b = part(sm, 110, NB, 1)
        parts = part(sm, 114, 4).bitcast(BF16)[:, 0:6]
        quarter_off = sm[:, 83:84]
        zero_col = sm[:, 88:89]
        token_sum = sm[:, 89:90]
        idx_src = sm[:, 125:127].bitcast(U32)
        spot_now = sm[:, 156:160]
        row_id = sm[:, 161:162]
        edge = sm[:, 164:180]
        extra_e = counts_i[0:1, NE + 2:NE + 2 + MAX_EXTRA]
        ss_2 = sm[:, 130:134]
        rstd_2 = sm[:, 134:138]
        extra_base = sm[:, 138:138 + MAX_EXTRA]

        rows = part(sh, 7168, P)[0:36, :]
        rows_i = part(sh, 7296, P)[0:36, :].bitcast(I32)
        AN, FN, PS, SL, POS = 0, 8, 16, 20, 32
        lam_in = part(sh, 7424, 256)[0:1, :].rearrange("p (a b c) -> p a b c", a=2, b=2)
        lam_pr = part(sh, 7680, 128)[0:1, :].rearrange("p (a c) -> p a c", a=2)
        lam_s = part(sh, 7808, 8)[0:1, :]
        ones_f = part(sh, 7824, P)[0:1, :]
        ang = part(sh, 8192, TT, 8)
        ang2 = part(sh, 8224, TT, 8)
        ang3 = part(sh, 8256, TT, 8)
        ang4 = part(sh, 8288, TT, 8)
        cos2 = part(sh, 8320, TT, ROT)
        sin2 = part(sh, 8384, TT, ROT)
        rot_a = part(sh, 8448, 2, 8, ROT)
        rot_b = part(sh, 8704, 2, 8, ROT)
        sq_junk = part(slot_a, 12288, D)

        ps = ctx.enter_context(nc.psum_tensor("ps", [P, 8, 512], F32))

        def x2h(i):
            return x_sb[:, i, :].rearrange("p (j t) -> p j t", j=KT)

        def bank4(b):
            return ps[:, b, :].rearrange("p (a c) -> p a c", a=4)

        def turned_act(b):
            return ps[:, 2 + b % 2, SUB * (b // 2):SUB * (b // 2) + SUB].rearrange("p (a t) -> p a t", a=2)

        x2_dram = nc.dram_tensor("x2_dram", [S, D], F32).ap()
        xn_dram = nc.dram_tensor("xn_dram", [S, D], F32).ap()
        ys_dram = nc.dram_tensor("ys_dram", [TOPK * S, D], F32).ap()

        x_tiles = x[0].rearrange("(i p) d -> i p d", p=P)
        out_tiles = out[0].rearrange("(i p) d -> i p d", p=P)
        x2_tiles = x2_dram.rearrange("(i p) d -> i p d", p=P)
        xn_tiles = xn_dram.rearrange("(i p) d -> i p d", p=P)
        ys_quarters = ys_dram.rearrange("r (h d) -> (r h) d", h=NB)
        ys_tiles = ys_dram.rearrange("(k i p) d -> i p k d", i=TT, p=P)
        w_in_v = w_in[0].rearrange("(j p) c -> p j c", p=P)
        w_out_v = w_out[0].rearrange("(j p) c -> p j c", p=P)
        w_gu_v = w_gate_up[0].rearrange("e (j p) c -> e p j c", p=P)
        w_dn_v = w_down[0].rearrange("e (j p) c -> e p j c", p=P)

        s_x = [sem(f"x_loaded{i}") for i in range(TT)]
        s_win = [sem(f"w_in_loaded{i}") for i in range(4)]
        s_wout = sem("w_out_loaded")
        s_small = sem("small_loaded")
        s_lam_in = sem("lambda_loaded")
        s_bias = sem("bias_rows_loaded")
        s_router = sem("router_loaded")
        s_poolw = sem("pool_w_loaded")
        gu_loaded = [[sem(f"gu_{slot}_loaded{c}") for c in range(KT)] for slot in "ab"]
        dn_loaded = [sem(f"dn_loaded{c}") for c in range(4)]
        dve_seq = sem("dve_seq")
        act_seq = sem("act_seq")
        pool_seq = sem("pool_seq")
        consts = sem("consts_ready")
        rows_ready = sem("rows_ready")
        turned = sem("vectors_turned")
        vec_ready = sem("vectors_ready")
        lam_exp = sem("lambda_exp")
        lam_sum = sem("lambda_sum")
        lam_bc = sem("lambda_spread")
        ang_ready = sem("angles_ready")
        sincos = sem("sincos_ready")
        sumsq = sem("sumsq_x")
        rstd_done = sem("rstd_x_done")
        xn_ready = sem("xn_ready")
        xn_turned = sem("xn_turned")
        ht_ready = sem("h_t_ready")
        proj = sem("qk_projected")
        proj_copied = sem("qk_copied")
        roped = sem("qk_roped")
        qk_turned = sem("qk_turned")
        qkt_ready = sem("qk_t_ready")
        v_proj = sem("v_projected")
        v_ready = sem("v_ready")
        u_proj = sem("u_projected")
        u_ready = sem("u_t_ready")
        scored = sem("scored")
        maxed = sem("row_max_ready")
        exped = sem("exp_done")
        coefed = sem("coef_ready")
        scaled = sem("map1_scaled")
        mixed = sem("mixed")
        mix_turned = sem("mix_turned")
        mixt_ready = sem("mix_t_ready")
        pv_done = sem("pv_done")
        o_copied = sem("o_copied")
        o_rstd = sem("o_rstd_done")
        o_normed = sem("o_normed")
        o_turned = sem("o_turned")
        cat_attn = sem("cat_attn_ready")
        pooled = sem("pool_diff_ready")
        pool_mm = sem("pool_projected")
        cat_pool = sem("cat_pool_ready")
        out_proj = sem("out_projected")
        x2_ready = sem("x2_ready")
        sumsq2 = sem("sumsq_x2")
        rstd2_done = sem("rstd_x2_done")
        xn2_ready = sem("xn2_ready")
        x2_stored = sem("x2_stored")
        xn_stored = sem("xn_stored")
        xn2_turned = sem("xn2_turned")
        h2_ready = sem("h2_t_ready")
        routed = sem("router_projected")
        logit_ready = sem("logits_ready")
        top_ready = sem("top_ready")
        gate_exp = sem("gate_exp_done")
        mask_ready = sem("mask_ready")
        spot_sum = sem("spots_summed")
        tables = sem("tables_ready")
        extra_ready = sem("extra_tasks_ready")
        hot_ready = sem("one_hot_ready")
        idx_sum = sem("indices_summed")
        idx_ready = sem("indices_ready")
        gathered = sem("rows_gathered")
        x_turned = sem("expert_rows_turned")
        xe_ready = sem("expert_x_t_ready")
        gu_done = sem("gate_up_done")
        gu_part = [sem(f"gate_up_chunks_used{c}") for c in range(1, KT - 1, 2)]
        g_ready = sem("gate_clamped")
        gu_evac = sem("gate_up_evacuated")
        sig_ready = sem("sigmoid_ready")
        act_ready = sem("act_ready")
        y_done = sem("y_done")
        glu_ready = sem("glu_ready")
        gates_taken = sem("gates_taken")
        dst_taken = sem("destinations_taken")
        parts_ready = sem("parts_ready")
        parts_spread = sem("parts_spread")
        act_turned = sem("act_turned")
        actt_ready = sem("act_t_ready")
        bias_split = sem("bias_parts_ready")
        yr_ready = sem("y_rows_ready")
        scattered = [sem(f"y_rows_scattered_block{b}") for b in range(NB)]
        all_scattered = sem("all_scattered")
        pool_touched = sem("pool_touched")
        ex_loaded = sem("extra_weights_loaded")
        ys_loaded = [[sem(f"ys_loaded{i}_{h}") for h in range(2)] for i in range(TT)]
        x2_loaded = sem("x2_loaded")
        dn_last_loaded = [sem(f"dn_last_loaded{c}") for c in range(4)]
        fnw_loaded = sem("final_norm_w_loaded")
        moe_sum = sem("moe_summed")
        sumsq3 = sem("sumsq_final")
        rstd3_done = sem("rstd_final_done")
        out_ready = sem("out_tile_ready")
        out_stored = sem("out_stored")
        slot_free = sem("slot_free")
        ordinals_ready = sem("block_ordinals_ready")
        lam_taken = sem("lambda_taken")

        ys_sb = part(slot_a, 0, TT, TOPK, D)
        x2_sb = part(slot_b, 0, TT, D)
        fnw_sb = part(slot_b, 4096, D)
        sq3 = part(slot_b, 5120, D)
        dn_last = part(slot_b, 8192, KT, D)

        block = ctx.enter_context(nc.Block())

        @block.sync
        def _(sp):
            def load_w_in(s):
                sp.dma_start(w_in_sb[:, :, 512 * s:512 * s + 512],
                             w_in_v[:, :, 512 * s:512 * s + 512]).then_inc(s_win[s], 16)

            for i in range(TT):
                sp.dma_start(x_sb[:, i, :], x_tiles[i]).then_inc(s_x[i], 16)
                if i == 1:
                    sp.wait_ge(s_small, 16 * 5)
                    load_w_in(0)
            for s in range(1, 4):
                load_w_in(s)
            sp.dma_start(w_out_sb[:, :, :], w_out_v).then_inc(s_wout, 16)

            def gu_chunk(slot, e, c, signal=None):
                src = w_gu_v[e] if isinstance(e, int) else \
                    w_gu_v[bass.ds(e, 1)].rearrange("a p j c -> (a p) j c")
                sp.dma_start(gu_slot[slot][:, c, :], src[:, c, :]).then_inc(signal or gu_loaded[slot][c], 16)

            def dn_chunk(e, c, signal=None):
                src = w_dn_v[e] if isinstance(e, int) else \
                    w_dn_v[bass.ds(e, 1)].rearrange("a p j c -> (a p) j c")
                sp.dma_start(dn_slot[:, 2 * c:2 * c + 2, :],
                             src[:, 2 * c:2 * c + 2, :]).then_inc(signal or dn_loaded[c], 16)

            load_order = [("gu", c) for c in range(DN_AFTER)] + [("dn", c) for c in range(4)] + \
                [("gu", c) for c in range(DN_AFTER, KT)]

            def load_round(it, s):
                slot, e = 1 - s, it * 2 + s
                q = blocks_before(it * 2 + (s + 1))
                n_gu, n_other, n_dn = it * 16 + 16, it * 16 + (16 + 16 * s), it * 32 + (16 * s + 16)
                for at, (kind, c) in enumerate(load_order):
                    if kind == "gu" and c % 2 == 0:
                        sp.wait_ge(gu_part[c // 2] if c < KT - 2 else gu_done, q)
                        sp.sem_inc(slot_free, 1)
                    if kind == "dn" and c == 0:
                        sp.wait_ge(y_done, q + 1)
                        sp.sem_inc(slot_free, 1)
                    kind_b, c_b = load_order[at - AHEAD]
                    if kind_b == "dn":
                        sp.wait_ge(dn_loaded[c_b], n_dn if at < AHEAD else n_dn + 16)
                    elif at < AHEAD:
                        sp.wait_ge(gu_loaded[s][c_b], n_other)
                    else:
                        sp.wait_ge(gu_loaded[slot][c_b], n_gu + 16)
                    if kind == "gu":
                        gu_chunk(slot, it * 2 + (s + 2), c)
                    else:
                        dn_chunk(it * 2 + (s + 1), c)

            sp.wait_ge(u_proj, 4)
            for c in range(KT - 1):
                if c >= AHEAD:
                    sp.wait_ge(gu_loaded[1][c - AHEAD], 16)
                gu_chunk(1, 0, c)
            sp.wait_ge(pool_mm, 4)
            gu_chunk(1, 0, KT - 1)
            sp.wait_ge(pv_done, 16)
            sp.wait_ge(o_copied, 16)
            for c in range(KT):
                if c >= AHEAD:
                    sp.wait_ge(gu_loaded[0][c - AHEAD], 16)
                gu_chunk(0, 1, c)
            sp.wait_ge(y_done, 1)
            for c in range(4):
                dn_chunk(0, c)
            sp.wait_ge(ordinals_ready, 1)

            def blocks_before(e):
                at = Q_AT + e if isinstance(e, int) else e + Q_AT
                return sp.value_load(counts_i[0:1, at:at + 1] if isinstance(e, int) else
                                     counts_i[0:1, bass.ds(at, 1)], min_val=1, max_val=NB * NE)

            with sp.Fori(0, NE // 2 - 1) as it:
                for s in range(2):
                    load_round(it, s)
            q = blocks_before(NE - 1)
            sp.wait_ge(gu_done, q)
            sp.sem_inc(slot_free, 1)
            for c in range(4):
                sp.dma_start(dn_last[:, 2 * c:2 * c + 2, :],
                             w_dn_v[NE - 1][:, 2 * c:2 * c + 2, :]).then_inc(dn_last_loaded[c], 16)
            for i in range(TT):
                sp.dma_start(x2_sb[:, i, :], x2_tiles[i]).then_inc(x2_loaded, 16)
            sp.dma_start(fnw_sb, final_norm_w.rearrange("(a n) -> a n", a=1).to_broadcast([P, D])).then_inc(fnw_loaded, 16)
            q_all = blocks_before(NE)
            sp.wait_ge(extra_ready, 1)
            n_extra = sp.value_load(counts_i[0:1, NE:NE + 1], min_val=0, max_val=MAX_EXTRA)
            with sp.If(n_extra > 0):
                with sp.Fori(0, MAX_EXTRA) as i:
                    with sp.If(n_extra > i):
                        e = sp.value_load(extra_e[0:1, bass.ds(i, 1)], min_val=0, max_val=NE - 1)
                        sp.wait_ge(y_done, q_all + i * NB + 1)
                        for c in range(KT):
                            gu_chunk(0, e, c, ex_loaded)
                        for c in range(4):
                            dn_chunk(e, c, ex_loaded)
            sp.wait_ge(all_scattered, 1)
            for i in range(TT):
                for h in range(2):
                    sp.dma_start(ys_sb[:, i, 2 * h:2 * h + 2, :],
                                 ys_tiles[i][:, 2 * h:2 * h + 2, :]).then_inc(ys_loaded[i][h], 16)
            for i in range(TT):
                sp.wait_ge(out_ready, i + 1)
                sp.dma_start(out_tiles[i], x2_sb[:, i, :]).then_inc(out_stored, 16)
            sp.wait_ge(out_stored, 16 * TT)

        @block.gpsimd
        def _(pool):
            seq = Count(pool, pool_seq)
            seq.tick(nc.gpsimd.memset(ident[:, :], 0.0))
            seq.tick(nc.gpsimd.memset(ident_h[:, :], 0.0))
            seq.tick(nc.gpsimd.memset(causal[:, :], 0.0))
            seq.tick(nc.gpsimd.memset(before[:, :], 1.0))
            seq.tick(nc.gpsimd.memset(sel3[:, :], 0.0))
            nc.gpsimd.memset(ones_h[:, :], 1.0).then_inc(consts, 1)
            nc.gpsimd.memset(half_neg, -0.5).then_inc(consts, 1)
            nc.gpsimd.memset(ones_f, 1.0).then_inc(consts, 1)
            seq.settle()
            for t in (ident, ident_h):
                nc.gpsimd.affine_select(out=t[:, :], in_=t[:, :], compare_op=ALU.not_equal, fill=1.0,
                                        base=0, pattern=[[-1, P]], channel_multiplier=1).then_inc(consts, 1)
            nc.gpsimd.affine_select(out=causal[:, :], in_=causal[:, :], compare_op=ALU.is_ge, fill=NEG,
                                    base=0, pattern=[[-1, P]], channel_multiplier=1).then_inc(consts, 1)
            nc.gpsimd.affine_select(out=before[:, :], in_=before[:, :], compare_op=ALU.is_ge, fill=0.0,
                                    base=-1, pattern=[[1, P]], channel_multiplier=-1).then_inc(consts, 1)
            for part3 in range(3):
                sel = nc.gpsimd.affine_select(out=sel3[:, 0:NE], in_=sel3[:, 0:NE], compare_op=ALU.not_equal,
                                              fill=1.0, base=-NE * part3, pattern=[[-1, NE]], channel_multiplier=1)
                if part3 < 2:
                    seq.tick(sel)
                    seq.settle()
                else:
                    sel.then_inc(consts, 1)
            nc.gpsimd.iota(row_id, pattern=[[0, 1]], base=0, channel_multiplier=1,
                           allow_small_or_imprecise_dtypes=True).then_inc(consts, 1)
            nc.gpsimd.iota(iota_n[:, :], pattern=[[1, BLK]], base=0, channel_multiplier=0,
                           allow_small_or_imprecise_dtypes=True).then_inc(consts, 1)

            def rstd(sums, result, exponent, width, signal):
                seq.tick(nc.gpsimd.tensor_scalar(result, sums, 1.0 / width, EPS, ALU.mult, ALU.add))
                seq.settle()
                nc.gpsimd.tensor_tensor(result, result, exponent, ALU.pow).then_inc(signal, 1)

            pool.wait_ge(consts, 10)
            for i in range(TT):
                pool.wait_ge(sumsq, i + 1)
                rstd(ss_x[:, i:i + 1], rstd_x[:, i:i + 1], half_neg[:, 0:1], D, rstd_done)

            pool.wait_ge(s_bias, 96)
            copy, sub = nc.gpsimd.tensor_copy, ALU.subtract
            seq.tick(copy(bias_parts[:, :], bias_rows))
            seq.settle()
            for first in (NE, 2 * NE):
                for again in range(first // NE):
                    r3 = slice(first, first + NE)
                    seq.tick(nc.gpsimd.tensor_tensor(bias_rows[r3, :], bias_rows[r3, :], bias_parts[r3, :], sub))
                    seq.settle()
                    seq.tick(copy(bias_parts[r3, :], bias_rows[r3, :]))
                    seq.settle()
            nc.gpsimd.tensor_scalar(zero_col, half_neg[:, 0:1], 0.0, 0.0, ALU.mult, ALU.add).then_inc(bias_split, 1)

            def o_rstds(i):
                pool.wait_ge(o_copied, 4 * i + 4)
                rstd(ss_o[:, i, :], rstd_o[:, i, :], half_neg[:, 0:4], P, o_rstd)

            pool.wait_ge(turned, 1)
            pool.wait_ge(lam_bc, 1)
            pool.wait_ge(v_proj, 4)
            pool.dma_start(pool_w_sb, pool_w[0].rearrange("g c d -> c g d")).then_inc(s_poolw, 16)
            pool.wait_ge(rows_ready, 3)
            for n, g in enumerate(POOL_ORDER):
                w = WINDOWS[g]
                pool.wait_ge(u_ready, n + 1)
                bufs = [pool_tmp, pool_d[:, g, :]]
                src, step = u_t[:, g, :], 1
                while step < w:
                    dst = bufs[0]
                    seq.tick(nc.gpsimd.tensor_copy(dst[:, 0:step], src[:, 0:step]))
                    seq.tick(nc.gpsimd.tensor_tensor(dst[:, step:S], src[:, step:S], src[:, 0:S - step], ALU.add))
                    seq.settle()
                    src, step, bufs = dst, 2 * step, bufs[::-1]
                seq.tick(nc.gpsimd.tensor_tensor(src[:, 0:w], src[:, 0:w], edge[:, 0:w], ALU.mult))
                seq.tick(nc.gpsimd.tensor_scalar(src[:, w:S], src[:, w:S], 1.0 / w, 0.0, ALU.mult, ALU.add))
                seq.settle()
                nc.gpsimd.tensor_tensor(pool_d[:, g, :], src, u_t[:, g, :], ALU.subtract).then_inc(pooled, 1)
                pool.wait_ge(pooled, n + 1)
                o_rstds(n)

            for i in range(TT):
                pool.wait_ge(sumsq2, i + 1)
                rstd(ss_2[:, i:i + 1], rstd_2[:, i:i + 1], half_neg[:, 0:1], D, rstd2_done)

            pool.wait_ge(x2_stored, 16 * TT)
            pool.wait_ge(xn2_ready, TT)
            nc.gpsimd.memset(xg, 0.0).then_inc(tables, 1)
            pool.wait_ge(tables, 1)

            def touch(at, signal=pool_touched):
                return nc.gpsimd.tensor_tensor(sm[:, 185 + at:186 + at], half_neg[:, 0:1], half_neg[:, 0:1],
                                               ALU.add).then_inc(signal, 1)

            def gather(b, n_idx, count=None):
                pool.wait_ge(idx_ready, n_idx)
                touch(NB)
                def rows_of(n_rows):
                    pool.indirect_dma_start(
                        out=xg[0:n_rows, :], out_offset=None, in_=xn_dram,
                        in_offset=bass.IndirectOffsetOnAxis(ap=idx_src[0:n_rows, b:b + 1], axis=0),
                        bounds_check=S - 1, oob_is_err=False).then_inc(gathered, 16)
                if count is None:
                    rows_of(BLK)
                else:
                    with pool.If(count > HALF):
                        rows_of(BLK)
                    with pool.If(count <= HALF):
                        rows_of(HALF)

            def scatter(s, b, n_rows):
                pool.wait_ge(yr_ready, n_rows)
                touch(b)
                pool.indirect_dma_start(
                    out=ys_quarters, out_offset=bass.IndirectOffsetOnAxis(ap=idx_dst[:, s, b, :], axis=0),
                    in_=y_rows[b], in_offset=None,
                    bounds_check=NB * TOPK * S - 1, oob_is_err=False).then_inc(scattered[b], 16)

            pool.wait_ge(xn_stored, 16 * TT)
            pool.wait_ge(idx_ready, 1)
            first_count = pool.value_load(counts_i[0:1, 0:1], min_val=0, max_val=S)
            gather(0, 1, first_count)
            pool.wait_ge(ordinals_ready, 1)
            for b in range(NB):
                pool.dma_start(y_rows[b][:, 0:1], half_neg[:, 0:1]).then_inc(scattered[b], 16)
            with pool.Fori(0, NE // 2) as it:
                for s in range(2):
                    e = it * 2 + s
                    q = pool.value_load(counts_i[0:1, bass.ds(e + Q_AT, 1)], min_val=0, max_val=NB * NE)
                    count = pool.value_load(counts_i[0:1, bass.ds(e, 1)], min_val=0, max_val=S)
                    next_count = pool.value_load(counts_i[0:1, bass.ds(e + 1, 1)], min_val=0, max_val=S)
                    gather(1 - s, it * 2 + (s + 2), next_count)
                    scatter(s, 0, q + 2)
                    for b in range(1, NB):
                        with pool.If(count > HB * b):
                            scatter(s, b, q + (b + 2))
            q_all = pool.value_load(counts_i[0:1, Q_AT + NE:Q_AT + NE + 1], min_val=0, max_val=NB * NE)
            pool.wait_ge(extra_ready, 1)
            n_extra = pool.value_load(counts_i[0:1, NE:NE + 1], min_val=0, max_val=MAX_EXTRA)
            d_all = [pool.value_load(counts_i[0:1, at:at + 1], min_val=0, max_val=NE)
                     for at in range(D_AT + NE, D_AT + NE + (NB - 1) * (NE + 1), NE + 1)]
            with pool.If(n_extra > 0):
                with pool.Fori(0, MAX_EXTRA) as i:
                    with pool.If(n_extra > i):
                        gather(0, i + (NE + 2))
                        for b in range(NB):
                            scatter(0, b, q_all + i * NB + (b + 2))
            pool.wait_ge(scattered[0], (n_extra + (NE + 1)) * 16)
            for b in range(1, NB):
                pool.wait_ge(scattered[b], (d_all[b - 1] + n_extra + 1) * 16)
            touch(NB + 1, all_scattered)

            for i in range(TT):
                pool.wait_ge(sumsq3, i + 1)
                rstd(ss_x[:, i:i + 1], rstd_x[:, i:i + 1], half_neg[:, 0:1], D, rstd3_done)

        @block.scalar
        def _(act):
            seq = Count(act, act_seq)
            for at, w, n in ((AN, attn_norm_w, 8), (FN, ffn_norm_w, 8), (PS, pool_scale, 4), (SL, subln_w, 1)):
                act.wait_ge(rows_ready, 1)
                act.dma_start(rows[at:at + n, :], w[0].rearrange("(a b) -> a b", b=P)).then_inc(s_small, 16)
            act.dma_start(rows_i[POS:POS + 4, :], positions[0].rearrange("(a b) -> a b", b=P)).then_inc(s_small, 16)
            for a, (q, k) in enumerate(((lambda_q1, lambda_k1), (lambda_q2, lambda_k2))):
                act.dma_start(lam_in[:, a, 0, :], q).then_inc(s_lam_in, 16)
                act.dma_start(lam_in[:, a, 1, :], k).then_inc(s_lam_in, 16)
            for i in range(TT):
                act.wait_ge(s_x[i], 16)
                if i:
                    act.wait_ge(sumsq, i)
                nc.scalar.activation(sq_junk, x_sb[:, i, :], ACT.Square, accum_out=ss_x[:, i:i + 1]).then_inc(sumsq, 1)
            for r in range(3):
                act.dma_start(bias_rows[NE * r:NE * r + NE, 0:2 * F], b_gate_up[0]).then_inc(s_bias, 16)
                act.dma_start(bias_rows[NE * r:NE * r + NE, 2 * F:3 * F], b_down[0]).then_inc(s_bias, 16)
            act.dma_start(router_sb[:, :, :], router_w[0].rearrange("(j p) e -> p j e", p=P)).then_inc(s_router, 16)
            act.dma_start(router_bias[:, :], router_b.to_broadcast([P, NE])).then_inc(s_router, 16)
            act.wait_ge(lam_sum, 1)
            nc.scalar.activation(lam_s[:, 2:4], lam_s[:, 0:2], ACT.Exp).then_inc(lam_exp, 1)
            act.wait_ge(ang_ready, 1)
            nc.scalar.activation(ang3, ang, ACT.Sin).then_inc(sincos, 1)
            nc.scalar.activation(ang4, ang2, ACT.Sin).then_inc(sincos, 1)

            def copy_qkt(n):
                s, i = divmod(n, TT)
                act.wait_ge(qk_turned, n + 1)
                nc.scalar.activation(qk_t[:, s, :, P * i:P * i + P], bank4(4 + n % 2), ACT.Copy).then_inc(qkt_ready, 1)

            for n in range(8):
                act.wait_ge(proj, n + 1)
                nc.scalar.activation(qk_tok[:, n // TT, n % TT, :], ps[:, n % 4, :], ACT.Copy).then_inc(proj_copied, 1)
                if n >= 2:
                    copy_qkt(n - 2)
            copy_qkt(6)
            copy_qkt(7)
            for i in range(TT):
                act.wait_ge(v_proj, i + 1)
                nc.scalar.activation(v_sb[:, i, :], ps[:, i, :], ACT.Copy).then_inc(v_ready, 1)

            def take_o(n):
                i, h = divmod(n, HEADS)
                act.wait_ge(pv_done, n + 1)
                if n == 0:
                    act.wait_ge(roped, 8)
                if h == 0 and i >= 2:
                    act.wait_ge(o_turned, i - 1)
                seq.tick(nc.scalar.activation(o_sb[:, i % 2, h, :], ps[:, 6, P * h:P * h + P], ACT.Square,
                                              accum_out=ss_o[:, i, h:h + 1]))
                seq.settle()
                nc.scalar.activation(o_sb[:, i % 2, h, :], ps[:, 6, P * h:P * h + P], ACT.Copy).then_inc(o_copied, 1)

            for n in range(16):
                i, h = divmod(n, HEADS)
                b, w = n % 2, P * (i + 1)
                act.wait_ge(maxed, n + 1)
                if n >= 2:
                    act.wait_ge(mixed, n - 1)
                for m in range(2):
                    nc.scalar.activation(probs[:, b, m, 0:w], ps[:, 2 * b + m, 0:w], ACT.Exp,
                                         bias=nbias[:, b, m:m + 1], scale=SCALE,
                                         accum_out=esum[:, b, m:m + 1]).then_inc(exped, 1)
                act.wait_ge(coefed, n + 1)
                act.wait_ge(exped, 2 * n + 2)
                nc.scalar.activation(probs[:, b, 1, 0:w], probs[:, b, 1, 0:w], ACT.Copy,
                                     scale=coef[:, b, 0:1]).then_inc(scaled, 1)
                if n % 4 == 3:
                    g = n // 4
                    act.wait_ge(u_proj, g + 1)
                    nc.scalar.activation(u_t[:, POOL_ORDER[g], :], ps[:, 7, :], ACT.Copy).then_inc(u_ready, 1)
                if n >= 3:
                    take_o(n - 3)
            for n in range(13, 16):
                take_o(n)
            act.wait_ge(o_copied, 16)
            for n, g in enumerate(POOL_ORDER):
                act.wait_ge(pool_mm, n + 1)
                nc.scalar.activation(cat_t[:, 4 + g, :], ps[:, g, :], ACT.Copy,
                                     scale=vec_t[:, PS + g:PS + g + 1]).then_inc(cat_pool, 1)

            for i in range(TT):
                act.wait_ge(x2_ready, i + 1)
                act.dma_start(x2_tiles[i], x_sb[:, i, :]).then_inc(x2_stored, 16)
                if i:
                    act.wait_ge(xn_stored, 16 * i)
                    act.wait_ge(xn2_turned, i)
                else:
                    act.wait_ge(o_turned, TT)
                nc.scalar.activation(xn_sb, x_sb[:, i, :], ACT.Square,
                                     accum_out=ss_2[:, i:i + 1]).then_inc(sumsq2, 1)
                act.wait_ge(xn2_ready, i + 1)
                act.dma_start(xn_tiles[i], xn_sb).then_inc(xn_stored, 16)

            act.wait_ge(top_ready, 1)
            for i in range(TT):
                nc.scalar.activation(gate4[:, i, :], top8[:, i, 0:TOPK], ACT.Exp, bias=neg_top[:, i:i + 1],
                                     accum_out=gate_sum[:, i:i + 1]).then_inc(gate_exp, 1)

            def sigmoid(b, q):
                act.wait_ge(g_ready, q + 1)
                nc.scalar.activation(s_t[:, b % 2, :], g_t[:, b % 2, :], ACT.Sigmoid, scale=ALPHA).then_inc(sig_ready, 1)

            def gate_rows(s, b, q, n_before):
                act.wait_ge(scattered[b], n_before * 16 + 16)
                act.wait_ge(y_done, q + 2)
                nc.scalar.activation(y_rows[b], ps[:, 4 + b % 2, SUB:2 * SUB], ACT.Copy,
                                     scale=gate_col[:, s, b, :]).then_inc(yr_ready, 1)

            act.wait_ge(ordinals_ready, 1)
            with act.Fori(0, NE // 2) as it:
                for s in range(2):
                    e = it * 2 + s
                    q = act.value_load(counts_i[0:1, bass.ds(e + Q_AT, 1)], min_val=0, max_val=NB * NE)
                    count = act.value_load(counts_i[0:1, bass.ds(e, 1)], min_val=0, max_val=S)
                    sigmoid(0, q)
                    for b in range(1, NB):
                        with act.If(count > HB * b):
                            sigmoid(b, q + b)
                    gate_rows(s, 0, q, e)
                    for b in range(1, NB):
                        with act.If(count > HB * b):
                            at = D_AT + (b - 1) * (NE + 1)
                            d = act.value_load(counts_i[0:1, bass.ds(e + at, 1)], min_val=0, max_val=NE)
                            gate_rows(s, b, q + b, d)
            q_all = act.value_load(counts_i[0:1, Q_AT + NE:Q_AT + NE + 1], min_val=0, max_val=NB * NE)
            act.wait_ge(extra_ready, 1)
            n_extra = act.value_load(counts_i[0:1, NE:NE + 1], min_val=0, max_val=MAX_EXTRA)
            with act.If(n_extra > 0):
                with act.Fori(0, MAX_EXTRA) as i:
                    with act.If(n_extra > i):
                        for b in range(NB):
                            sigmoid(b, q_all + (i * NB + b))
                        gate_rows(0, 0, q_all + i * NB, i + NE)
                        for b in range(1, NB):
                            at = D_AT + (b - 1) * (NE + 1) + NE
                            d_all = act.value_load(counts_i[0:1, at:at + 1], min_val=0, max_val=NE)
                            gate_rows(0, b, q_all + (i * NB + b), d_all + i)

            act.wait_ge(all_scattered, 1)
            for i in range(TT):
                act.wait_ge(moe_sum, i + 1)
                if i:
                    act.wait_ge(sumsq3, i)
                nc.scalar.activation(sq3, x2_sb[:, i, :], ACT.Square,
                                     accum_out=ss_x[:, i:i + 1]).then_inc(sumsq3, 1)

        @block.vector
        def _(dve):
            V = nc.vector
            seq = Count(dve, dve_seq)
            V.memset(rows, 0.0).then_inc(rows_ready, 1)
            dve.wait_ge(s_small, 16 * 5)
            V.tensor_copy(rows[POS:POS + 4, :], rows_i[POS:POS + 4, :]).then_inc(rows_ready, 1)
            dve.wait_ge(consts, 10)
            seq.tick(V.tensor_scalar(edge, iota_n[:, 0:16], 1.0, None, ALU.add))
            seq.settle()
            V.reciprocal(edge, edge).then_inc(rows_ready, 1)
            def norm_x(i):
                dve.wait_ge(rstd_done, i + 1)
                if i >= 2:
                    dve.wait_ge(xn_turned, i - 1)
                V.tensor_scalar(xn1_sb[:, i % 2, :], x_sb[:, i, :], rstd_x[:, i:i + 1], None, ALU.mult).then_inc(xn_ready, 1)

            dve.wait_ge(turned, 1)
            V.tensor_copy(vec_t[:, :], ps[:, 3, 0:36]).then_inc(vec_ready, 1)
            dve.wait_ge(vec_ready, 1)
            norm_x(0)
            for i in range(TT):
                if i + 1 < TT:
                    norm_x(i + 1)
                dve.wait_ge(xn_turned, i + 1)
                for half in range(2):
                    V.tensor_tensor(h_t[:, 4 * half:4 * half + 4, P * i:P * i + P], bank4(4 + half),
                                    vec_t[:, AN + 4 * half:AN + 4 * half + 4, None].to_broadcast([P, 4, P]),
                                    ALU.mult).then_inc(ht_ready, 1)
            dve.wait_ge(s_lam_in, 64)
            seq.tick(V.tensor_tensor(lam_pr, lam_in[:, :, 0, :], lam_in[:, :, 1, :], ALU.mult))
            seq.settle()
            V.reduce_sum(lam_s[:, 0:2], lam_pr, AX).then_inc(lam_sum, 1)
            inv_freq = np.float32(THETA) ** (-np.arange(0, ROT, 2, dtype=np.float32) / np.float32(ROT))
            for f in range(ROT // 2):
                seq.tick(V.tensor_scalar(ang[:, :, f], vec_t[:, POS:POS + 4], float(inv_freq[f]), None, ALU.mult))
            seq.settle()
            seq.tick(V.tensor_scalar(ang2, ang, 1.0 / (2 * math.pi), ROUND, ALU.mult, ALU.add))
            seq.settle()
            seq.tick(V.tensor_scalar(ang2, ang2, -ROUND, None, ALU.add))
            seq.settle()
            for piece in (PI2_A, PI2_B, PI2_C):
                seq.tick(V.scalar_tensor_tensor(ang, ang2, -piece, ang, ALU.mult, ALU.add))
                seq.settle()
            seq.tick(V.tensor_scalar(ang2, ang, math.pi / 2, None, ALU.add))
            seq.settle()
            seq.tick(V.tensor_scalar(ang3, ang2, math.pi, -2 * math.pi, ALU.is_gt, ALU.mult))
            seq.settle()
            seq.tick(V.tensor_tensor(ang2, ang2, ang3, ALU.add))
            seq.tick(V.tensor_scalar(ang, ang, PI_SAFE, -PI_SAFE, ALU.min, ALU.max))
            seq.settle()
            V.tensor_scalar(ang2, ang2, PI_SAFE, -PI_SAFE, ALU.min, ALU.max).then_inc(ang_ready, 1)
            dve.wait_ge(lam_exp, 1)
            seq.tick(V.tensor_tensor(lam_s[:, 4:5], lam_s[:, 3:4], lam_s[:, 2:3], ALU.subtract))
            seq.settle()
            V.tensor_scalar(lam_s[:, 5:6], lam_s[:, 4:5], -LAM_INIT, None, ALU.add).then_inc(lam_sum, 1)
            dve.wait_ge(sincos, 2)
            seq.tick(V.tensor_copy(cos2[:, :, 0:8], ang4))
            seq.tick(V.tensor_copy(cos2[:, :, 8:16], ang4))
            seq.tick(V.tensor_copy(sin2[:, :, 8:16], ang3))
            seq.tick(V.tensor_scalar(sin2[:, :, 0:8], ang3, -1.0, None, ALU.mult))
            seq.settle()

            for n in range(8):
                s, i = divmod(n, TT)
                dve.wait_ge(proj_copied, n + 1)
                src = ps[:, n % 4, :].rearrange("p (g d) -> p g d", g=8)
                dst = qk_tok[:, s, i, :].rearrange("p (g d) -> p g d", g=8)
                ra, rb = rot_a[:, n % 2], rot_b[:, n % 2]
                co = cos2[:, i, None, :].to_broadcast([P, 8, ROT])
                si = sin2[:, i, None, :].to_broadcast([P, 8, ROT])
                seq.tick(V.tensor_tensor(ra, src[:, :, 0:16], co, ALU.mult))
                seq.tick(V.tensor_tensor(rb[:, :, 0:8], src[:, :, 8:16], si[:, :, 0:8], ALU.mult))
                seq.tick(V.tensor_tensor(rb[:, :, 8:16], src[:, :, 0:8], si[:, :, 8:16], ALU.mult))
                seq.settle()
                V.tensor_tensor(dst[:, :, 0:16], ra, rb, ALU.add).then_inc(roped, 1)
            dve.wait_ge(lam_bc, 1)
            V.tensor_copy(neg_lam, ps[:, 7, 0:1]).then_inc(lam_taken, 1)
            dve.wait_ge(lam_taken, 1)

            def evac_mix(n):
                w = P * (n // HEADS + 1)
                dve.wait_ge(mix_turned, n + 1)
                V.tensor_copy(mix_t[:, n % 2, 0:w], ps[:, 4 + n % 2, 0:w]).then_inc(mixt_ready, 1)

            def norm_o(i):
                dve.wait_ge(o_rstd, i + 1)
                V.tensor_tensor(o_sb[:, i % 2], o_sb[:, i % 2], rstd_o[:, i, :, None].to_broadcast([P, HEADS, P]),
                                ALU.mult).then_inc(o_normed, 1)

            def take_cat(i):
                dve.wait_ge(o_turned, i + 1)
                V.tensor_scalar(cat_t[:, 0:4, P * i:P * i + P], bank4(O_BANK[i]), vec_t[:, SL:SL + 1],
                                1.0 - LAM_INIT, ALU.mult, ALU.mult).then_inc(cat_attn, 1)

            for n in range(16):
                b, w = n % 2, P * (n // HEADS + 1)
                if n >= 10 and (n - 10) % 4 == 0:
                    take_cat((n - 10) // 4)
                dve.wait_ge(scored, n + 1)
                seq.tick(V.reduce_max(mx[:, b, :], ps[:, 2 * b:2 * b + 2, 0:w], AX))
                seq.settle()
                V.tensor_scalar(nbias[:, b, :], mx[:, b, :], -SCALE, None, ALU.mult).then_inc(maxed, 1)
                if n >= 2:
                    evac_mix(n - 2)
                if n >= 9 and (n - 9) % 4 == 0:
                    norm_o((n - 9) // 4)
                dve.wait_ge(exped, 2 * n + 2)
                seq.tick(V.reciprocal(rsum[:, b, :], esum[:, b, :]))
                seq.settle()
                V.tensor_tensor(coef[:, b, :], rsum[:, b, 1:2], neg_lam, ALU.mult).then_inc(coefed, 1)
                dve.wait_ge(scaled, n + 1)
                V.scalar_tensor_tensor(mix[:, b, 0:w], probs[:, b, 0, 0:w], rsum[:, b, 0:1], probs[:, b, 1, 0:w],
                                       ALU.mult, ALU.add).then_inc(mixed, 1)
            evac_mix(14)
            evac_mix(15)
            for i in (2, 3):
                norm_o(i)
                take_cat(i)

            for i in range(TT):
                dve.wait_ge(out_proj, i + 1)
                V.tensor_tensor(x_sb[:, i, :], x_sb[:, i, :],
                                ps[:, 2 * (i % 2):2 * (i % 2) + 2, :].rearrange("p a b -> p (a b)"),
                                ALU.add).then_inc(x2_ready, 1)
                if i == TT - 1:
                    for c in range(NB):
                        seq.tick(V.memset(quarter_off[HB * c:HB * c + HB, :], float(NB * OUT_OF_ROWS + c)))
                    seq.tick(V.memset(table, 0.0))
                    for k in range(TOPK):
                        seq.tick(V.memset(dst4[:, :, k:k + 1], float(S * k - OUT_OF_ROWS + OUT_OF_TOKENS)))
                    seq.tick(V.memset(zero32, 0.0))
                dve.wait_ge(rstd2_done, i + 1)
                if i:
                    dve.wait_ge(xn_stored, 16 * i)
                    dve.wait_ge(xn2_turned, i)
                else:
                    dve.wait_ge(cat_attn, TT)
                V.tensor_scalar(xn_sb, x_sb[:, i, :], rstd_2[:, i:i + 1], None, ALU.mult).then_inc(xn2_ready, 1)
                dve.wait_ge(xn2_turned, i + 1)
                dve.wait_ge(x2_stored, 16 * i + 16)
                V.tensor_tensor(x2h(i), ps[:, 4:6, :].rearrange("p a (c n) -> p (a c) n", c=4),
                                vec_t[:, FN:FN + 8, None].to_broadcast([P, KT, P]), ALU.mult).then_inc(h2_ready, 1)
                dve.wait_ge(routed, i + 1)
                V.tensor_tensor(logits[:, i, :], ps[:, 6, NE * i:NE * i + NE], router_bias[:, :],
                                ALU.add).then_inc(logit_ready, 1)

            dve.wait_ge(logit_ready, TT)
            for i in range(TT):
                seq.tick(V.max(top8[:, i, :], logits[:, i, :]))
            seq.settle()
            seq.tick(V.tensor_scalar(neg_top, top8[:, :, 0], -1.0, None, ALU.mult))
            for i in range(TT):
                seq.tick(V.max_index(top_idx[:, i, :], top8[:, i, :], logits[:, i, :]))
            seq.settle()
            V.tensor_copy(idx_f, top_idx).then_inc(top_ready, 1)
            dve.wait_ge(top_ready, 1)
            seq.tick(V.tensor_tensor(eq4, iota_n[:, None, None, 0:NE].to_broadcast([P, TT, TOPK, NE]),
                                     idx_f[:, :, 0:TOPK, None].to_broadcast([P, TT, TOPK, NE]), ALU.is_equal))
            seq.settle()
            seq.tick(V.reduce_sum(mask_f, eq4.rearrange("p i k e -> p i e k"), AX))
            seq.settle()
            V.tensor_copy(mask_h, mask_f).then_inc(mask_ready, 1)
            dve.wait_ge(gate_exp, TT)
            seq.tick(V.reciprocal(gate_sum, gate_sum))
            seq.settle()
            seq.tick(V.tensor_tensor(gate4, gate4, gate_sum[:, :, None].to_broadcast([P, TT, TOPK]), ALU.mult))
            seq.settle()
            seq.tick(V.tensor_scalar(table[:, :, 0:NE, 0], mask_f, row_id, None, ALU.mult))
            for i in range(TT):
                seq.tick(V.tensor_scalar(table[:, i, 0:NE, 1], mask_f[:, i, :], float(P * i - OUT_OF_TOKENS), None,
                                         ALU.mult))
            dve.wait_ge(xn_stored, 16 * TT)
            seq.tick(V.tensor_tensor(eq4b, eq4, gate4[:, :, :, None].to_broadcast([P, TT, TOPK, NE]), ALU.mult))
            seq.settle()
            seq.tick(V.reduce_sum(gate_f, eq4b.rearrange("p i k e -> p i e k"), AX))
            seq.settle()
            seq.tick(V.tensor_tensor(eq4b, eq4, dst4[:, :, :, None].to_broadcast([P, TT, TOPK, NE]), ALU.mult))
            for c in (2, 3, 4):
                seq.tick(V.tensor_copy(table[:, :, 0:NE, c], gate_f))
                seq.settle()
                if c < 4:
                    seq.tick(V.tensor_tensor(gate_f, gate_f, table[:, :, 0:NE, c], ALU.subtract))
                    seq.settle()
            seq.tick(V.reduce_sum(gate_r, eq4b.rearrange("p i k e -> p i e k"), AX))
            seq.settle()
            seq.tick(V.tensor_copy(table[:, :, 0:NE, 5], gate_r))
            dve.wait_ge(spot_sum, 1)
            seq.tick(V.scalar_tensor_tensor(spot[:, :, 0:NE], ps[:, 4, 0:TT * NE].rearrange("p (i e) -> p i e", i=TT),
                                            1.0, mask_f, ALU.add, ALU.mult))
            seq.tick(V.memset(spot[:, :, NE:NE + 2], 0.0))
            seq.settle()
            seq.tick(V.tensor_scalar(spot, spot, -1.0, None, ALU.add))
            seq.tick(V.tensor_copy(counts_i[0:1, 0:NE], ps[0:1, 5, 0:NE]))
            seq.tick(V.memset(counts_i[0:1, NE:NE + 1], 0))
            seq.tick(V.tensor_copy(count_f, ps[:, 5, 0:NE]))
            seq.settle()

            def select_bias(s, e):
                src = sel3[:, e:e + 1] if isinstance(e, int) else sel3[:, bass.ds(e, 1)]
                seq.tick(V.tensor_copy(bias_sel[:, s, :], src.to_broadcast([3 * NE, HB])))

            def hot(e):
                src = spot[:, :, e:e + 1] if isinstance(e, int) else spot[:, :, bass.ds(e, 1)]
                V.tensor_tensor(one_hot, iota_n[:, None, :].to_broadcast([P, TT, BLK]),
                                src.to_broadcast([P, TT, BLK]), ALU.is_equal).then_inc(hot_ready, 1)

            def take_tokens(s, n):
                dve.wait_ge(idx_sum, n)
                seq.tick(V.tensor_scalar(token_sum, ps[:, 5, 0:1], float(OUT_OF_TOKENS), None, ALU.add))
                seq.settle()
                seq.tick(V.tensor_tensor(token_sum, token_sum, ps[:, 5, 1:2], ALU.add))
                seq.settle()
                V.tensor_copy(idx_src[:, s:s + 1], token_sum).then_inc(idx_ready, 1)
                V.tensor_copy(parts, ps[:, 5, 0:6]).then_inc(parts_ready, 1)

            def take_rows(s, n):
                dve.wait_ge(parts_spread, n)
                blocks = ps[:, 5, 8:8 + 6 * NB].rearrange("p (b c) -> p b c", b=NB)
                seq.tick(V.tensor_copy(tmp_a, blocks[:, :, 2:3]))
                seq.tick(V.tensor_copy(tmp_b, blocks[:, :, 0:1]))
                seq.settle()
                seq.tick(V.tensor_tensor(tmp_a, tmp_a, blocks[:, :, 3:4], ALU.add))
                seq.tick(V.tensor_tensor(tmp_b, tmp_b, blocks[:, :, 1:2], ALU.add))
                seq.settle()
                V.tensor_tensor(gate_col[:, s], tmp_a, blocks[:, :, 4:5], ALU.add).then_inc(gates_taken, 1)
                seq.tick(V.tensor_tensor(tmp_b, tmp_b, blocks[:, :, 5:6], ALU.add))
                seq.settle()
                V.tensor_scalar(idx_dst[:, s], tmp_b, float(NB), quarter_off, ALU.mult, ALU.add).then_inc(dst_taken, 1)

            def take_x(b, n):
                dve.wait_ge(x_turned, n)
                V.tensor_tensor(xe_t[:, b], ps[:, 6:8, :].rearrange("p a (c n) -> p (a c) n", c=4),
                                vec_t[:, FN:FN + 8, None].to_broadcast([P, KT, BLK]), ALU.mult).then_inc(xe_ready, 1)

            def clamp(b, q):
                dve.wait_ge(gu_done, q + 1)
                V.tensor_scalar(g_t[:, b % 2, :], ps[:, b % 2, 0:SUB], LIMIT, None, ALU.min).then_inc(g_ready, 1)
                V.tensor_scalar(u1_t[:, b % 2, :], ps[:, b % 2, SUB:2 * SUB], -LIMIT, LIMIT,
                                ALU.max, ALU.min).then_inc(gu_evac, 1)

            def glu(b, q):
                dve.wait_ge(sig_ready, q + 1)
                V.tensor_tensor(s_t[:, b % 2, :], g_t[:, b % 2, :], s_t[:, b % 2, :], ALU.mult).then_inc(glu_ready, 1)
                dve.wait_ge(gu_evac, q + 2)
                dve.wait_ge(glu_ready, q + 1)
                V.scalar_tensor_tensor(act_sb[:, b % 2, :], u1_t[:, b % 2, :], 1.0, s_t[:, b % 2, :],
                                       ALU.add, ALU.mult).then_inc(act_ready, 1)

            def take_act(b, q):
                dve.wait_ge(act_turned, q + 1)
                V.tensor_copy(act_t[b], turned_act(b)).then_inc(actt_ready, 1)

            dve.wait_ge(x2_stored, 16 * TT)
            dve.wait_ge(x2_ready, TT)
            dve.sem_inc(gu_evac, 1)
            dve.sem_inc(yr_ready, 1)
            hot(0)
            select_bias(0, 0)
            for b in range(NB):
                seq.tick(V.tensor_copy(spread[:, b], ident_h[:, None, HB * b:HB * b + HB].to_broadcast([P, NB, HB])))
            seq.settle()
            take_tokens(0, 1)
            hot(1)
            for b in range(1, NB):
                seq.tick(V.tensor_scalar(more[:, b - 1], count_f, float(HB * b), None, ALU.is_gt))
            seq.settle()
            for b in range(1, NB):
                seq.tick(V.tensor_tensor_scan(more_sum[:, b - 1], more[:, b - 1], zero32, 0.0, ALU.add, ALU.add))
            seq.settle()
            last = more_sum[0:1, :, NE - 1]
            for b in range(1, NB):
                at = D_AT + (b - 1) * (NE + 1) + NE
                seq.tick(V.tensor_copy(counts_i[0:1, at:at + 1], last[:, b - 1:b]))
            seq.tick(V.reduce_sum(q_total[0:1, :], last, AX))
            seq.settle()
            seq.tick(V.tensor_scalar(counts_i[0:1, Q_AT + NE:Q_AT + NE + 1], q_total[0:1, :], float(NE), None, ALU.add))
            seq.tick(V.tensor_tensor(more_sum, more_sum, more, ALU.subtract))
            seq.settle()
            seq.tick(V.reduce_sum(q_f, more_sum.rearrange("p b e -> p e b"), AX))
            for b in range(1, NB):
                at = D_AT + (b - 1) * (NE + 1)
                seq.tick(V.tensor_copy(counts_i[0:1, at:at + NE], more_sum[0:1, b - 1, :]))
            seq.settle()
            V.tensor_tensor(counts_i[0:1, Q_AT:Q_AT + NE], q_f[0:1, :], iota_n[0:1, 0:NE],
                            ALU.add).then_inc(ordinals_ready, 1)
            take_rows(0, 1)
            take_x(0, 1)
            dve.wait_ge(ordinals_ready, 1)

            n0 = seq.n
            per = 0
            with dve.Fori(0, NE // 2) as it:
                seq.off = it * LOOP_DVE
                for s in range(2):
                    e = it * 2 + s
                    q = dve.value_load(counts_i[0:1, bass.ds(e + Q_AT, 1)], min_val=0, max_val=NB * NE)
                    count = dve.value_load(counts_i[0:1, bass.ds(e, 1)], min_val=0, max_val=S)
                    d = [dve.value_load(counts_i[0:1, bass.ds(e + (D_AT + b * (NE + 1)), 1)], min_val=0, max_val=NE)
                         for b in range(NB - 1)]
                    dve.wait_ge(pool_touched, q + e + 1)
                    take_tokens(1 - s, it * 2 + (s + 2))
                    clamp(0, q)
                    select_bias(1 - s, it * 2 + (s + 1))
                    glu(0, q)
                    for b in range(1, NB):
                        with dve.If(count > HB * b):
                            clamp(b, q + b)
                            take_act(b - 1, q + (b - 1))
                            glu(b, q + b)
                    dve.wait_ge(scattered[0], e * 16 + 16)
                    for b in range(1, NB):
                        dve.wait_ge(scattered[b], d[b - 1] * 16 + 16)
                    take_rows(1 - s, it * 2 + (s + 2))
                    take_x(1 - s, it * 2 + (s + 2))
                    with dve.If(count <= HB):
                        take_act(0, q)
                    for b in range(1, NB - 1):
                        with dve.If(count > HB * b):
                            with dve.If(count <= HB * (b + 1)):
                                take_act(b, q + b)
                    with dve.If(count > HB * (NB - 1)):
                        take_act(NB - 1, q + (NB - 1))
                    hot(it * 2 + (s + 2))
                per = seq.n - n0
            assert per == LOOP_DVE, per
            seq.n, seq.off = n0 + LOOP_DVE * (NE // 2), None
            seq.tick(V.tensor_scalar(over, count_f, float(BLK), None, ALU.is_gt))
            seq.settle()
            for j in (2, 3):
                seq.tick(V.scalar_tensor_tensor(over, count_f, float(BLK * j), over, ALU.is_gt, ALU.add))
                seq.settle()
            seq.tick(V.tensor_tensor_scan(over_sum, over, zero32, 0.0, ALU.add, ALU.add))
            seq.settle()
            seq.tick(V.tensor_tensor(ov_cmp, over_sum[:, None, :].to_broadcast([P, MAX_EXTRA, NE]),
                                     iota_n[:, 0:MAX_EXTRA, None].to_broadcast([P, MAX_EXTRA, NE]), ALU.is_le))
            seq.settle()
            seq.tick(V.reduce_sum(ov_e, ov_cmp, AX))
            seq.settle()
            seq.tick(V.tensor_tensor(ov_cmp, ov_cmp, over[:, None, :].to_broadcast([P, MAX_EXTRA, NE]), ALU.mult))
            seq.settle()
            seq.tick(V.reduce_sum(ov_b, ov_cmp, AX))
            seq.settle()
            seq.tick(V.tensor_tensor(extra_base, iota_n[:, 0:MAX_EXTRA], ov_b, ALU.subtract))
            seq.tick(V.tensor_scalar(ov_e, ov_e, float(NE - 1), None, ALU.min))
            seq.settle()
            seq.tick(V.tensor_scalar(extra_base, extra_base, 1.0, float(BLK), ALU.add, ALU.mult))
            seq.tick(V.tensor_copy(extra_e, ov_e[0:1, :]))
            seq.settle()
            V.tensor_copy(counts_i[0:1, NE:NE + 1], over_sum[0:1, NE - 1:NE]).then_inc(extra_ready, 1)
            dve.wait_ge(extra_ready, 1)
            q_all = dve.value_load(counts_i[0:1, Q_AT + NE:Q_AT + NE + 1], min_val=0, max_val=NB * NE)
            n_extra = dve.value_load(counts_i[0:1, NE:NE + 1], min_val=0, max_val=MAX_EXTRA)
            d_all = [dve.value_load(counts_i[0:1, at:at + 1], min_val=0, max_val=NE)
                     for at in range(D_AT + NE, D_AT + NE + (NB - 1) * (NE + 1), NE + 1)]
            n1 = seq.n
            with dve.If(n_extra > 0):
                with dve.Fori(0, MAX_EXTRA) as i:
                    with dve.If(n_extra > i):
                        seq.off = i * EXTRA_DVE
                        e = dve.value_load(extra_e[0:1, bass.ds(i, 1)], min_val=0, max_val=NE - 1)
                        dve.wait_ge(pool_touched, q_all + i * (NB + 1) + (NE + 1))
                        dve.wait_ge(scattered[0], (i + (NE + 1)) * 16)
                        for b in range(1, NB):
                            dve.wait_ge(scattered[b], (d_all[b - 1] + i + 1) * 16)
                        seq.tick(V.tensor_scalar(spot_now, spot[:, :, bass.ds(e, 1)].rearrange("p i a -> p (i a)"),
                                                 extra_base[:, bass.ds(i, 1)], None, ALU.subtract))
                        seq.settle()
                        V.tensor_tensor(one_hot, iota_n[:, None, :].to_broadcast([P, TT, BLK]),
                                        spot_now[:, :, None].to_broadcast([P, TT, BLK]),
                                        ALU.is_equal).then_inc(hot_ready, 1)
                        take_tokens(0, i + (NE + 2))
                        take_rows(0, i + (NE + 2))
                        select_bias(0, e)
                        take_x(0, i + (NE + 2))
                        for b in range(NB):
                            clamp(b, q_all + (i * NB + b))
                            if b:
                                take_act(b - 1, q_all + (i * NB + (b - 1)))
                            glu(b, q_all + (i * NB + b))
                        take_act(NB - 1, q_all + (i * NB + (NB - 1)))
                        per = seq.n - n1
            assert per == EXTRA_DVE, per
            seq.off = n_extra * EXTRA_DVE
            seq.n = n1

            def finish_tile(i):
                dve.wait_ge(rstd3_done, i + 1)
                V.scalar_tensor_tensor(x2_sb[:, i, :], x2_sb[:, i, :], rstd_x[:, i:i + 1], fnw_sb,
                                       ALU.mult, ALU.mult).then_inc(out_ready, 1)
            dve.wait_ge(x2_loaded, 16 * TT)
            for i in range(TT):
                for k in range(TOPK):
                    if k % 2 == 0:
                        dve.wait_ge(ys_loaded[i][k // 2], 16)
                    add = V.tensor_tensor(x2_sb[:, i, :], x2_sb[:, i, :], ys_sb[:, i, k, :], ALU.add)
                    if k < TOPK - 1:
                        seq.tick(add)
                        seq.settle()
                    else:
                        add.then_inc(moe_sum, 1)
                if i == 1:
                    dve.wait_ge(fnw_loaded, 16)
                if i:
                    finish_tile(i - 1)
            finish_tile(TT - 1)

        @block.tensor
        def _(pe):
            MM = nc.tensor.matmul
            TR = nc.tensor.transpose
            pe.wait_ge(consts, 10)
            pe.wait_ge(rows_ready, 2)
            TR(ps[:, 3, 0:36], rows, ident[0:36, 0:36]).then_inc(turned, 1)
            def turn_xn(i):
                pe.wait_ge(xn_ready, i + 1)
                if i:
                    pe.wait_ge(ht_ready, 2 * i)
                for j in range(KT):
                    mm = TR(bank4(4 + j // 4)[:, j % 4, :], xn1_sb[:, i % 2, P * j:P * j + P], ident[:, :])
                mm.then_inc(xn_turned, 1)

            def turn_qk(n):
                s, i = divmod(n, TT)
                pe.wait_ge(roped, n + 1)
                if n < 2:
                    pe.wait_ge(ht_ready, 2 * TT)
                else:
                    pe.wait_ge(qkt_ready, n - 1)
                for h in range(HEADS):
                    mm = TR(bank4(4 + n % 2)[:, h, :], qk_tok[:, s, i, P * h:P * h + P], ident[:, :])
                mm.then_inc(qk_turned, 1)

            turn_xn(0)
            turn_xn(1)
            for n in range(8):
                s, i = divmod(n, TT)
                pe.wait_ge(s_win[s], 16)
                pe.wait_ge(ht_ready, 2 * i + 2)
                if n >= 4:
                    pe.wait_ge(roped, n - 3)
                for j in range(KT):
                    mm = MM(ps[:, n % 4, :], h_t[:, j, P * i:P * i + P], w_in_sb[:, j, 512 * s:512 * s + 512],
                            start=(j == 0), stop=(j == KT - 1))
                mm.then_inc(proj, 1)
                if n < 2:
                    turn_xn(n + 2)
                if n == 3:
                    pe.wait_ge(lam_sum, 2)
                    MM(ps[:, 7, 0:1], ones_f, lam_s[:, 5:6], start=True, stop=True).then_inc(lam_bc, 1)
                if n >= 2:
                    turn_qk(n - 2)
            pe.wait_ge(s_win[2], 16)
            for i in range(TT):
                pe.wait_ge(roped, 5 + i)
                for j in range(KT):
                    mm = MM(ps[:, i, :], h_t[:, j, P * i:P * i + P], w_in_sb[:, j, 1024:1536],
                            start=(j == 0), stop=(j == KT - 1))
                mm.then_inc(v_proj, 1)
                if i < 2:
                    turn_qk(6 + i)

            def scores(n):
                i, h = divmod(n, HEADS)
                b = n % 2
                if n == 0:
                    pe.wait_ge(qkt_ready, 8)
                    pe.wait_ge(lam_taken, 1)
                if n < 2:
                    pe.wait_ge(v_ready, 2 * n + 2)
                else:
                    pe.wait_ge(exped, 2 * n - 2)
                for m in range(2):
                    r = slice(QKD * m, QKD * m + QKD)
                    o = ps[:, 2 * b + m, :]
                    MM(o[:, P * i:P * i + P], ident_h[:, :], causal[:, :], start=True, stop=False,
                       skip_group_check=True)
                    mm = MM(o[:, 0:P * (i + 1)], qk_t[r, 0, h, P * i:P * i + P], qk_t[r, 1, h, 0:P * (i + 1)],
                            start=False, stop=True, skip_group_check=True)
                mm.then_inc(scored, 1)

            def turn_mix(n):
                i = n // HEADS
                pe.wait_ge(mixed, n + 1)
                if n < 2:
                    pe.wait_ge(qkt_ready, 8)
                else:
                    pe.wait_ge(mixt_ready, n - 1)
                if n >= 9 and (n - 9) % 4 == 0:
                    pe.wait_ge(cat_attn, (n - 9) // 4 + 1)
                for kb in range(i + 1):
                    mm = TR(bank4(4 + n % 2)[:, kb, :], mix[:, n % 2, P * kb:P * kb + P], ident[:, :])
                mm.then_inc(mix_turned, 1)

            def pv(n):
                i, h = divmod(n, HEADS)
                pe.wait_ge(mixt_ready, n + 1)
                if n == 0:
                    pe.wait_ge(v_ready, TT)
                else:
                    pe.wait_ge(o_copied, n)
                for kb in range(i + 1):
                    mm = MM(ps[:, 6, P * h:P * h + P], mix_t[:, n % 2, P * kb:P * kb + P],
                            v_sb[:, kb, P * h:P * h + P], start=(kb == 0), stop=(kb == i))
                mm.then_inc(pv_done, 1)

            def turn_o(i, n_mix):
                pe.wait_ge(o_normed, i + 1)
                pe.wait_ge(mixt_ready, n_mix)
                for h in range(HEADS):
                    mm = TR(bank4(O_BANK[i])[:, h, :], o_sb[:, i % 2, h, :], ident[:, :])
                mm.then_inc(o_turned, 1)

            pe.wait_ge(s_win[3], 16)
            for n in range(16):
                scores(n)
                c, r = divmod(n, 4)
                if r == 0 and c:
                    pe.wait_ge(u_ready, c)
                uc = 1536 + P * POOL_ORDER[c]
                for j in (2 * r, 2 * r + 1):
                    mm = MM(ps[:, 7, :], w_in_sb[:, j, uc:uc + P], h_t[:, j, :],
                            start=(j == 0), stop=(j == KT - 1))
                if r == 3:
                    mm.then_inc(u_proj, 1)
                if n >= 2:
                    turn_mix(n - 2)
                if n >= 3:
                    pv(n - 3)
                if n >= 9 and (n - 9) % 4 == 0:
                    turn_o((n - 9) // 4, n - 1)
            turn_mix(14)
            pv(13)
            turn_mix(15)
            pv(14)
            pv(15)
            pe.wait_ge(s_poolw, 16)
            pe.wait_ge(exped, 32)
            for n, g in enumerate(POOL_ORDER):
                pe.wait_ge(pooled, n + 1)
                MM(ps[:, g, :], pool_w_sb[:, g, :], pool_d[:, g, :], start=True, stop=True).then_inc(pool_mm, 1)
            for i in (2, 3):
                turn_o(i, 16)

            def turn_xn2(i):
                pe.wait_ge(xn2_ready, i + 1)
                if i:
                    pe.wait_ge(h2_ready, i)
                for j in range(KT):
                    mm = TR(bank4(4 + j // 4)[:, j % 4, :], xn_sb[:, P * j:P * j + P], ident[:, :])
                mm.then_inc(xn2_turned, 1)

            def router(i):
                pe.wait_ge(h2_ready, i + 1)
                if i == 0:
                    pe.wait_ge(o_copied, 16)
                    pe.wait_ge(s_router, 32)
                for j in range(KT):
                    mm = MM(ps[:, 6, NE * i:NE * i + NE], x2h(i)[:, j, :], router_sb[:, j, :],
                            start=(j == 0), stop=(j == KT - 1))
                mm.then_inc(routed, 1)

            pe.wait_ge(s_wout, 16)
            pe.wait_ge(cat_pool, 4)
            for i in range(TT):
                pe.wait_ge(cat_attn, i + 1)
                if i >= 2:
                    pe.wait_ge(x2_ready, i - 1)
                for half in range(2):
                    if half and i:
                        turn_xn2(i - 1)
                    for n, j in enumerate((4, 5, 6, 7, 0, 1, 2, 3)):
                        if half and i and n == 4:
                            router(i - 1)
                        mm = MM(ps[:, 2 * (i % 2) + half, :], cat_t[:, j, P * i:P * i + P],
                                w_out_sb[:, j, 512 * half:512 * half + 512], start=(n == 0), stop=(n == KT - 1))
                mm.then_inc(out_proj, 1)
            turn_xn2(TT - 1)
            router(TT - 1)
            pe.wait_ge(x2_ready, TT)
            pe.sem_inc(y_done, 1)
            pe.wait_ge(mask_ready, 1)
            pe.wait_ge(h2_ready, TT)
            for i in range(TT):
                for k in range(i + 1):
                    MM(ps[:, 4, NE * i:NE * i + NE], before[:, :] if k == i else ones_h[:, :], mask_h[:, k, :],
                       start=(k == 0), stop=(k == i))
            for k in range(TT):
                mm = MM(ps[:, 5, 0:NE], ones_h[:, :], mask_h[:, k, :], start=(k == 0), stop=(k == TT - 1))
            mm.then_inc(spot_sum, 1)

            def sum_indices(e, n_hot):
                pe.wait_ge(hot_ready, n_hot)
                for i in range(TT):
                    r = table[:, i, e, :] if isinstance(e, int) else \
                        table[:, i, bass.ds(e, 1), :].rearrange("p a c -> p (a c)")
                    mm = MM(ps[:, 5, 0:6], one_hot[:, i, :], r, start=(i == 0), stop=(i == TT - 1))
                mm.then_inc(idx_sum, 1)

            def spread_parts(n):
                pe.wait_ge(parts_ready, n)
                for b in range(NB):
                    mm = MM(ps[:, 5, 8 + 6 * b:14 + 6 * b], spread[:, b].rearrange("p r n -> p (r n)"), parts,
                            start=True, stop=True)
                mm.then_inc(parts_spread, 1)

            def turn_x(n):
                pe.wait_ge(gathered, n * 16)
                for j in range(KT):
                    mm = TR(bank4(6 + j // 4)[:, j % 4, :], xg[:, P * j:P * j + P], ident[:, :])
                mm.then_inc(x_turned, 1)

            def gate_up(slot, s, b, q, n_loaded=None):
                pe.wait_ge(gu_evac, q if b else q + 1)
                for j in range(-1, KT):
                    if n_loaded is not None and j >= 0:
                        pe.wait_ge(gu_loaded[slot][j], n_loaded)
                    src = bias_parts[:, 0:2 * F] if j < 0 else gu_slot[slot][:, j, :]
                    src = src.rearrange("p (a c) -> p a c", a=2)
                    for r in range(NB):
                        mm = MM(ps[HB * r:HB * r + HB, b % 2, :].rearrange("p (a c) -> p a c", a=2),
                                bias_sel[:, s, :] if j < 0 else xe_t[:, s, j, HB * b:HB * b + HB],
                                src[:, :, SUB * r:SUB * r + SUB], start=(j < 0), stop=(j == KT - 1))
                    if j % 2 and 0 < j < KT - 1:
                        mm.then_inc(gu_part[j // 2], 1)
                mm.then_inc(gu_done, 1)

            def turn_act(b, q):
                pe.wait_ge(act_ready, q + 1)
                if b >= 2:
                    pe.wait_ge(actt_ready, q - 1)
                for a in range(2):
                    mm = TR(turned_act(b)[:, a, :], act_sb[:, b % 2, P * a:P * a + P], ident[:, :])
                mm.then_inc(act_turned, 1)

            def down(s, b, q, n_loaded=None, n_dst=None, dn=dn_slot, dn_sems=dn_loaded):
                pe.wait_ge(actt_ready, q + 1)
                pe.wait_ge(yr_ready, q if b else q + 1)
                if b % 2:
                    pe.wait_ge(dst_taken, n_dst)
                for r in range(NB):
                    MM(ps[HB * r:HB * r + HB, 4 + b % 2, SUB:2 * SUB], bias_sel[:, s, :],
                       bias_parts[:, 2 * F + SUB * r:2 * F + SUB * r + SUB], start=True, stop=False)
                for c in range(NB):
                    if n_loaded is not None:
                        pe.wait_ge(dn_sems[c], n_loaded)
                    for a in range(2):
                        for r in range(NB):
                            mm = MM(ps[HB * r:HB * r + HB, 4 + b % 2, SUB:2 * SUB], act_t[b][:, a, HB * c:HB * c + HB],
                                    dn[:, 2 * c + a, SUB * r:SUB * r + SUB],
                                    start=False, stop=(c == NB - 1 and a == 1))
                mm.then_inc(y_done, 1)

            sum_indices(0, 1)
            spread_parts(1)
            turn_x(1)
            pe.wait_ge(ordinals_ready, 1)

            def expert(it, s, dn=dn_slot, dn_sems=dn_loaded, n_dn=None):
                slot, e = 1 - s, it * 2 + s
                q = pe.value_load(counts_i[0:1, bass.ds(e + Q_AT, 1)], min_val=0, max_val=NB * NE)
                count = pe.value_load(counts_i[0:1, bass.ds(e, 1)], min_val=0, max_val=S)
                pe.wait_ge(xe_ready, e + 1)
                gate_up(slot, s, 0, q, it * 16 + 16)
                pe.wait_ge(yr_ready, q + 1)
                sum_indices(it * 2 + (s + 1), it * 2 + (s + 2))
                for b in range(1, NB):
                    with pe.If(count > HB * b):
                        gate_up(slot, s, b, q + b)
                        turn_act(b - 1, q + (b - 1))
                spread_parts(it * 2 + (s + 2))
                turn_x(it * 2 + (s + 2))
                with pe.If(count <= HB):
                    turn_act(0, q)
                for b in range(1, NB - 1):
                    with pe.If(count > HB * b):
                        with pe.If(count <= HB * (b + 1)):
                            turn_act(b, q + b)
                with pe.If(count > HB * (NB - 1)):
                    turn_act(NB - 1, q + (NB - 1))
                down(s, 0, q, it * 32 + (16 * s + 16) if n_dn is None else n_dn, dn=dn, dn_sems=dn_sems)
                for b in range(1, NB):
                    with pe.If(count > b * HB):
                        down(s, b, q + b, n_dst=it * 2 + (s + 2), dn=dn)

            with pe.Fori(0, NE // 2 - 1) as it:
                for s in range(2):
                    expert(it, s)
            expert(NE // 2 - 1, 0)
            expert(NE // 2 - 1, 1, dn=dn_last, dn_sems=dn_last_loaded, n_dn=16)
            q_all = pe.value_load(counts_i[0:1, Q_AT + NE:Q_AT + NE + 1], min_val=0, max_val=NB * NE)
            pe.wait_ge(extra_ready, 1)
            n_extra = pe.value_load(counts_i[0:1, NE:NE + 1], min_val=0, max_val=MAX_EXTRA)
            with pe.If(n_extra > 0):
                with pe.Fori(0, MAX_EXTRA) as i:
                    with pe.If(n_extra > i):
                        e = pe.value_load(extra_e[0:1, bass.ds(i, 1)], min_val=0, max_val=NE - 1)
                        pe.wait_ge(yr_ready, q_all + i * NB + 1)
                        sum_indices(e, i + (NE + 3))
                        spread_parts(i + (NE + 2))
                        turn_x(i + (NE + 2))
                        pe.wait_ge(xe_ready, i + (NE + 2))
                        pe.wait_ge(ex_loaded, i * (16 * (KT + 4)) + 16 * (KT + 4))
                        for b in range(NB):
                            gate_up(0, 0, b, q_all + (i * NB + b))
                            if b:
                                turn_act(b - 1, q_all + (i * NB + (b - 1)))
                        turn_act(NB - 1, q_all + (i * NB + (NB - 1)))
                        for b in range(NB):
                            down(0, b, q_all + (i * NB + b), n_dst=i + (NE + 2))


_INS = ["x", "positions", "attn_norm_w", "w_in", "lambda_q1", "lambda_k1", "lambda_q2", "lambda_k2",
        "subln_w", "pool_w", "pool_scale", "w_out", "ffn_norm_w", "router_w", "router_b",
        "w_gate_up", "b_gate_up", "w_down", "b_down", "final_norm_w"]


def kernel(**inputs):
    import numpy as _np
    import concourse.bacc as _bacc
    from concourse import mybir as _mybir
    from concourse.bass_utils import run_bass_kernel_spmd as _run

    nc = _bacc.Bacc("TRN2", target_bir_lowering=False, num_devices=1)
    arrays, args = {}, []
    for name in _INS:
        a = _np.ascontiguousarray(inputs[name])
        arrays[f"in_{name}"] = a
        args.append(nc.dram_tensor(f"in_{name}", a.shape, _mybir.dt.from_np(a.dtype), kind="ExternalInput").ap())
    args.append(nc.dram_tensor("out_dram", (1, S, D), _mybir.dt.float32, kind="ExternalOutput").ap())
    hybrid_block(nc, *args)
    r = _run(nc, [arrays], core_ids=[0])
    return r.results[0]["out_dram"]
```
